# Optimizing a Trainium2 kernel written in Bass

```python
import math
import jax, jax.numpy as jnp
from jax import lax
import numpy as np
import jax
import jax.numpy as jnp

D_MODEL = 1024
BATCH = 1
SEQ = 512
DEPTH = 2

D_MIX = 1024
MLA_HEADS = 6
MLA_Q_RANK = 256
MLA_KV_RANK = 128
MLA_NOPE = 64
MLA_ROPE = 32
MLA_V = 64
ROPE_THETA = 10000.0
POOL_WINDOWS = (2, 4, 8, 16)
POOL_GROUP = 64
POOL_WIDTH = POOL_GROUP * len(POOL_WINDOWS)
FOX_HEADS = 6
FOX_HEAD_DIM = 64
FOX_GATE_BIAS_INIT = 2.0
BLOCK_Q = 128
D_FF = 2816
EPS = 1e-6
IN_Q_A = MLA_Q_RANK
IN_KV_A = MLA_KV_RANK
IN_K_ROPE = MLA_ROPE
IN_POOL = POOL_WIDTH
IN_FOX_QKV = 3 * FOX_HEADS * FOX_HEAD_DIM
IN_FOX_F = FOX_HEADS
N_IN = IN_Q_A + IN_KV_A + IN_K_ROPE + IN_POOL + IN_FOX_QKV + IN_FOX_F


def rmsnorm(x, g):
    xf = x.astype(jnp.float32)
    y = xf * lax.rsqrt(jnp.mean(xf * xf, axis=-1, keepdims=True) + EPS)
    return y.astype(x.dtype) * g

def rope(x, pos):
    r = x.shape[-1]
    inv_freq = ROPE_THETA ** (-jnp.arange(0, r, 2, dtype=jnp.float32) / r)
    ang = pos.astype(jnp.float32)[:, None] * inv_freq[None, :]
    cos = jnp.cos(ang).astype(x.dtype)
    sin = jnp.sin(ang).astype(x.dtype)
    x1, x2 = x[..., : r // 2], x[..., r // 2:]
    return jnp.concatenate([x1 * cos - x2 * sin, x2 * cos + x1 * sin], axis=-1)

def causal_block_attention(q, k, v, scale, log_decay_cum=None):
    b, h, s, dk = q.shape
    dv = v.shape[-1]
    nb = s // BLOCK_Q
    qb = q.reshape(b, h, nb, BLOCK_Q, dk).transpose(2, 0, 1, 3, 4)
    kpos = jnp.arange(s)
    xs = (jnp.arange(nb), qb)
    if log_decay_cum is not None:
        xs = xs + (log_decay_cum.reshape(b, h, nb, BLOCK_Q).transpose(2, 0, 1, 3),)

    def one_block(args):
        i, q_blk = args[0], args[1]
        sc = jnp.einsum('bhqd,bhkd->bhqk', q_blk, k, preferred_element_type=jnp.float32) * scale
        if log_decay_cum is not None:
            c_blk = args[2]
            sc = sc + c_blk[..., :, None] - log_decay_cum[..., None, :].astype(jnp.float32)
        qpos = i * BLOCK_Q + jnp.arange(BLOCK_Q)
        sc = jnp.where(kpos[None, :] <= qpos[:, None], sc, -jnp.inf)
        p = jax.nn.softmax(sc, axis=-1).astype(v.dtype)
        return jnp.einsum('bhqk,bhkd->bhqd', p, v)

    out = lax.map(one_block, xs)
    return out.transpose(1, 2, 0, 3, 4).reshape(b, h, s, dv)

def mla_mixer(q_a, kv_a, k_rope, q_a_norm, w_q_b, kv_a_norm, w_kv_b, pos):
    b, s, _ = q_a.shape
    q = (rmsnorm(q_a, q_a_norm) @ w_q_b).reshape(b, s, MLA_HEADS, MLA_NOPE + MLA_ROPE).transpose(0, 2, 1, 3)
    q_nope, q_pe = q[..., :MLA_NOPE], rope(q[..., MLA_NOPE:], pos)
    kv = (rmsnorm(kv_a, kv_a_norm) @ w_kv_b).reshape(b, s, MLA_HEADS, MLA_NOPE + MLA_V).transpose(0, 2, 1, 3)
    k_nope, v = kv[..., :MLA_NOPE], kv[..., MLA_NOPE:]
    k_pe = jnp.broadcast_to(rope(k_rope, pos)[:, None], (b, MLA_HEADS, s, MLA_ROPE))
    qf = jnp.concatenate([q_nope, q_pe], axis=-1)
    kf = jnp.concatenate([k_nope, k_pe], axis=-1)
    o = causal_block_attention(qf, kf, v, 1.0 / math.sqrt(MLA_NOPE + MLA_ROPE))
    return o.transpose(0, 2, 1, 3).reshape(b, s, MLA_HEADS * MLA_V)

def pool_mixer(u, pool_w, pool_scale):
    b, s, _ = u.shape
    ng = len(POOL_WINDOWS)
    ug = u.reshape(b, s, ng, POOL_GROUP)
    cs = jnp.cumsum(ug.astype(jnp.float32), axis=1)
    count = jnp.arange(1, s + 1, dtype=jnp.float32)
    means = []
    for g, w in enumerate(POOL_WINDOWS):
        c = cs[:, :, g]
        prev = jnp.pad(c[:, : s - w], ((0, 0), (w, 0), (0, 0)))
        means.append((c - prev) / jnp.minimum(count, float(w))[None, :, None])
    pooled = jnp.stack(means, axis=2).astype(u.dtype) - ug
    y = jnp.einsum('bsgc,gcd->bsgd', pooled, pool_w)
    return y.reshape(b, s, POOL_WIDTH) * pool_scale

def fox_mixer(qkv, f_logit, fox_b_f):
    b, s, _ = qkv.shape
    qkv = qkv.reshape(b, s, 3, FOX_HEADS, FOX_HEAD_DIM).transpose(2, 0, 3, 1, 4)
    q, k, v = qkv[0], qkv[1], qkv[2]
    log_f = jax.nn.log_sigmoid((f_logit + fox_b_f).astype(jnp.float32))
    cum = jnp.cumsum(log_f, axis=1).transpose(0, 2, 1)
    o = causal_block_attention(q, k, v, 1.0 / math.sqrt(FOX_HEAD_DIM), cum)
    return o.transpose(0, 2, 1, 3).reshape(b, s, FOX_HEADS * FOX_HEAD_DIM)

def swiglu(h, w_gu, w_down):
    gu = h @ w_gu
    g, u = gu[..., :D_FF], gu[..., D_FF:]
    return (jax.nn.silu(g) * u) @ w_down

def hybrid_mixing(h, w_in, q_a_norm, w_q_b, kv_a_norm, w_kv_b, pool_w, pool_scale, fox_b_f, w_out, pos):
    z = h @ w_in
    o0 = 0
    o1 = o0 + IN_Q_A
    o2 = o1 + IN_KV_A
    o3 = o2 + IN_K_ROPE
    o4 = o3 + IN_POOL
    o5 = o4 + IN_FOX_QKV
    o6 = o5 + IN_FOX_F
    ya = mla_mixer(z[..., o0:o1], z[..., o1:o2], z[..., o2:o3], q_a_norm, w_q_b, kv_a_norm, w_kv_b, pos)
    yb = pool_mixer(z[..., o3:o4], pool_w, pool_scale)
    yc = fox_mixer(z[..., o4:o5], z[..., o5:o6], fox_b_f)
    return jnp.concatenate([ya, yb, yc], axis=-1) @ w_out

def first_inputs(seed: int = 0) -> dict:
    key = jax.random.key(seed)
    ks = jax.random.split(key, 24)
    L, D, F = DEPTH, D_MODEL, D_FF
    f32 = jnp.float32

    def nrm(k, shape, fan_in):
        return jax.random.normal(k, shape, f32) * (fan_in ** -0.5)

    def gain(k, shape):
        return 1.0 + 0.02 * jax.random.normal(k, shape, f32)

    return {
        "x": jax.random.normal(ks[0], (BATCH, SEQ, D), f32),
        "ffn1_norm": gain(ks[1], (L, D)),
        "ffn1_w_gu": nrm(ks[2], (L, D, 2 * F), D),
        "ffn1_w_down": nrm(ks[3], (L, F, D), F),
        "mix_norm": gain(ks[4], (L, D)),
        "w_in": nrm(ks[5], (L, D, N_IN), D),
        "q_a_norm": gain(ks[6], (L, MLA_Q_RANK)),
        "w_q_b": nrm(ks[7], (L, MLA_Q_RANK, MLA_HEADS * (MLA_NOPE + MLA_ROPE)), MLA_Q_RANK),
        "kv_a_norm": gain(ks[8], (L, MLA_KV_RANK)),
        "w_kv_b": nrm(ks[9], (L, MLA_KV_RANK, MLA_HEADS * (MLA_NOPE + MLA_V)), MLA_KV_RANK),
        "pool_w": nrm(ks[10], (L, len(POOL_WINDOWS), POOL_GROUP, POOL_GROUP), POOL_GROUP),
        "pool_scale": gain(ks[11], (L, POOL_WIDTH)),
        "fox_b_f": FOX_GATE_BIAS_INIT + 0.5 * jax.random.normal(ks[12], (L, FOX_HEADS), f32),
        "w_out": nrm(ks[13], (L, D_MIX, D), D_MIX),
        "ffn2_norm": gain(ks[14], (L, D)),
        "ffn2_w_gu": nrm(ks[15], (L, D, 2 * F), D),
        "ffn2_w_down": nrm(ks[16], (L, F, D), F),
        "final_norm": gain(ks[17], (D,)),
    }

def first_block(x, ffn1_norm, ffn1_w_gu, ffn1_w_down, mix_norm, w_in, q_a_norm, w_q_b, kv_a_norm, w_kv_b,
              pool_w, pool_scale, fox_b_f, w_out, ffn2_norm, ffn2_w_gu, ffn2_w_down, final_norm):
    pos = jnp.arange(x.shape[1], dtype=jnp.int32)
    for l in range(DEPTH):
        x = x + 0.5 * swiglu(rmsnorm(x, ffn1_norm[l]), ffn1_w_gu[l], ffn1_w_down[l])
        x = x + hybrid_mixing(rmsnorm(x, mix_norm[l]), w_in[l], q_a_norm[l], w_q_b[l], kv_a_norm[l], w_kv_b[l],
                              pool_w[l], pool_scale[l], fox_b_f[l], w_out[l], pos)
        x = x + 0.5 * swiglu(rmsnorm(x, ffn2_norm[l]), ffn2_w_gu[l], ffn2_w_down[l])
    return rmsnorm(x, final_norm)


DEPTH_2 = 1

HEAD_DIM = 64
ATTN_WIDTH = 3 * D_MODEL // 8
ATTN_HEADS = ATTN_WIDTH // HEAD_DIM
ATTN_GROUPS = ((128, 1), (512, 4), (2048, 16))
ATTN_HEADS_PER_GROUP = ATTN_HEADS // len(ATTN_GROUPS)
RWKV_WIDTH = 3 * D_MODEL // 8
RWKV_HEADS = RWKV_WIDTH // HEAD_DIM
DECAY_LORA = 64
AAA_LORA = 64
GATE_LORA = 128
RWKV_IN = 3 * RWKV_WIDTH + DECAY_LORA + AAA_LORA + GATE_LORA
RWKV_SPLITS = (RWKV_WIDTH, 2 * RWKV_WIDTH, 3 * RWKV_WIDTH,
               3 * RWKV_WIDTH + DECAY_LORA, 3 * RWKV_WIDTH + DECAY_LORA + AAA_LORA)
GN_EPS = 64e-5
SSM_WIDTH = D_MODEL // 4
SSM_GROUP_CH = 16
SSM_GROUPS = SSM_WIDTH // SSM_GROUP_CH
SSM_STATE = 64
STEP_MIN = 1e-3
STEP_MAX = 1e-1
N_BRANCH = 3
ATTN_IN = 3 * ATTN_WIDTH
RWKV_OFF = ATTN_IN
SSM_OFF = RWKV_OFF + RWKV_IN
GATE_OFF = SSM_OFF + SSM_WIDTH
N_IN_2 = GATE_OFF + N_BRANCH * D_MODEL
FFN_HIDDEN = ((8 * D_MODEL + 3 * 256 - 1) // (3 * 256)) * 256
NORM_EPS = 1e-6


def rmsnorm_2(z, gain):
    zf = z.astype(jnp.float32)
    y = zf * lax.rsqrt(jnp.mean(zf * zf, axis=-1, keepdims=True) + NORM_EPS) * gain.astype(jnp.float32)
    return y.astype(z.dtype)

def token_shift(z):
    return jnp.pad(z, ((0, 0), (1, 0), (0, 0)))[:, :-1]

def dilated_window_attention(q, k, v, window, dilation):
    bsz, s, h, e = q.shape
    n_back = window // dilation
    span = n_back * dilation
    s_pad = -(-s // span) * span
    nb = s_pad // span

    def blocks(z):
        z = jnp.pad(z, ((0, 0), (0, s_pad - s), (0, 0), (0, 0)))
        return z.reshape(bsz, nb, n_back, dilation, h, e)

    def with_prev(z):
        prev = jnp.pad(z, ((0, 0), (1, 0), (0, 0), (0, 0), (0, 0), (0, 0)))[:, :-1]
        return jnp.concatenate([prev, z], axis=2)

    qb = blocks(q).astype(jnp.float32)
    kb = with_prev(blocks(k)).astype(jnp.float32)
    vb = with_prev(blocks(v)).astype(jnp.float32)
    scores = jnp.einsum('bnqrhe,bnkrhe->bnrhqk', qb, kb) * (e ** -0.5)
    qi = jnp.arange(n_back)[:, None]
    kj = jnp.arange(2 * n_back)[None, :]
    band = (kj >= qi) & (kj <= qi + n_back)
    has_prev = (jnp.arange(nb) > 0)[:, None, None] | (jnp.arange(2 * n_back) >= n_back)[None, None, :]
    mask = band[None] & has_prev
    scores = jnp.where(mask[None, :, None, None], scores, -jnp.inf)
    mx = jnp.max(scores, axis=-1, keepdims=True)
    p = jnp.exp(scores - mx)
    den = jnp.sum(p, axis=-1, keepdims=True)
    out = jnp.einsum('bnrhqk,bnkrhe->bnqrhe', p / den, vb)
    lse = (mx + jnp.log(den))[..., 0]
    out = out.reshape(bsz, s_pad, h, e)[:, :s]
    lse = jnp.transpose(lse, (0, 1, 4, 2, 3)).reshape(bsz, s_pad, h)[:, :s]
    return out, lse

def dilated_mixture_attention(p_attn):
    bsz, s, _ = p_attn.shape
    q, k, v = (t.reshape(bsz, s, ATTN_HEADS, HEAD_DIM) for t in jnp.split(p_attn, 3, axis=-1))
    outs, lses = [], []
    for g, (window, dilation) in enumerate(ATTN_GROUPS):
        hs = slice(g * ATTN_HEADS_PER_GROUP, (g + 1) * ATTN_HEADS_PER_GROUP)
        o, lse = dilated_window_attention(q[:, :, hs], k[:, :, hs], v[:, :, hs], window, dilation)
        outs.append(o)
        lses.append(lse)
    alpha = jax.nn.softmax(jnp.stack(lses, axis=0), axis=0)
    o = jnp.concatenate([o_g * alpha[g][..., None] for g, o_g in enumerate(outs)], axis=2)
    return o.reshape(bsz, s, ATTN_WIDTH)

def wkv7_scan(r, w, k, v, a, b):
    bsz, _, h, e = r.shape

    def step(state, inp):
        r_t, w_t, k_t, v_t, a_t, b_t = inp
        sa = jnp.einsum('bhij,bhj->bhi', state, a_t)
        state = (state * w_t[:, :, None, :] + sa[..., None] * b_t[:, :, None, :]
                 + v_t[..., None] * k_t[:, :, None, :])
        return state, jnp.einsum('bhij,bhj->bhi', state, r_t)

    xs = tuple(jnp.moveaxis(t, 1, 0) for t in (r, w, k, v, a, b))
    _, y = lax.scan(step, jnp.zeros((bsz, h, e, e), jnp.float32), xs)
    return jnp.moveaxis(y, 0, 1)

def rwkv7_time_mix(p_rwkv, shift_mix, w0, w2, a0, a2, g2, k_k, k_a, r_k, ln_w, ln_b):
    bsz, s, _ = p_rwkv.shape
    z = p_rwkv.astype(jnp.float32)
    z = z + (token_shift(z) - z) * shift_mix
    r, k, v, xw, xa, xg = jnp.split(z, RWKV_SPLITS, axis=-1)
    w = -jax.nn.softplus(-(w0 + jnp.tanh(xw) @ w2)) - 0.5
    decay = jnp.exp(-jnp.exp(w))
    a = jax.nn.sigmoid(a0 + xa @ a2)
    g = jax.nn.sigmoid(xg) @ g2

    def heads(t):
        return t.reshape(bsz, s, RWKV_HEADS, HEAD_DIM)

    kk = heads(k * k_k)
    kk = kk / jnp.maximum(jnp.linalg.norm(kk, axis=-1, keepdims=True), 1e-12)
    k = k * (1.0 + (a - 1.0) * k_a)
    r_h, k_h, v_h, a_h = heads(r), heads(k), heads(v), heads(a)
    y = wkv7_scan(r_h, heads(decay), k_h, v_h, -kk, kk * a_h)
    mu = jnp.mean(y, axis=-1, keepdims=True)
    var = jnp.mean(jnp.square(y - mu), axis=-1, keepdims=True)
    y = ((y - mu) * lax.rsqrt(var + GN_EPS)).reshape(bsz, s, RWKV_WIDTH) * ln_w + ln_b
    bonus = jnp.sum(r_h * k_h * r_k, axis=-1, keepdims=True) * v_h
    return (y + bonus.reshape(bsz, s, RWKV_WIDTH)) * g

def _complex_linear_combine(e1, e2):
    a1r, a1i, b1r, b1i = e1
    a2r, a2i, b2r, b2i = e2
    return (a2r * a1r - a2i * a1i, a2r * a1i + a2i * a1r,
            a2r * b1r - a2i * b1i + b2r, a2r * b1i + a2i * b1r + b2i)

def s5_glu(p_ssm, a_re, a_im, log_step, b_re, b_im, c_re, c_im, d_skip, w_val, w_gate):
    bsz, s, _ = p_ssm.shape
    u = p_ssm.astype(jnp.float32).reshape(bsz, s, SSM_GROUPS, SSM_GROUP_CH)
    lam_re = a_re.astype(jnp.float32)
    lam_im = a_im.astype(jnp.float32)
    step = jnp.exp(log_step.astype(jnp.float32))[:, None]
    mag = jnp.exp(lam_re * step)
    ang = lam_im * step
    abar_re, abar_im = mag * jnp.cos(ang), mag * jnp.sin(ang)
    inv = 1.0 / (lam_re * lam_re + lam_im * lam_im)
    f_re = ((abar_re - 1.0) * lam_re + abar_im * lam_im) * inv
    f_im = (abar_im * lam_re - (abar_re - 1.0) * lam_im) * inv
    bbar_re = f_re[..., None] * b_re - f_im[..., None] * b_im
    bbar_im = f_re[..., None] * b_im + f_im[..., None] * b_re
    bu_re = jnp.einsum('bsgc,gpc->bsgp', u, bbar_re)
    bu_im = jnp.einsum('bsgc,gpc->bsgp', u, bbar_im)
    shape = bu_re.shape
    _, _, x_re, x_im = lax.associative_scan(
        _complex_linear_combine,
        (jnp.broadcast_to(abar_re, shape), jnp.broadcast_to(abar_im, shape), bu_re, bu_im),
        axis=1)
    y = (jnp.einsum('bsgp,gcp->bsgc', x_re, c_re) - jnp.einsum('bsgp,gcp->bsgc', x_im, c_im)
         + d_skip.reshape(SSM_GROUPS, SSM_GROUP_CH) * u)
    zg = jax.nn.gelu(y.reshape(bsz, s, SSM_WIDTH))
    return (zg @ w_val) * jax.nn.sigmoid(zg @ w_gate)

def swiglu_2(u, w_gate_up, w_down):
    a, b = jnp.split(u @ w_gate_up, 2, axis=-1)
    return (jax.nn.silu(a) * b) @ w_down

def second_inputs(seed: int = 0) -> dict:
    key = jax.random.key(seed)
    ks = iter(jax.random.split(key, 40))
    f32 = jnp.float32

    def nrm(shape, scale):
        return jax.random.normal(next(ks), shape, f32) * scale

    def uni(shape, lo, hi):
        return jax.random.uniform(next(ks), shape, f32, lo, hi)

    L, D = DEPTH_2, D_MODEL
    G, P, C = SSM_GROUPS, SSM_STATE, SSM_GROUP_CH
    return {
        "x": nrm((BATCH, SEQ, D), 1.0),
        "norm_mix": 1.0 + nrm((L, D), 0.02),
        "w_in": nrm((L, D, N_IN_2), D ** -0.5),
        "rwkv_shift_mix": uni((L, RWKV_IN), 0.0, 1.0),
        "rwkv_w0": uni((L, RWKV_WIDTH), -6.0, -1.0),
        "rwkv_w2": nrm((L, DECAY_LORA, RWKV_WIDTH), 0.1 * DECAY_LORA ** -0.5),
        "rwkv_a0": nrm((L, RWKV_WIDTH), 0.1),
        "rwkv_a2": nrm((L, AAA_LORA, RWKV_WIDTH), 0.5 * AAA_LORA ** -0.5),
        "rwkv_g2": nrm((L, GATE_LORA, RWKV_WIDTH), GATE_LORA ** -0.5),
        "rwkv_k_k": 0.85 + nrm((L, RWKV_WIDTH), 0.02),
        "rwkv_k_a": 1.0 + nrm((L, RWKV_WIDTH), 0.02),
        "rwkv_r_k": nrm((L, RWKV_HEADS, HEAD_DIM), 0.1),
        "rwkv_ln_w": 1.0 + nrm((L, RWKV_WIDTH), 0.02),
        "rwkv_ln_b": nrm((L, RWKV_WIDTH), 0.02),
        "ssm_a_re": -0.5 + nrm((L, G, P), 0.01),
        "ssm_a_im": jnp.pi * jnp.arange(P, dtype=f32) + nrm((L, G, P), 0.01),
        "ssm_log_step": uni((L, G), math.log(STEP_MIN), math.log(STEP_MAX)),
        "ssm_b_re": nrm((L, G, P, C), (2 * C) ** -0.5),
        "ssm_b_im": nrm((L, G, P, C), (2 * C) ** -0.5),
        "ssm_c_re": nrm((L, G, C, P), P ** -0.5),
        "ssm_c_im": nrm((L, G, C, P), P ** -0.5),
        "ssm_d": nrm((L, SSM_WIDTH), 1.0),
        "ssm_glu_val": nrm((L, SSM_WIDTH, SSM_WIDTH), SSM_WIDTH ** -0.5),
        "ssm_glu_gate": nrm((L, SSM_WIDTH, SSM_WIDTH), SSM_WIDTH ** -0.5),
        "w_branch_attn": nrm((L, ATTN_WIDTH, D), ATTN_WIDTH ** -0.5),
        "w_branch_rwkv": nrm((L, RWKV_WIDTH, D), RWKV_WIDTH ** -0.5),
        "w_branch_ssm": nrm((L, SSM_WIDTH, D), SSM_WIDTH ** -0.5),
        "w_out": nrm((L, D, D), D ** -0.5),
        "norm_ffn": 1.0 + nrm((L, D), 0.02),
        "ffn_w_gate_up": nrm((L, D, 2 * FFN_HIDDEN), D ** -0.5),
        "ffn_w_down": nrm((L, FFN_HIDDEN, D), FFN_HIDDEN ** -0.5),
        "norm_final": 1.0 + nrm((D,), 0.02),
    }

def second_block(x, norm_mix, w_in, rwkv_shift_mix, rwkv_w0, rwkv_w2, rwkv_a0, rwkv_a2, rwkv_g2,
              rwkv_k_k, rwkv_k_a, rwkv_r_k, rwkv_ln_w, rwkv_ln_b, ssm_a_re, ssm_a_im, ssm_log_step,
              ssm_b_re, ssm_b_im, ssm_c_re, ssm_c_im, ssm_d, ssm_glu_val, ssm_glu_gate,
              w_branch_attn, w_branch_rwkv, w_branch_ssm, w_out, norm_ffn, ffn_w_gate_up,
              ffn_w_down, norm_final):
    h = x
    for l in range(DEPTH_2):
        u = rmsnorm_2(h, norm_mix[l])
        p = u @ w_in[l]
        bsz, s, _ = p.shape
        y_attn = dilated_mixture_attention(p[..., :ATTN_IN]) @ w_branch_attn[l]
        y_rwkv = rwkv7_time_mix(p[..., RWKV_OFF:SSM_OFF], rwkv_shift_mix[l], rwkv_w0[l], rwkv_w2[l],
                                rwkv_a0[l], rwkv_a2[l], rwkv_g2[l], rwkv_k_k[l], rwkv_k_a[l],
                                rwkv_r_k[l], rwkv_ln_w[l], rwkv_ln_b[l]) @ w_branch_rwkv[l]
        y_ssm = s5_glu(p[..., SSM_OFF:GATE_OFF], ssm_a_re[l], ssm_a_im[l], ssm_log_step[l],
                       ssm_b_re[l], ssm_b_im[l], ssm_c_re[l], ssm_c_im[l], ssm_d[l],
                       ssm_glu_val[l], ssm_glu_gate[l]) @ w_branch_ssm[l]
        gates = jax.nn.sigmoid(p[..., GATE_OFF:].astype(jnp.float32)).reshape(bsz, s, N_BRANCH, D_MODEL)
        merged = gates[:, :, 0] * y_attn + gates[:, :, 1] * y_rwkv + gates[:, :, 2] * y_ssm
        h = h + (merged @ w_out[l]).astype(h.dtype)
        u = rmsnorm_2(h, norm_ffn[l])
        h = h + swiglu_2(u, ffn_w_gate_up[l], ffn_w_down[l]).astype(h.dtype)
    return rmsnorm_2(h, norm_final)


_first_inputs = second_inputs


def second_inputs(seed=0):
    import zlib

    import numpy as np

    out = dict(_first_inputs(seed))
    spreads = {}
    factors = {'norm_mix': 3.94,
     'rwkv_w2': 64.0,
     'rwkv_a0': 3.808,
     'rwkv_k_k': 64.0,
     'rwkv_k_a': 8.0,
     'rwkv_ln_w': 64.0,
     'rwkv_ln_b': 64.0,
     'ssm_a_re': 64.0,
     'ssm_a_im': 26.376,
     'ssm_log_step': 26.904,
     'ssm_b_re': 36.352,
     'ssm_b_im': 37.024,
     'ssm_c_re': 37.4,
     'ssm_c_im': 37.216,
     'norm_ffn': 24.56,
     'norm_final': 8.398,
     'ssm_glu_gate': 2.741}
    for name, (base, spread) in spreads.items():
        noise = np.random.default_rng([zlib.crc32(name.encode()), seed]).standard_normal(out[name].shape)
        drawn = base * np.exp(spread * noise) if base else spread * noise
        out[name] = jnp.asarray(drawn.astype(out[name].dtype))
    for name, factor in factors.items():
        out[name] = (out[name] * factor).astype(out[name].dtype)
    return out


_narrow_inputs = second_inputs


def second_inputs(seed=0):
    out = dict(_narrow_inputs(seed))
    wider = {'rwkv_k_k': 11.08, 'rwkv_ln_w': 3.81, 'rwkv_ln_b': 3.92, 'norm_final': 3.26}
    for name, times in wider.items():
        mean = out[name].mean()
        out[name] = (mean + times * (out[name] - mean)).astype(out[name].dtype)
    return out


def setup_inputs(seed=0):
    out = dict(first_inputs(seed))
    for name, value in second_inputs(seed + 1).items():
        if name != "x":
            out[name + "_2"] = value
    return out


def reference(
    x, ffn1_norm, ffn1_w_gu, ffn1_w_down, mix_norm, w_in, q_a_norm, w_q_b, kv_a_norm, w_kv_b,
    pool_w, pool_scale, fox_b_f, w_out, ffn2_norm, ffn2_w_gu, ffn2_w_down, final_norm,
    norm_mix_2, w_in_2, rwkv_shift_mix_2, rwkv_w0_2, rwkv_w2_2, rwkv_a0_2, rwkv_a2_2, rwkv_g2_2,
    rwkv_k_k_2, rwkv_k_a_2, rwkv_r_k_2, rwkv_ln_w_2, rwkv_ln_b_2, ssm_a_re_2, ssm_a_im_2,
    ssm_log_step_2, ssm_b_re_2, ssm_b_im_2, ssm_c_re_2, ssm_c_im_2, ssm_d_2, ssm_glu_val_2,
    ssm_glu_gate_2, w_branch_attn_2, w_branch_rwkv_2, w_branch_ssm_2, w_out_2, norm_ffn_2,
    ffn_w_gate_up_2, ffn_w_down_2, norm_final_2,
):
    x = first_block(
        x, ffn1_norm, ffn1_w_gu, ffn1_w_down, mix_norm, w_in, q_a_norm, w_q_b, kv_a_norm,
        w_kv_b, pool_w, pool_scale, fox_b_f, w_out, ffn2_norm, ffn2_w_gu, ffn2_w_down,
        final_norm,
    )
    return second_block(
        x, norm_mix_2, w_in_2, rwkv_shift_mix_2, rwkv_w0_2, rwkv_w2_2, rwkv_a0_2, rwkv_a2_2,
        rwkv_g2_2, rwkv_k_k_2, rwkv_k_a_2, rwkv_r_k_2, rwkv_ln_w_2, rwkv_ln_b_2, ssm_a_re_2,
        ssm_a_im_2, ssm_log_step_2, ssm_b_re_2, ssm_b_im_2, ssm_c_re_2, ssm_c_im_2, ssm_d_2,
        ssm_glu_val_2, ssm_glu_gate_2, w_branch_attn_2, w_branch_rwkv_2, w_branch_ssm_2,
        w_out_2, norm_ffn_2, ffn_w_gate_up_2, ffn_w_down_2, norm_final_2,
    )


_drawn_inputs = setup_inputs


def setup_inputs(seed=0):
    import zlib

    import numpy as np

    out = dict(_drawn_inputs(seed))
    spreads = {}
    factors = {'q_a_norm': 7.133, 'kv_a_norm': 4.736}
    for name, (base, spread) in spreads.items():
        noise = np.random.default_rng([zlib.crc32(name.encode()), seed]).standard_normal(out[name].shape)
        drawn = base * np.exp(spread * noise) if base else spread * noise
        out[name] = jnp.asarray(drawn.astype(out[name].dtype))
    for name, factor in factors.items():
        out[name] = (out[name] * factor).astype(out[name].dtype)
    return out
```

```python
from contextlib import ExitStack

import concourse.bass as bass
from concourse import mybir

ALU = mybir.AluOpType
ACT = mybir.ActivationFunctionType
AX = mybir.AxisListType
F32 = mybir.dt.float32
BF16 = mybir.dt.bfloat16

P = 128
S = 512
D = 1024
KD = D // P
FF = 2816
NJ = FF // P
HALF = D // 2
LAYERS = 2
EPS = 1e-6
NT = S // P

QR, KVR, ROPE, NOPE = 256, 128, 32, 64
HEADS = 6
HD = 64
MLA_SCALE = (NOPE + ROPE) ** -0.5
FOX_SCALE = HD ** -0.5
UNITS = 2 * HEADS * NT

SLOT = 8 * 384
MIX_ITEMS = 10
LAYER_ITEMS = 2 * NJ + MIX_ITEMS

C_ID, C_ONE, C_COS, C_SIN, C_RC, C_EPS = 0, 128, 256, 768, 1280, 2304
C_W = 2308
M_QB, M_KV, M_PW = 0, 1536, 2304
M_W = 2560
G_N1, G_NM, G_N2, G_QA, G_KVA, G_PS, G_FB, G_FIN = 0, 8, 16, 24, 26, 27, 29, 30
G_W = 38



RW = 384
CHUNK = 64
KAPPA = 0.6065306597126334
B2_ITEMS = 24
UNITS2 = 6 * NT
W2_WA, W2_G, W2_GV, W2_GG, W2_C, W2_B = 0, 384, 768, 1280, 1792, 2048
(H_NM, H_NF, H_FIN, H_MIX, H_W0, H_A0, H_KK, H_KA, H_RK, H_LW, H_LB, H_AR, H_AI, H_LS, H_D) = (
    0, 8, 16, 24, 35, 38, 41, 44, 47, 50, 53, 56, 64, 72, 80)
G2_W = 82
PRODUCTS = (["xwa", "xg", "r0", "k0", "v0"] + ["lw0", "lw1", "lw2", "la0", "la1", "la2", "lg0", "lg1", "lg2"]
            + ["r1", "k1", "v1", "kn0", "bn0", "r2", "k2", "v2", "kn1", "bn1", "aq0", "aq1", "aq2", "kn2", "bn2",
               "ak0", "ak1", "ak2", "av0", "av1", "av2", "su0", "su1", "av2t"]
            + [f"t{n}{t}" for n in "ABKV" for t in range(NT)])
NUM = {n: i for i, n in enumerate(PRODUCTS)}
MM_STEPS = ("M12a", "M12b", "M34a", "M34b", "NN2", "M5a", "M5b", "Y2", "NN4", "Y4", "N8", "X1", "Y8", "TF1", "Y32",
            "TF2", "XT", "GW", "PTa", "PTb", "S0a", "S0b", "S1a", "S1b", "Ua", "Ub", "Y")
VEC_STEPS = ("N", "M34", "Y1", "M5", "Y2", "Y4", "Y8", "Y32", "XT", "PT", "Z0", "Z1", "U")
ACT_STEPS = ("N2", "N4", "N8", "X1", "TF1", "TF2", "GW", "GT", "Y")


def done(steps, name, t, p):
    return (t * len(steps) + steps.index(name)) * 3 + p + 1

TWO_PI = 6.283185307179586
PI_HI = 6.28125
PI_LO = TWO_PI - PI_HI
ROUND = 12582912.0
GELU_C = 0.7978845608028654
W_STEPS = 283


class Chain:

    def __init__(self, eng, sem, base, steps):
        self.eng, self.sem, self.base, self.steps, self.k = eng, sem, base, steps, 0

    def __call__(self, ins):
        self.k += 1
        ins.then_inc(self.sem, 1)
        self.eng.wait_ge(self.sem, self.base + self.k)

    def end(self):
        assert self.k == self.steps, (self.k, self.steps)


def used(n):
    return n + 3


def build(nc, t_in, out):
    with ExitStack() as ctx:
        def sb(name, shape, dt=F32):
            return ctx.enter_context(nc.sbuf_tensor(name, shape, dt))

        def sem(name):
            return ctx.enter_context(nc.semaphore(name))

        psum = ctx.enter_context(nc.psum_tensor("psum", [P, 8, 512], F32))
        x = sb("x", [P, KD, S])
        h = sb("h", [P, KD, S])
        hid = sb("hid", [P, 24, S])
        ring = sb("ring", [P, 2, SLOT])
        wdr = sb("wdr", [P, 2, HALF])
        d2 = sb("d2", [P, NJ, HALF])
        mixw = sb("mixw", [P, M_W])
        gains = sb("gains", [P, LAYERS, G_W])
        cst = sb("cst", [P, C_W])
        cstb = sb("cstb", [P, 4, P], BF16)
        scr = sb("scr", [P, 6720])
        tmp = scr[:, 0:6 * S].rearrange("p (a c) -> p a c", a=6)
        probs = scr[:, 6 * S:9 * S].rearrange("p (a c) -> p a c", a=3)
        upad = scr[:, 4608:5664].rearrange("p (a c) -> p a c", a=2)
        wsum = scr[:, 5664:6720].rearrange("p (a c) -> p a c", a=2)
        stat = sb("stat", [P, 3, 4])
        ident = cst[:, C_ID:C_ID + P]
        ones = cst[:, C_ONE:C_ONE + P]
        cos = cst[:, C_COS:C_COS + S]
        sin = cst[:, C_SIN:C_SIN + S]
        eps = cst[:, C_EPS:C_EPS + 1]
        y = d2[:, 0:8, :]
        vt = [d2[:, 8 + 3 * b:11 + 3 * b, :].rearrange("p a b -> p (a b)").rearrange(
            "p (t c) -> p t c", t=NT) for b in range(2)]
        pt = [d2[:, 14 + 4 * b:18 + 4 * b, :] for b in range(2)]

        cst_in = sem("cst_in")
        cstb_in = sem("cstb_in")
        gains_in = sem("gains_in")
        x_in = sem("x_in")
        ring_in = [sem("ring_in0"), sem("ring_in1")]
        wdr_in = [sem("wdr_in0"), sem("wdr_in1")]
        d2_in = sem("d2_in")
        mixw_in = sem("mixw_in")
        aug_in = sem("aug_in")
        out_done = sem("out_done")
        ring_free = sem("ring_free")
        wdr_free = sem("wdr_free")
        sq_ready = sem("sq_ready")
        sumsq_ready = sem("sumsq_ready")
        rms_ready = sem("rms_ready")
        pads_zero = sem("pads_zero")
        rstd_ready = sem("rstd_ready")
        h_ready = sem("h_ready")
        x_upd = sem("x_upd")
        gate_ready = sem("gate_ready")
        silu_ready = sem("silu_ready")
        hid_ready = sem("hid_ready")
        down_ready = sem("down_ready")
        p_kv = sem("p_kv")
        p_qa = sem("p_qa")
        p_pool = sem("p_pool")
        p_foxqk = sem("p_foxqk")
        p_foxv = sem("p_foxv")
        p_sw = sem("p_sw")
        p_mlaq = sem("p_mlaq")
        p_mlak = sem("p_mlak")
        p_mlav = sem("p_mlav")
        lat_sq = sem("lat_sq")
        lat_ss = sem("lat_ss")
        lat_rms = sem("lat_rms")
        lat_n = sem("lat_n")
        pool_in = sem("pool_in")
        pooled = sem("pooled")
        p_pooly = sem("p_pooly")
        pool_out = sem("pool_out")
        kr_done = sem("kr_done")
        kpe_put = sem("kpe_put")
        fz_ready = sem("fz_ready")
        fe_ready = sem("fe_ready")
        cum_ready = sem("cum_ready")
        foxq_put = sem("foxq_put")
        foxk_put = sem("foxk_put")
        foxv_put = sem("foxv_put")
        mlaqn_put = sem("mlaqn_put")
        mlaqr_put = sem("mlaqr_put")
        mlak_put = sem("mlak_put")
        mlav_put = sem("mlav_put")
        scores = sem("scores")
        nmax = sem("nmax")
        expd = sem("expd")
        rsum = sem("rsum")
        normd = sem("normd")
        turned = sem("turned")
        pt_put = sem("pt_put")
        yh_ready = sem("yh_ready")
        y_put = sem("y_put")
        wout_ready = sem("wout_ready")
        carrier = sem("carrier")
        vstep = sem("vstep")
        astep = sem("astep")
        gstep = sem("gstep")
        VSTEPS, GSTEPS = 26, 12


        made = sem("made")
        read = sem("read")
        mixw2_in = sem("mixw2_in")
        mixed = sem("mixed")
        lora_act = sem("lora_act")
        kk_in = sem("kk_in")
        kk_sq = sem("kk_sq")
        bonus_in = sem("bonus_in")
        decay_in = sem("decay_in")
        decay_exp = sem("decay_exp")
        rwkv_fm = sem("rwkv_fm")
        bonus_put = sem("bonus_put")
        w_step = sem("w_step")
        d_scores = sem("d_scores")
        d_nmax = sem("d_nmax")
        d_exp = sem("d_exp")
        d_norm = sem("d_norm")
        d_turned = sem("d_turned")
        d_put = sem("d_put")
        d_out = sem("d_out")
        d_ln = sem("d_ln")
        d_lse = sem("d_lse")
        d_lseb = sem("d_lseb")
        d_diff = sem("d_diff")
        d_wexp = sem("d_wexp")
        d_rsum = sem("d_rsum")
        attn_y = sem("attn_y")
        rw_mm = sem("rw_mm")
        rw_vec = sem("rw_vec")
        rw_act = sem("rw_act")
        gn_mm = sem("gn_mm")
        gn_act = sem("gn_act")
        gn_in = sem("gn_in")
        rwkv_y = sem("rwkv_y")
        z_zero = sem("z_zero")
        s_par = sem("s_par")
        s_trig = sem("s_trig")
        s_bu = sem("s_bu")
        s_rot = sem("s_rot")
        s_back = sem("s_back")
        s_c = sem("s_c")
        s_cw = sem("s_cw")
        s_ym = sem("s_ym")
        s_gl = sem("s_gl")
        s_gla = sem("s_gla")
        glu_mm = sem("glu_mm")
        glu_act = sem("glu_act")
        ssm_y = sem("ssm_y")
        gate_mm = sem("gate_mm")
        branch_mm = sem("branch_mm")
        gate_act = sem("gate_act")
        merged_put = sem("merged_put")
        out2_ready = sem("out2_ready")
        raw = scr[:, 4608:6720].rearrange("p (a c) -> p a c", a=4)
        fm = {n: hid[:, 3 * i:3 * i + 3, :] for i, n in enumerate("ABKR")}
        tm = {n: hid[:, 12 + 3 * i:15 + 3 * i, :].rearrange("p a b -> p (a b)").rearrange("p (t c) -> p t c", t=NT)
              for i, n in enumerate("ABKV")}
        sig, icl = hid[:, 12:15, :], hid[:, 15:18, :]
        vfm = d2[:, 3:6, :]
        ussm = d2[:, 6:8, :]
        glora, bonus = d2[:, 8:11, :], d2[:, 11:14, :]
        dq, dk = d2[:, 14:17, :], d2[:, 17:20, :]
        dv = [d2[:, 20, :], d2[:, 21, :], wdr[:, 0, :]]
        dpt = wdr[:, 1, :].rearrange("p (b c) -> p b c", b=2)
        c2 = cst[:, C_COS:C_COS + 2048]
        mk16l, mke1, mke2, mk16u, mkus, mkui = (c2[:, i * P:(i + 1) * P] for i in range(6))
        heads2 = c2[:, 6 * P:7 * P]
        ident64 = c2[:, 7 * P:7 * P + 64]
        restart = c2[:, 960:960 + S]
        g2s = sb("g2s", [P, G2_W])
        dvec = sb("dvec", [P, 3, 8])
        dstat = sb("dstat", [P, 3, 24])
        core = [d2[:, 14:22, :].rearrange("p a b -> p (a b)")[:, 0:3328], scr[:, 0:3328], scr[:, 3328:6656]]
        zst = d2[:, 14:22, :].rearrange("p a b -> p (a b)")[:, 3328:4096].rearrange("p (q s c) -> p q s c", q=3, s=4)
        R = {n: i for i, n in enumerate(
            ("N", "E1", "E2", "Nt", "Mak", "Mrb", "Mrk", "N2", "N2t", "Ya", "Yb", "N4", "N4t"))}

        def cm(p, name, w=256):
            return core[p][:, R[name] * 256:R[name] * 256 + w]

        merged = hid[:, 0:KD, :]
        tabs = hid[:, 8:12, :].rearrange("p (b i) c -> p b i c", b=2)
        cmat = d2[:, 14:18, :].rearrange("p a b -> p (a b)").rearrange("p (i s c) -> p i s c", i=2, s=8)
        xst = d2[:, 18:22, :].rearrange("p (b i) c -> p b i c", b=2)
        spar = sb("spar", [P, 13, 8])
        sw = sb("sw", [P, 4, 8, 16])
        fine = sb("fine", [P, 2, 8, 33])
        coarse = sb("coarse", [P, 2, 8, 17])
        cst2_eps = cst[:, C_EPS + 1:C_EPS + 2]
        s_tab = sem("s_tab")
        s_cz = sem("s_cz")
        wgu, wd1, wd2, wmix, wsmall = t_in["wgu"], t_in["wd1"], t_in["wd2"], t_in["wmix"], t_in["wsmall"]

        block = ctx.enter_context(nc.Block())

        def mm(o, w, r, start, stop):
            return nc.tensor.matmul(o, w, r, start=start, stop=stop, skip_group_check=True)

        @block.sync
        def _(sp):
            sp.dma_start(x[:, :, :], t_in["x"]).then_inc(x_in, 16)

            def gu_item(f, j, s, n):
                sp.wait_ge(ring_free, n + 1)
                sp.dma_start(ring[:, s, 0:2 * KD * P], wgu[f, j]).then_inc(ring_in[s], 16)

            def wd_item(f, j, s, n):
                sp.wait_ge(wdr_free, n + 1)
                sp.dma_start(wdr[:, s, :], wd1[f, j]).then_inc(wdr_in[s], 16)

            def swiglu(f, n0):
                with sp.Fori(0, NJ // 2) as jj:
                    for s in range(2):
                        gu_item(f, 2 * jj + s, s, n0 + 2 * jj + s)
                        wd_item(f, 2 * jj + s, s, f * NJ + 2 * jj + s)

            def mixer(l, n0):
                for i in range(MIX_ITEMS):
                    sp.wait_ge(ring_free, n0 + i + 1)
                    sp.dma_start(ring[:, i % 2, :], wmix[l, i]).then_inc(ring_in[i % 2], 16)

            with sp.Fori(0, LAYERS) as l:
                swiglu(2 * l, l * LAYER_ITEMS)
                mixer(l, l * LAYER_ITEMS + NJ)
                swiglu(2 * l + 1, l * LAYER_ITEMS + NJ + MIX_ITEMS)
            base = LAYERS * LAYER_ITEMS
            last = ["xg", "v0", "v1", "v2", "aq2", "ak2", "av2", "su1"]
            for i in range(8):
                if i < 2:
                    sp.wait_ge(ring_free, base + i + 1)
                else:
                    sp.wait_ge(made, NUM[last[i - 2]] + 1)
                sp.dma_start(ring[:, i % 2, :], t_in["wmix2"][i]).then_inc(ring_in[i % 2], 16)
            for i in range(12):
                if i < 2:
                    sp.wait_ge(made, NUM[last[6 + i]] + 1)
                else:
                    sp.wait_ge(branch_mm, 2 * (i - 2) + 2)
                sp.dma_start(ring[:, i % 2, :], t_in["wmix2"][8 + i]).then_inc(ring_in[i % 2], 16)
            for i in range(4):
                if i < 2:
                    sp.wait_ge(branch_mm, 2 * (10 + i) + 2)
                else:
                    sp.wait_ge(out2_ready, 2 * (i - 2) + 2)
                sp.dma_start(ring[:, i % 2, :], t_in["wmix2"][20 + i]).then_inc(ring_in[i % 2], 16)
            sp.wait_ge(out2_ready, KD)
            swiglu(2 * LAYERS, base)
            sp.wait_ge(x_upd, 88)
            sp.dma_start(out, x[:, :, :]).then_inc(out_done, 16)
            sp.wait_ge(out_done, 16)

        @block.tensor
        def _(pe):
            pe.sem_inc(ring_free, 2)
            pe.sem_inc(wdr_free, 2)
            pe.wait_ge(cst_in, 16)
            pe.wait_ge(cstb_in, 16)

            def norm(n):
                for k in range(KD):
                    pe.wait_ge(sq_ready, 8 * n + k + 1)
                    last = mm(psum[:, 4, :], ones, h[:, k, :], k == 0, k == KD - 1)
                last.then_inc(sumsq_ready, 1)

            def gate_up(j, s, n0, first=None):
                pe.wait_ge(ring_in[s], n0 * 8 + 8 * (j - s) + 16)
                for g in range(2):
                    for k in range(KD):
                        if first is not None and g == 0:
                            pe.wait_ge(h_ready, first + k + 1)
                        c = (g * KD + k) * P
                        last = mm(psum[:, 2 * g + s, :], ring[:, s, c:c + P], h[:, k, :], k == 0, k == KD - 1)
                    last.then_inc(ring_free if g else gate_ready, 1)

            def down1(j, s, f, start, stop):
                pe.wait_ge(wdr_in[s], (f * NJ + j - s) * 8 + 16)
                pe.wait_ge(hid_ready, f * NJ + j + 1)
                for m in range(4):
                    last = mm(psum[:, 4 + m, :], wdr[:, s, m * P:(m + 1) * P], hid[:, j, :], start, stop)
                    if m == 3:
                        last.then_inc(wdr_free, 1)
                    elif stop:
                        last.then_inc(down_ready, 1)

            def swiglu(f, n0, h0):
                gate_up(0, 0, n0, first=h0)
                gate_up(1, 1, n0)
                down1(0, 0, f, True, False)
                with pe.Fori(1, NJ // 2) as jj:
                    for s in range(2):
                        j = 2 * jj + s
                        pe.wait_ge(hid_ready, f * NJ + j - 1)
                        gate_up(j, s, n0)
                        down1(j - 1, 1 - s, f, False, False)
                down1(NJ - 1, 1, f, False, True)
                pe.wait_ge(d2_in, 32 * f + 32)
                for k in range(NJ):
                    for m in range(4):
                        last = mm(psum[:, m, :], d2[:, k, m * P:(m + 1) * P], hid[:, k, :], k == 0, k == NJ - 1)
                        if k == NJ - 1:
                            last.then_inc(down_ready, 1)

            def mixer(l, n0):
                def item(i, cols):
                    pe.wait_ge(ring_in[i % 2], n0 * 8 + 8 * (i - i % 2) + 16)
                    return ring[:, i % 2, 0:KD * cols].rearrange("p (k c) -> p k c", k=KD)

                def project(bank, w, c0, m, done):
                    for k in range(KD):
                        last = mm(psum[0:m, bank, :], w[:, k, c0:c0 + m], h[:, k, :], k == 0, k == KD - 1)
                    last.then_inc(done, 1)

                for k in range(KD):
                    pe.wait_ge(h_ready, 24 * l + 8 + k + 1)
                w = item(0, 198)
                project(1, w, 0, 128, p_kv)
                project(2, w, 128, 70, ring_free)
                w = item(1, 256)
                project(3, w, 0, 128, p_qa)
                project(4, w, 128, 128, ring_free)
                w = item(2, 256)
                project(7, w, 0, 128, p_pool)
                project(0, w, 128, 128, ring_free)
                pe.wait_ge(lat_sq, 3 * l + 1)
                mm(psum[:, 5, :], ones, tmp[:, 0, :], True, True).then_inc(lat_ss, 1)
                pe.wait_ge(lat_sq, 3 * l + 3)
                mm(psum[:, 6, :], ones, tmp[:, 1, :], True, False)
                mm(psum[:, 6, :], ones, tmp[:, 2, :], False, True).then_inc(lat_ss, 1)
                for p in range(3):
                    w = item(3 + p, 256)
                    if p != 1:
                        pe.wait_ge(pool_in, 2 * l + 2)
                    else:
                        pe.wait_ge(lat_rms, 2 * l + 2)
                    if p == 2:
                        pe.wait_ge(foxq_put, 6 * l + 2)
                        pe.wait_ge(foxk_put, 6 * l + 2)
                    project((7, 5, 7)[p], w, 0, 128, p_foxqk)
                    project((0, 6, 0)[p], w, 128, 128, ring_free)
                w = item(6, 384)
                pe.wait_ge(lat_n, 3 * l + 3)
                pe.wait_ge(cum_ready, l + 1)
                for t in range(NT):
                    for k in range(KD):
                        last = mm(psum[:, 1 + t, 0:384], h[:, k, t * P:(t + 1) * P], w[:, k, :], k == 0, k == KD - 1)
                    last.then_inc(p_foxv if t < NT - 1 else ring_free, 1)
                pe.wait_ge(mixw_in, 16 * l + 16)
                wq = mixw[:, M_QB:M_QB + 1536].rearrange("p (k c) -> p k c", k=2)
                pe.wait_ge(foxq_put, 6 * l + 4)
                pe.wait_ge(foxk_put, 6 * l + 4)
                for g in range(2):
                    for k in range(2):
                        last = mm(psum[0:96, 5 + g, :], wq[:, k, 576 + 96 * g:672 + 96 * g], tmp[:, 3 + k, :], k == 0, k == 1)
                    last.then_inc(p_sw, 1)
                for a in range(HEADS):
                    if a == 0:
                        pe.wait_ge(foxq_put, 6 * l + 6)
                        pe.wait_ge(foxk_put, 6 * l + 6)
                    if a >= 2:
                        pe.wait_ge(mlaqn_put, 6 * l + a - 1)
                        pe.wait_ge(mlaqr_put, 6 * l + a - 1)
                    for k in range(2):
                        last = mm(psum[0:96, (7, 0)[a % 2], :], wq[:, k, 96 * a:96 * a + 96], tmp[:, 3 + k, :], k == 0, k == 1)
                    last.then_inc(p_mlaq, 1)
                wkv = mixw[:, M_KV:M_KV + 768]
                pe.wait_ge(foxv_put, 4 * l + 4)
                for p in range(3):
                    mm(psum[:, 1 + p, :], wkv[:, p * P:(p + 1) * P], tmp[:, 5, :], True, True).then_inc(p_mlak, 1)
                for t in range(NT):
                    if t:
                        pe.wait_ge(mlak_put, 6 * l + 2 * t)
                    mm(psum[:, (4, 1, 2, 3)[t], 0:384], tmp[:, 5, t * P:(t + 1) * P], wkv[:, 384:768], True, True)\
                        .then_inc(p_mlav, 1)
                pe.wait_ge(mlaqn_put, 6 * l + 6)
                pe.wait_ge(mlaqr_put, 6 * l + 6)
                pe.wait_ge(mlak_put, 6 * l + 6)
                pe.wait_ge(mlav_put, 4 * l + 4)
                pe.wait_ge(kpe_put, l + 1)
                pe.wait_ge(aug_in, 64 * l + 64)

                def score(u):
                    a, i = divmod(u, NT)
                    rows, n = (96 if a < HEADS else 66), (i + 1) * P
                    if u >= 3:
                        pe.wait_ge(expd, UNITS * l + u - 2)
                    mm(psum[:, u % 3, 0:n], hid[0:rows, a, i * P:(i + 1) * P], hid[0:rows, 12 + a, 0:n], True, False)
                    mm(psum[:, u % 3, n - P:n], cstb[:, 0, :], cstb[:, 1, :], False, True).then_inc(scores, 1)

                def turn(u):
                    i = u % NT
                    pe.wait_ge(normd, UNITS * l + u + 1)
                    if u >= 2:
                        pe.wait_ge(pt_put, UNITS * l + u - 1)
                    for t in range(i + 1):
                        last = nc.tensor.transpose(psum[:, 3 + u % 2, t * P:(t + 1) * P],
                                                   probs[:, u % 3, t * P:(t + 1) * P], ident)
                    last.then_inc(turned, 1)

                def attend(a):
                    pair = a // 2
                    pe.wait_ge(pt_put, UNITS * l + 4 * a + 4)
                    if pair >= 2:
                        pe.wait_ge(y_put, 6 * l + pair - 1)
                    c = HD * (a % HEADS)
                    for t in range(NT):
                        last = mm(psum[HD * (a % 2):HD * (a % 2) + HD, 5 + pair % 2, t * P:S],
                                  vt[a // HEADS][:, t, c:c + HD], pt[a % 2][:, t, t * P:S], t == 0, t == NT - 1)
                    last.then_inc(yh_ready, 1)

                for u in range(UNITS + 4):
                    if u < UNITS:
                        score(u)
                    if 2 <= u < UNITS + 2:
                        turn(u - 2)
                    if u >= 4 and (u - 4) % NT == NT - 1:
                        attend((u - 4) // NT)
                pe.wait_ge(pooled, 2 * l + 2)
                pe.sem_inc(carrier, 1)
                for t in range(2):
                    for g in range(2):
                        r = slice(HD * g, HD * g + HD)
                        last = mm(psum[r, 7, :] if t else psum[r, 0, :], mixw[r, M_PW + HD * t:M_PW + HD * t + HD],
                                  tmp[r, 4 * t, :], True, True)
                    last.then_inc(p_pooly, 1)
                for m in range(KD):
                    i = 7 + m // 3
                    if m % 3 == 0:
                        pe.wait_ge(ring_in[i % 2], n0 * 8 + 8 * (i - i % 2) + 16)
                    if m == 0:
                        pe.wait_ge(y_put, 6 * l + 6)
                        pe.wait_ge(pool_out, 2 * l + 2)
                    w = ring[:, i % 2, (m % 3) * D:(m % 3 + 1) * D].rearrange("p (k c) -> p k c", k=KD)
                    for k in range(KD):
                        last = mm(psum[:, (m + 4) % 8, :], w[:, k, :], y[:, k, :], k == 0, k == KD - 1)
                    last.then_inc(ring_free if m in (2, 5, 7) else wout_ready, 1)

            with pe.Fori(0, LAYERS) as l:
                norm(3 * l)
                swiglu(2 * l, l * LAYER_ITEMS, 24 * l)
                norm(3 * l + 1)
                mixer(l, l * LAYER_ITEMS + NJ)
                norm(3 * l + 2)
                swiglu(2 * l + 1, l * LAYER_ITEMS + NJ + MIX_ITEMS, 24 * l + 16)
            norm(3 * LAYERS)
            base = LAYERS * LAYER_ITEMS
            norm(3 * LAYERS + 1)
            pe.wait_ge(mixw2_in, 32)
            hn = 24 * LAYERS
            for k in range(KD):
                pe.wait_ge(h_ready, hn + k + 1)

            def ring_item(i, cols):
                pe.wait_ge(ring_in[i % 2], (base // 2 + i // 2 + 1) * 16)
                return ring[:, i % 2, 0:KD * cols].rearrange("p (k c) -> p k c", k=KD)

            def product(name):
                n = NUM[name]
                if n >= 8:
                    pe.wait_ge(read, n - 7)
                return psum[:, n % 8, :]

            def project(name, w, c0):
                o = product(name)
                for k in range(KD):
                    last = mm(o, w[:, k, c0:c0 + P], h[:, k, :], k == 0, k == KD - 1)
                last.then_inc(made, 1)

            def head_sum(name, src, ready, value):
                pe.wait_ge(ready, value)
                mm(product(name), heads2, src, True, True).then_inc(made, 1)

            def rkv(p):
                w = ring_item(1 + p, 384)
                for i, n in enumerate("rkv"):
                    project(f"{n}{p}", w, i * P)

            w = ring_item(0, 256)
            project("xwa", w, 0)
            project("xg", w, P)
            rkv(0)
            lo, hi = slice(0, 64), slice(64, 128)
            for n, r, src, need in (("lw", lo, 2, 1), ("la", hi, 2, 2), ("lg", slice(0, P), 3, 3)):
                pe.wait_ge(lora_act, need)
                c = W2_G if n == "lg" else W2_WA
                for p in range(3):
                    mm(product(f"{n}{p}"), mixw[r, c + p * P:c + (p + 1) * P], tmp[r, src, :], True, True).then_inc(made, 1)
            rkv(1)
            head_sum("kn0", tmp[:, 1, :], kk_sq, 1)
            head_sum("bn0", tmp[:, 2, :], bonus_in, 1)
            rkv(2)
            head_sum("kn1", tmp[:, 1, :], kk_sq, 2)
            head_sum("bn1", tmp[:, 2, :], bonus_in, 2)
            w = ring_item(4, 384)
            for g in range(3):
                project(f"aq{g}", w, g * P)
            head_sum("kn2", tmp[:, 1, :], kk_sq, 3)
            head_sum("bn2", tmp[:, 2, :], bonus_in, 3)
            w = ring_item(5, 384)
            for g in range(3):
                project(f"ak{g}", w, g * P)
            w = ring_item(6, 384)
            for g in range(2):
                o = product(f"av{g}")
                for t in range(NT):
                    for k in range(KD):
                        if g == 0:
                            tok = h[:, k, t * P:(t + 1) * P]
                        else:
                            tok = h[:, k, :].rearrange("p (a r) -> p r a", r=4)[:, t, :]
                        last = mm(o[:, t * P:(t + 1) * P], tok, w[:, k, g * P:(g + 1) * P], k == 0, k == KD - 1)
                last.then_inc(made, 1)
            project("av2", w, 2 * P)
            w = ring_item(7, 256)
            project("su0", w, 0)
            project("su1", w, P)
            o = product("av2t")
            pe.wait_ge(read, NUM["av2"] + 1)
            for t in range(NT):
                last = nc.tensor.transpose(o[:, t * P:(t + 1) * P], hid[:, 18, t * P:(t + 1) * P], ident)
            last.then_inc(made, 1)
            pe.wait_ge(rwkv_fm, 3)
            for n in "ABKV":
                for t in range(NT):
                    o = product(f"t{n}{t}")
                    for p in range(3):
                        src = vfm[:, p, t * P:(t + 1) * P] if n == "V" else fm[n][:, p, t * P:(t + 1) * P]
                        last = nc.tensor.transpose(o[:, p * P:(p + 1) * P], src, ident)
                    last.then_inc(made, 1)
            pe.wait_ge(read, len(PRODUCTS))

            def d_keys(u):
                g, i = u // 8, u % NT
                return 2 if g == 0 and i else 1

            def d_score(u):
                hd, i = divmod(u, NT)
                g, r = hd // 2, slice(HD * (hd % 2), HD * (hd % 2) + HD)
                n = d_keys(u)
                if u >= 3:
                    pe.wait_ge(d_exp, u - 2)
                o = psum[:, u % 3, 0:n * P]
                mm(o, dq[r, g, i * P:(i + 1) * P], dk[r, g, (i + 1 - n) * P:(i + 1) * P], True, False)
                if n == 2:
                    mm(o[:, 0:P], cstb[:, 0, :], cstb[:, 2, :], False, False)
                mm(o[:, (n - 1) * P:n * P], cstb[:, 0, :], cstb[:, 3 if g == 2 else 1, :], False, True).then_inc(d_scores, 1)

            def d_turn(u):
                pe.wait_ge(d_norm, u + 1)
                if u >= 2:
                    pe.wait_ge(d_put, u - 1)
                for t in range(d_keys(u)):
                    last = nc.tensor.transpose(psum[:, 3 + u % 2, t * P:(t + 1) * P], probs[:, u % 3, t * P:(t + 1) * P], ident)
                last.then_inc(d_turned, 1)

            def d_attend(u):
                hd, i = divmod(u, NT)
                g, e, n = hd // 2, hd % 2, d_keys(u)
                pe.wait_ge(d_put, u + 1)
                for t in range(n):
                    kt = i + 1 - n + t
                    last = mm(psum[HD * e:HD * e + HD, 5 + g, i * P:(i + 1) * P],
                              dv[g][:, kt * P + HD * e:kt * P + HD * e + HD], dpt[:, u % 2, t * P:(t + 1) * P],
                              t == 0, t == n - 1)
                last.then_inc(d_out, 1)

            for u in range(UNITS2 + 3):
                if u < UNITS2:
                    d_score(u)
                if 2 <= u < UNITS2 + 2:
                    d_turn(u - 2)
                if u >= 3:
                    d_attend(u - 3)
            pe.wait_ge(d_lse, 1)
            for g in range(3):
                for e in range(2):
                    for i in range(NT):
                        u = 8 * g + 4 * e + i
                        last = mm(psum[HD * e:HD * e + HD, g, i * P:(i + 1) * P],
                                  dstat[:, 2, u:u + 1].to_broadcast([P, HD]), ident, True, True)
                last.then_inc(d_lseb, 1)
            pe.wait_ge(attn_y, 3)
            pe.wait_ge(z_zero, 1)

            def vec(name, t, p):
                pe.wait_ge(rw_vec, done(VEC_STEPS, name, t, p))

            def act_(name, t, p):
                pe.wait_ge(rw_act, done(ACT_STEPS, name, t, p))

            def rw_step(name, t, p):
                A, B = psum[:, 2 * p, :], psum[:, 2 * p + 1, :]
                tok = slice(t * P, (t + 1) * P)
                last = None

                def rows(e):
                    return slice(HD * e, HD * e + HD)

                def sq(o, c, l_, r_):
                    for e in range(2):
                        res = mm(o[:, c + e * P:c + e * P + P], l_[:, e * P:(e + 1) * P], r_[:, e * P:(e + 1) * P], True, True)
                    return res

                def head(o, c, l_, r_):
                    return mm(o[:, c + half * P:c + half * P + P], fm[l_][rows(half), p, tok], fm[r_][rows(half), p, tok],
                              True, True)

                half = 0
                if name[-1] == "b":
                    half = 1
                    pe.wait_ge(rw_mm, done(MM_STEPS, name[:-1] + "a", t, p))

                if name in ("M12a", "M12b"):
                    if t:
                        act_("Y", t - 1, p)
                    head(A, 0, "A", "B")
                    last = head(A, 256, "B", "A")
                elif name in ("M34a", "M34b"):
                    if t:
                        vec("U", t - 1, p)
                    head(B, 0, "K", "A")
                    last = head(B, 256, "B", "R")
                elif name == "NN2":
                    vec("N", t, p)
                    sq(A, 0, cm(p, "Nt"), cm(p, "N"))
                    last = sq(A, 256, cm(p, "N"), cm(p, "Nt"))
                elif name in ("M5a", "M5b"):
                    vec("M34", t, p)
                    last = head(B, 0, "K", "R")
                elif name == "Y2":
                    act_("N2", t, p)
                    vec("M5", t, p)
                    last = sq(B, 0, cm(p, "N2"), cm(p, "Ya"))
                elif name == "NN4":
                    sq(A, 0, cm(p, "N2t"), cm(p, "N2"))
                    last = sq(A, 256, cm(p, "N2"), cm(p, "N2t"))
                elif name == "Y4":
                    act_("N4", t, p)
                    vec("Y2", t, p)
                    last = sq(B, 0, cm(p, "N4"), cm(p, "Yb"))
                elif name == "N8":
                    last = sq(A, 0, cm(p, "N4t"), cm(p, "N4"))
                elif name == "X1":
                    act_("N8", t, p)
                    for e in range(2):
                        last = mm(A[:, e * HD:e * HD + HD], cm(p, "Mak")[:, e * P:(e + 1) * P],
                                  tm["V"][:, t, (2 * p + e) * HD:(2 * p + e + 1) * HD], True, True)
                elif name == "Y8":
                    vec("Y4", t, p)
                    last = sq(B, 0, cm(p, "N2"), cm(p, "Ya"))
                elif name in ("TF1", "TF2"):
                    y_ = cm(p, "Yb" if name == "TF1" else "Ya")
                    vec("Y8" if name == "TF1" else "Y32", t, p)
                    act_("X1" if name == "TF1" else "TF1", t, p)
                    for e in range(2):
                        nc.tensor.transpose(A[:, e * P:(e + 1) * P], y_[:, e * P:(e + 1) * P], ident)
                    last = sq(A, 256, cm(p, "E1" if name == "TF1" else "E2"), y_)
                elif name in ("Y32", "XT"):
                    act_("TF1" if name == "Y32" else "TF2", t, p)
                    last = sq(B, 0, cm(p, "N2"), cm(p, "N2t"))
                elif name == "GW":
                    vec("XT", t, p)
                    for e in range(2):
                        xt = cm(p, "Yb")[:, e * P:(e + 1) * P]
                        a_ = tm["A"][:, t, (2 * p + e) * HD:(2 * p + e + 1) * HD]
                        mm(B[:, e * HD:e * HD + HD], xt, a_, True, True)
                        mm(B[:, P + e * HD:P + e * HD + HD], xt, cm(p, "Nt")[:, e * HD:e * HD + HD], True, True)
                        last = mm(B[rows(e), 256:384], a_, xt, True, True)
                elif name in ("PTa", "PTb"):
                    act_("GW", t, p)
                    c = half
                    for e in range(2):
                        last = mm(A[rows(e), c * HD:c * HD + HD], cm(p, "N")[rows(c), e * HD:e * HD + HD],
                                  tm["B"][rows(c), t, (2 * p + e) * HD:(2 * p + e + 1) * HD], True, True)
                elif name in ("S0a", "S1a"):
                    c = int(name[1])
                    if c == 0:
                        vec("PT", t, p)
                    else:
                        vec("Z0", t, p)
                    for e in range(2):
                        hc = slice((2 * p + e) * HD, (2 * p + e + 1) * HD)
                        o = A[rows(e), 0:HD]
                        mm(o, tm["B"][rows(c), t, hc], cm(p, "N")[rows(c), P + e * HD:P + e * HD + HD], True, False)
                        last = mm(o, tm["K"][rows(c), t, hc], tm["V"][rows(c), t, hc], False, False)
                elif name in ("S0b", "S1b"):
                    c = int(name[1])
                    if t and c == 0:
                        vec("Z1", t - 1, p)
                    for e in range(2):
                        last = mm(A[rows(e), 0:HD], cm(p, "E2")[rows(e), c * HD:c * HD + HD],
                                  zst[rows(e), p, (2 * t + c) % 4, :], False, True)
                elif name in ("Ua", "Ub"):
                    act_("GT", t, p)
                    e = half
                    for c in range(2):
                        last = mm(B[rows(c), e * HD:e * HD + HD], cm(p, "E1")[rows(e), c * HD:c * HD + HD],
                                  zst[rows(e), p, (2 * t + c) % 4, :], True, True)
                else:
                    vec("Z1", t, p)
                    vec("U", t, p)
                    for e in range(2):
                        hc = slice((2 * p + e) * HD, (2 * p + e + 1) * HD)
                        o = A[rows(e), 0:P]
                        ec = slice(e * P, (e + 1) * P)
                        mm(o, tm["V"][:, t, hc], cm(p, "Mrk")[:, ec], True, False)
                        for c in range(2):
                            mm(o[:, c * HD:c * HD + HD], zst[rows(e), p, (2 * t + c) % 4, :],
                               fm["R"][rows(e), p, t * P + c * HD:t * P + c * HD + HD], False, False)
                        last = mm(o, cm(p, "N4")[:, e * HD:e * HD + HD], cm(p, "Mrb")[:, ec], False, True)
                last.then_inc(rw_mm, 1)

            for t in range(NT):
                for name in MM_STEPS:
                    for p in range(3):
                        rw_step(name, t, p)

            for p in range(3):
                pe.wait_ge(rw_act, done(ACT_STEPS, "Y", NT - 1, p))
            for p in range(3):
                mm(psum[:, p, :], heads2, y[:, 3 + p, :], True, True).then_inc(gn_mm, 1)
            for p in range(3):
                pe.wait_ge(gn_act, p + 1)
                mm(psum[:, p, :], heads2, tmp[:, 3 + p, :], True, True).then_inc(gn_mm, 1)

            def merge(branch, m):
                q = branch * KD + m
                item, half = 8 + q // 2, q % 2
                if half == 0:
                    pe.wait_ge(ring_in[item % 2], (base // 2 + item // 2 + 1) * 16)
                w = ring[:, item % 2, half * 1408:half * 1408 + 1408].rearrange("p (k c) -> p k c", k=11)
                if q >= 2:
                    pe.wait_ge(merged_put, q - 1)
                    pe.wait_ge(gate_act, q - 1)
                for k in range(KD):
                    last = mm(psum[:, 6 + q % 2, :], w[:, k, :], h[:, k, :], k == 0, k == KD - 1)
                last.then_inc(gate_mm, 1)
                k0, n = ((0, 3), (3, 3), (6, 2))[branch]
                if m == 0 and branch == 1:
                    pe.wait_ge(rwkv_y, 3)
                if m == 0 and branch == 2:
                    pe.wait_ge(ssm_y, 2)
                for k in range(n):
                    last = mm(psum[:, 4 + q % 2, :], w[:, KD + k, :], y[:, k0 + k, :], k == 0, k == n - 1)
                last.then_inc(branch_mm, 1)

            def drive(s):
                r = slice(32 * (s % 4), 32 * (s % 4) + 32)
                if s:
                    pe.wait_ge(s_rot, s)
                for im in range(2):
                    c = W2_B + ((s // 4) * 2 + im) * P
                    last = mm(psum[:, im, :], mixw[r, c:c + P], ussm[r, s // 4, :], True, True)
                last.then_inc(s_bu, 1)

            def readout(s):
                if s == 0:
                    pe.wait_ge(s_cw, 2)
                pe.wait_ge(s_back, s + 1)
                for im in range(2):
                    last = mm(psum[:, 2 + s // 4, :], cmat[:, im, s, :], xst[:, s % 2, im, :],
                              s % 4 == 0 and im == 0, s % 4 == 3 and im == 1)
                last.then_inc(s_ym if s % 4 == 3 else s_c, 1)

            merge(0, 0)
            pe.wait_ge(gn_act, 6)
            drive(0)
            for s in range(8):
                if s:
                    merge(2 * s // KD, 2 * s % KD)
                    readout(s - 1)
                if s < 7:
                    pass
                merge((2 * s + 1) // KD, (2 * s + 1) % KD)
                if s < 7:
                    drive(s + 1)
            readout(7)
            pe.wait_ge(s_gl, 6)
            for n in range(2):
                for m in range(2):
                    for k in range(2):
                        c = (W2_GV, W2_GG)[n] + k * 256 + m * P
                        last = mm(psum[:, 2 * n + m, :], mixw[:, c:c + P], hid[:, 22 + k, :], k == 0, k == 1)
                    last.then_inc(glu_mm, 1)
            for m in range(KD):
                merge(2, m)
            for m in range(KD):
                item = 20 + m // 2
                if m % 2 == 0:
                    pe.wait_ge(ring_in[item % 2], (base // 2 + item // 2 + 1) * 16)
                if m == 0:
                    pe.wait_ge(merged_put, 3 * KD)
                w = ring[:, item % 2, (m % 2) * D:(m % 2 + 1) * D].rearrange("p (k c) -> p k c", k=KD)
                for k in range(KD):
                    last = mm(psum[:, (m + 4) % 8, :], w[:, k, :], merged[:, k, :], k == 0, k == KD - 1)
                last.then_inc(out2_ready, 1)
            norm(3 * LAYERS + 2)
            swiglu(2 * LAYERS, base + B2_ITEMS, 24 * LAYERS + 8)
            norm(3 * LAYERS + 3)

        @block.scalar
        def _(act):
            act.dma_start(cst[:, :], t_in["cst"]).then_inc(cst_in, 16)
            act.dma_start(gains[:, :, :], t_in["gains"]).then_inc(gains_in, 16)
            act.dma_start(g2s[:, :], t_in["g2s"]).then_inc(gains_in, 16)
            act.wait_ge(cst_in, 16)
            act.wait_ge(gains_in, 32)
            act.wait_ge(x_in, 16)

            def norm(n):
                for k in range(KD):
                    act.wait_ge(x_upd, 8 * n + k + 1)
                    nc.scalar.activation(h[:, k, :], x[:, k, :], ACT.Square).then_inc(sq_ready, 1)
                act.wait_ge(sumsq_ready, n + 1)
                nc.scalar.activation(tmp[:, 0, :], psum[:, 4, :], ACT.Sqrt, bias=eps, scale=1.0 / D).then_inc(rms_ready, 1)

            def swiglu(f):
                for b in range(2):
                    act.dma_start(d2[:, 11 * b:11 * b + 11, :], wd2[f, b]).then_inc(d2_in, 16)
                with act.Fori(0, NJ // 2) as jj:
                    for s in range(2):
                        act.wait_ge(gate_ready, f * NJ + 2 * jj + s + 1)
                        nc.scalar.activation(probs[:, s, :], psum[:, s, :], ACT.Silu).then_inc(silu_ready, 1)

            def mixer(l):
                n0 = l * LAYER_ITEMS + NJ
                act.dma_start(mixw[:, :], wsmall[l]).then_inc(mixw_in, 16)
                act.wait_ge(p_kv, l + 1)
                nc.scalar.activation(tmp[:, 0, :], psum[:, 1, :], ACT.Square).then_inc(lat_sq, 1)
                act.wait_ge(p_qa, l + 1)
                nc.scalar.activation(tmp[:, 1, :], psum[:, 3, :], ACT.Square).then_inc(lat_sq, 1)
                act.wait_ge(ring_free, used(n0 + 1))
                nc.scalar.activation(tmp[:, 2, :], psum[:, 4, :], ACT.Square).then_inc(lat_sq, 1)
                act.wait_ge(pads_zero, 2)
                for t in range(2):
                    if t:
                        act.wait_ge(ring_free, used(n0 + 2))
                    else:
                        act.wait_ge(p_pool, l + 1)
                    nc.scalar.activation(upad[:, t, 16:], psum[:, (7, 0)[t], :], ACT.Copy).then_inc(pool_in, 1)
                act.wait_ge(lat_ss, 2 * l + 1)
                nc.scalar.activation(tmp[:, 0, :], psum[:, 5, :], ACT.Sqrt, bias=eps, scale=1.0 / KVR).then_inc(lat_rms, 1)
                act.wait_ge(lat_ss, 2 * l + 2)
                nc.scalar.activation(tmp[:, 1, :], psum[:, 6, :], ACT.Sqrt, bias=eps, scale=1.0 / QR).then_inc(lat_rms, 1)
                g = slice(64, 70)
                act.wait_ge(fz_ready, l + 1)
                nc.scalar.activation(wdr[g, 0, :], probs[g, 1, :], ACT.Exp, scale=-1.0).then_inc(astep, 1)
                act.wait_ge(astep, l + 1)
                nc.scalar.activation(wdr[g, 1, :], wdr[g, 0, :], ACT.Ln, bias=1.0).then_inc(fe_ready, 1)
                for p in range(3):
                    act.wait_ge(p_foxqk, 3 * l + p + 1)
                    for e in range(2):
                        nc.scalar.activation(hid[0:HD, 6 + 2 * p + e, :], psum[HD * e:HD * e + HD, (7, 5, 7)[p], :],
                                             ACT.Copy, scale=FOX_SCALE).then_inc(foxq_put, 1)
                for t in range(NT):
                    if t < NT - 1:
                        act.wait_ge(p_foxv, 3 * l + t + 1)
                    else:
                        act.wait_ge(ring_free, used(n0 + 6))
                    nc.scalar.activation(vt[1][:, t, :], psum[:, 1 + t, 0:384], ACT.Copy).then_inc(foxv_put, 1)
                for a in range(HEADS):
                    act.wait_ge(p_mlaq, 6 * l + a + 1)
                    nc.scalar.activation(hid[0:NOPE, a, :], psum[0:NOPE, (7, 0)[a % 2], :], ACT.Copy,
                                         scale=MLA_SCALE).then_inc(mlaqn_put, 1)
                for t in range(NT):
                    act.wait_ge(p_mlav, 4 * l + t + 1)
                    nc.scalar.activation(vt[0][:, t, :], psum[:, (4, 1, 2, 3)[t], 0:384], ACT.Copy).then_inc(mlav_put, 1)

                def put_turned(u):
                    a, i = divmod(u, NT)
                    act.wait_ge(turned, UNITS * l + u + 1)
                    if i == 0 and a >= 2:
                        act.wait_ge(yh_ready, 12 * l + a - 1)
                    nc.scalar.activation(pt[a % 2][:, 0:i + 1, i * P:(i + 1) * P],
                                         psum[:, 3 + u % 2, 0:(i + 1) * P].rearrange("p (t c) -> p t c", t=i + 1),
                                         ACT.Copy).then_inc(pt_put, 1)

                def put_y(pair):
                    act.wait_ge(yh_ready, 12 * l + 2 * pair + 2)
                    nc.scalar.activation(y[:, pair if pair < 3 else pair + 2, :], psum[:, 5 + pair % 2, :],
                                         ACT.Copy).then_inc(y_put, 1)

                for u in range(UNITS + 2):
                    if u < UNITS:
                        n = (u % NT + 1) * P
                        act.wait_ge(nmax, UNITS * l + u + 1)
                        if u >= 3:
                            act.wait_ge(turned, UNITS * l + u - 2)
                        nc.scalar.activation(probs[:, u % 3, 0:n], psum[:, u % 3, 0:n], ACT.Exp,
                                             bias=stat[:, u % 3, 0:1], accum_out=stat[:, u % 3, 1:2]).then_inc(expd, 1)
                    if u >= 2:
                        put_turned(u - 2)
                    if u >= 12 and (u - 12) % 8 == 0:
                        put_y((u - 12) // 8)
                put_y(5)
                for t in range(2):
                    act.wait_ge(p_pooly, 2 * l + t + 1)
                    nc.scalar.activation(y[:, 3 + t, :], psum[:, (0, 7)[t], :], ACT.Copy,
                                         scale=gains[:, l, G_PS + t:G_PS + t + 1]).then_inc(pool_out, 1)

            with act.Fori(0, LAYERS) as l:
                norm(3 * l)
                swiglu(2 * l)
                norm(3 * l + 1)
                mixer(l)
                norm(3 * l + 2)
                swiglu(2 * l + 1)
            norm(3 * LAYERS)
            norm(3 * LAYERS + 1)
            act.dma_start(mixw[:, :], t_in["wsmall2"]).then_inc(mixw2_in, 16)
            act.dma_start(c2, t_in["cst2"]).then_inc(mixw2_in, 16)

            def read_out(name, out_, in_, func=ACT.Copy, **kw):
                act.wait_ge(made, NUM[name] + 1)
                nc.scalar.activation(out_, in_, func, **kw).then_inc(read, 1)

            def bank(name):
                return psum[:, NUM[name] % 8, :]

            raws = ["xwa", "xg", "r0", "k0", "v0", "r1", "k1", "v1", "r2", "k2", "v2"]

            def raw_out(name):
                i = raws.index(name)
                if i >= 4:
                    act.wait_ge(mixed, i - 3)
                read_out(name, raw[:, i % 4, 16:], bank(name))

            def prep(p):
                act.wait_ge(decay_in, p + 1)
                nc.scalar.activation(dvec[:, p, 0:7], dvec[:, p, 0:7], ACT.Exp, scale=-KAPPA).then_inc(decay_exp, 1)
                nc.scalar.activation(probs[:, 2, :], probs[:, 2, :], ACT.Exp, scale=-KAPPA).then_inc(decay_exp, 1)
                nc.scalar.activation(probs[:, 0, :], probs[:, 1, :], ACT.Exp, scale=KAPPA).then_inc(decay_exp, 1)
                act.wait_ge(decay_exp, 4 * p + 3)
                nc.scalar.activation(probs[:, 1, :], probs[:, 1, :], ACT.Exp, scale=-KAPPA).then_inc(decay_exp, 1)
                act.wait_ge(kk_in, p + 1)
                nc.scalar.activation(tmp[:, 1, :], tmp[:, 0, :], ACT.Square).then_inc(kk_sq, 1)
                act.wait_ge(made, NUM[f"kn{p}"] + 1)
                nc.scalar.activation(tmp[:, 1, :], bank(f"kn{p}"), ACT.Sqrt).then_inc(read, 1)
                read_out(f"bn{p}", tmp[:, 3, :], bank(f"bn{p}"))

            raw_out("xwa")
            raw_out("xg")
            raw_out("r0")
            raw_out("k0")
            act.wait_ge(mixed, 2)
            nc.scalar.activation(tmp[0:64, 2, :], tmp[0:64, 0, :], ACT.Tanh).then_inc(lora_act, 1)
            nc.scalar.activation(tmp[64:128, 2, :], tmp[64:128, 0, :], ACT.Copy).then_inc(lora_act, 1)
            nc.scalar.activation(tmp[:, 3, :], tmp[:, 1, :], ACT.Sigmoid).then_inc(lora_act, 1)
            raw_out("v0")
            for p in range(3):
                read_out(f"lw{p}", sig[:, p, :], bank(f"lw{p}"), ACT.Sigmoid, bias=g2s[:, H_W0 + p:H_W0 + p + 1])
            for p in range(3):
                read_out(f"la{p}", icl[:, p, :], bank(f"la{p}"), ACT.Sigmoid, bias=g2s[:, H_A0 + p:H_A0 + p + 1])
            for p in range(3):
                read_out(f"lg{p}", glora[:, p, :], bank(f"lg{p}"))
            raw_out("r1")
            raw_out("k1")
            raw_out("v1")
            prep(0)
            raw_out("r2")
            raw_out("k2")
            raw_out("v2")
            prep(1)

            def ordered(t, g):
                return t if g == 0 else t.rearrange("p (a r) -> p r a", r=4 if g == 1 else 16)

            def as_group(t, g):
                return t if g == 0 else t.rearrange("p (r a) -> p r a", r=4 if g == 1 else 16)

            for g in range(3):
                read_out(f"aq{g}", as_group(dq[:, g, :], g), ordered(bank(f"aq{g}"), g), scale=HD ** -0.5)
            nc.scalar.activation(spar[:, 0, :], g2s[:, H_LS:H_LS + 8], ACT.Exp).then_inc(s_trig, 1)
            prep(2)
            for g in range(3):
                read_out(f"ak{g}", as_group(dk[:, g, :], g), ordered(bank(f"ak{g}"), g))
            for g in range(2):
                read_out(f"av{g}", dv[g], bank(f"av{g}"))
            read_out("av2", as_group(hid[:, 18, :], 2), ordered(bank("av2"), 2))
            for m in range(2):
                read_out(f"su{m}", ussm[:, m, :], bank(f"su{m}"))
            read_out("av2t", dv[2], bank("av2t"))
            act.wait_ge(s_par, 1)
            nc.scalar.activation(spar[:, 3, :], spar[:, 2, :], ACT.Sin).then_inc(s_trig, 1)
            nc.scalar.activation(spar[:, 5, :], spar[:, 4, :], ACT.Sin).then_inc(s_trig, 1)
            act.wait_ge(bonus_put, 3)
            for n in "ABKV":
                for t in range(NT):
                    read_out(f"t{n}{t}", tm[n][:, t, :], bank(f"t{n}{t}")[:, 0:384])

            def d_keys(u):
                return 2 if u // 8 == 0 and u % NT else 1

            for u in range(UNITS2 + 2):
                if u < UNITS2:
                    n = d_keys(u) * P
                    act.wait_ge(d_nmax, u + 1)
                    if u >= 3:
                        act.wait_ge(d_turned, u - 2)
                    nc.scalar.activation(probs[:, u % 3, 0:n], psum[:, u % 3, 0:n], ACT.Exp, bias=dstat[:, 0, u:u + 1],
                                         accum_out=dstat[:, 1, u:u + 1]).then_inc(d_exp, 1)
                if u >= 2:
                    v = u - 2
                    n = d_keys(v) * P
                    act.wait_ge(d_turned, v + 1)
                    if v >= 2:
                        act.wait_ge(d_out, v - 1)
                    nc.scalar.activation(dpt[:, v % 2, 0:n], psum[:, 3 + v % 2, 0:n], ACT.Copy).then_inc(d_put, 1)
            act.wait_ge(d_exp, UNITS2)
            nc.scalar.activation(dstat[:, 2, :], dstat[:, 1, :], ACT.Ln).then_inc(d_ln, 1)
            for g in range(3):
                act.wait_ge(d_diff, g + 1)
                nc.scalar.activation(tmp[:, 3 + g, :], tmp[:, 3 + g, :], ACT.Exp).then_inc(d_wexp, 1)

            for t in range(NT):
                for name in ACT_STEPS:
                    for p in range(3):
                        A, B = psum[:, 2 * p, :], psum[:, 2 * p + 1, :]
                        src = {"N2": ("NN2", cm(p, "N2", 512), A), "N4": ("NN4", cm(p, "N4", 512), A),
                               "N8": ("N8", cm(p, "N2"), A[:, 0:256]), "X1": ("X1", cm(p, "Nt", P), A[:, 0:P]),
                               "TF1": ("TF1", cm(p, "N2", 512), A), "TF2": ("TF2", cm(p, "N2", 512), A),
                               "GW": ("GW", cm(p, "N"), B[:, 0:256]), "GT": ("GW", cm(p, "E1", P), B[:, 256:384]),
                               "Y": ("Y", y[:, 3 + p, t * P:(t + 1) * P], A[:, 0:P])}[name]
                        act.wait_ge(rw_mm, done(MM_STEPS, src[0], t, p))
                        nc.scalar.activation(src[1], src[2], ACT.Copy).then_inc(rw_act, 1)
            for p in range(3):
                act.wait_ge(gn_in, p + 1)
                nc.scalar.activation(tmp[:, 3 + p, :], tmp[:, p, :], ACT.Square).then_inc(gn_act, 1)
            for p in range(3):
                act.wait_ge(gn_mm, 4 + p)
                nc.scalar.activation(tmp[:, 3 + p, :], psum[:, p, :], ACT.Sqrt, bias=cst2_eps, scale=1.0 / HD)\
                    .then_inc(gn_act, 1)

            def gate(q):
                act.wait_ge(gate_mm, q + 1)
                nc.scalar.activation(probs[:, q % 2, :], psum[:, 6 + q % 2, :], ACT.Sigmoid).then_inc(gate_act, 1)

            for q in range(2 * KD):
                gate(q)
            for m in range(2):
                act.wait_ge(s_gl, m + 1)
                nc.scalar.activation(hid[:, 14 + m, :], hid[:, 12 + m, :], ACT.Square).then_inc(s_gla, 1)
            for m in range(2):
                act.wait_ge(s_gl, 3 + m)
                nc.scalar.activation(hid[:, 14 + m, :], hid[:, 14 + m, :], ACT.Sigmoid, scale=2 * GELU_C).then_inc(s_gla, 1)
            for m in range(2):
                act.wait_ge(glu_mm, 3 + m)
                nc.scalar.activation(hid[:, 16 + m, :], psum[:, 2 + m, :], ACT.Sigmoid).then_inc(glu_act, 1)
            for q in range(2 * KD, 3 * KD):
                gate(q)
            norm(3 * LAYERS + 2)
            swiglu(2 * LAYERS)
            norm(3 * LAYERS + 3)

        @block.vector
        def _(dve):
            nc.vector.memset(upad[:, :, :], 0.0).then_inc(pads_zero, 1)
            nc.vector.memset(wsum[:, :, :], 0.0).then_inc(pads_zero, 1)
            dve.wait_ge(cst_in, 16)
            dve.wait_ge(gains_in, 32)
            dve.wait_ge(x_in, 16)
            for k in range(KD):
                dve.sem_inc(x_upd, 1)

            def norm(n, gain, into):
                dve.wait_ge(rms_ready, n + 1)
                nc.vector.reciprocal(tmp[:, 1, :], tmp[:, 0, :]).then_inc(rstd_ready, 1)
                dve.wait_ge(rstd_ready, n + 1)
                for k in range(KD):
                    nc.vector.scalar_tensor_tensor(out=into[:, k, :], in0=x[:, k, :], scalar=gain[:, k:k + 1],
                                                   in1=tmp[:, 1, :], op0=ALU.mult, op1=ALU.mult)\
                        .then_inc(h_ready if into is h else x_upd, 1)

            def residual(order, scale):
                for m, bank, ready, value in order:
                    dve.wait_ge(ready, value)
                    nc.vector.scalar_tensor_tensor(out=x[:, m, :], in0=psum[:, bank, :], scalar=scale, in1=x[:, m, :],
                                                   op0=ALU.mult, op1=ALU.add).then_inc(x_upd, 1)

            def swiglu(f, n0, scale=0.5):
                with dve.Fori(0, NJ // 2) as jj:
                    for s in range(2):
                        j = 2 * jj + s
                        dve.wait_ge(silu_ready, f * NJ + j + 1)
                        dve.wait_ge(ring_free, used(n0 + j))
                        nc.vector.tensor_tensor(hid[:, j, :], probs[:, s, :], psum[:, 2 + s, :], ALU.mult)\
                            .then_inc(hid_ready, 1)
                residual([(m, 4 + m, down_ready, 7 * f + m + 1) for m in range(3)]
                         + [(3, 7, wdr_free, used((f + 1) * NJ - 1))]
                         + [(4 + m, m, down_ready, 7 * f + m + 4) for m in range(4)], scale)

            def mixer(l):
                n0 = l * LAYER_ITEMS + NJ
                step = Chain(dve, vstep, VSTEPS * l, VSTEPS)
                dve.wait_ge(ring_free, used(n0))
                step(nc.vector.tensor_tensor(probs[0:32, 0, :], psum[0:32, 2, :], cos[0:32, :], ALU.mult))
                step(nc.vector.tensor_tensor(probs[0:32, 2, :], psum[32:64, 2, :], sin[32:64, :], ALU.mult))
                nc.vector.tensor_tensor(probs[64:96, 0, :], probs[0:32, 0, :], probs[0:32, 2, :], ALU.add).then_inc(kr_done, 1)
                g = slice(64, 70)
                step(nc.vector.tensor_scalar(probs[g, 2, :], psum[g, 2, :], gains[g, l, G_FB:G_FB + 1], None, ALU.add))
                nc.vector.scalar_tensor_tensor(out=probs[g, 1, :], in0=probs[g, 2, :], scalar=-1.0, in1=probs[g, 2, :],
                                               op0=ALU.mult, op1=ALU.max).then_inc(fz_ready, 1)
                step(nc.vector.tensor_scalar(probs[g, 2, :], probs[g, 2, :], 0.0, None, ALU.min))
                dve.wait_ge(lat_rms, 2 * l + 1)
                step(nc.vector.reciprocal(tmp[:, 0, :], tmp[:, 0, :]))
                nc.vector.scalar_tensor_tensor(out=tmp[:, 5, :], in0=psum[:, 1, :], scalar=gains[:, l, G_KVA:G_KVA + 1],
                                               in1=tmp[:, 0, :], op0=ALU.mult, op1=ALU.mult).then_inc(lat_n, 1)
                dve.wait_ge(lat_rms, 2 * l + 2)
                step(nc.vector.reciprocal(tmp[:, 1, :], tmp[:, 1, :]))
                for k in range(2):
                    nc.vector.scalar_tensor_tensor(out=tmp[:, 3 + k, :], in0=psum[:, 3 + k, :],
                                                   scalar=gains[:, l, G_QA + k:G_QA + k + 1],
                                                   in1=tmp[:, 1, :], op0=ALU.mult, op1=ALU.mult).then_inc(lat_n, 1)
                dve.wait_ge(fe_ready, l + 1)
                step(nc.vector.tensor_tensor(probs[g, 2, :], probs[g, 2, :], wdr[g, 1, :], ALU.subtract))
                step(nc.vector.tensor_tensor_scan(probs[g, 1, :], ones[g, 0:1].to_broadcast([6, S]), probs[g, 2, :], 0.0, ALU.mult, ALU.add))
                nc.vector.tensor_scalar(probs[g, 2, :], probs[g, 1, :], -1.0, None, ALU.mult).then_inc(cum_ready, 1)
                for p in range(3):
                    dve.wait_ge(ring_free, used(n0 + 3 + p))
                    for e in range(2):
                        nc.vector.tensor_copy(hid[0:HD, 18 + 2 * p + e, :], psum[HD * e:HD * e + HD, (0, 6, 0)[p], :])\
                            .then_inc(foxk_put, 1)
                for a in range(HEADS):
                    dve.wait_ge(p_sw, 2 * l + a // 3 + 1)
                    r = slice(32 * (a % 3), 32 * (a % 3) + 32)
                    b = a % 2
                    dve.wait_ge(p_mlaq, 6 * l + a + 1)
                    step(nc.vector.scalar_tensor_tensor(out=tmp[64:96, 1, :], in0=psum[64:96, (7, 0)[b], :], scalar=MLA_SCALE,
                                                        in1=cos[64:96, :], op0=ALU.mult, op1=ALU.mult))
                    step(nc.vector.scalar_tensor_tensor(out=tmp[64:96, 2, :], in0=psum[r, 5 + a // 3, :], scalar=MLA_SCALE,
                                                        in1=sin[r, :], op0=ALU.mult, op1=ALU.mult))
                    step(nc.vector.tensor_tensor(hid[64:96, a, :], tmp[64:96, 1, :], tmp[64:96, 2, :], ALU.add))
                    dve.sem_inc(mlaqr_put, 1)
                for p in range(3):
                    dve.wait_ge(p_mlak, 3 * l + p + 1)
                    for e in range(2):
                        nc.vector.tensor_copy(hid[0:NOPE, 12 + 2 * p + e, :], psum[HD * e:HD * e + HD, 1 + p, :])\
                            .then_inc(mlak_put, 1)

                def negmax(u):
                    n = (u % NT + 1) * P
                    dve.wait_ge(scores, UNITS * l + u + 1)
                    nc.vector.tensor_reduce(stat[:, u % 3, 0:1], psum[:, u % 3, 0:n], AX.X, ALU.max, negate=True)\
                        .then_inc(nmax, 1)

                def normalise(u):
                    n = (u % NT + 1) * P
                    dve.wait_ge(expd, UNITS * l + u + 1)
                    nc.vector.reciprocal(stat[:, u % 3, 2:3], stat[:, u % 3, 1:2]).then_inc(rsum, 1)
                    dve.wait_ge(rsum, UNITS * l + u + 1)
                    nc.vector.tensor_scalar(probs[:, u % 3, 0:n], probs[:, u % 3, 0:n], stat[:, u % 3, 2:3], None, ALU.mult)\
                        .then_inc(normd, 1)

                for u in range(UNITS + 1):
                    if u < UNITS:
                        negmax(u)
                    if u >= 1:
                        normalise(u - 1)
                residual([(m, (m + 4) % 8, ring_free, used(n0 + 7 + m // 3)) if m in (2, 5, 7)
                          else (m, (m + 4) % 8, wout_ready, 5 * l + (1, 2, 0, 3, 4, 0, 5)[m]) for m in range(KD)], 1.0)
                step.end()

            with dve.Fori(0, LAYERS) as l:
                norm(3 * l, gains[:, l, G_N1:G_N1 + 8], h)
                swiglu(2 * l, l * LAYER_ITEMS)
                norm(3 * l + 1, gains[:, l, G_NM:G_NM + 8], h)
                mixer(l)
                norm(3 * l + 2, gains[:, l, G_N2:G_N2 + 8], h)
                swiglu(2 * l + 1, l * LAYER_ITEMS + NJ + MIX_ITEMS)
            norm(3 * LAYERS, gains[:, 0, G_FIN:G_FIN + 8], x)
            norm(3 * LAYERS + 1, g2s[:, H_NM:H_NM + 8], h)
            base = LAYERS * LAYER_ITEMS
            step = Chain(dve, w_step, 0, W_STEPS)
            TT, TS, STT = nc.vector.tensor_tensor, nc.vector.tensor_scalar, nc.vector.scalar_tensor_tensor
            raws = ["xwa", "xg", "r0", "k0", "v0", "r1", "k1", "v1", "r2", "k2", "v2"]
            mix_col = [9, 10, 0, 3, 6, 1, 4, 7, 2, 5, 8]

            def mix(name, o):
                i = raws.index(name)
                dve.wait_ge(read, NUM[name] + 1)
                z, zp = raw[:, i % 4, 16:], raw[:, i % 4, 15:15 + S]
                step(TT(o, zp, z, ALU.subtract))
                c = H_MIX + mix_col[i]
                STT(out=o, in0=o, scalar=g2s[:, c:c + 1], in1=z, op0=ALU.mult, op1=ALU.add).then_inc(mixed, 1)
                dve.wait_ge(mixed, i + 1)

            dve.wait_ge(mixw2_in, 32)
            mix("xwa", tmp[:, 0, :])
            mix("xg", tmp[:, 1, :])

            def col(c, p):
                return g2s[:, c + p:c + p + 1]

            def chunks(t):
                return t.rearrange("p (c s) -> p c s", s=CHUNK)

            for p in range(3):
                if p == 0:
                    dve.wait_ge(lora_act, 3)
                rr, kx, vv = tmp[:, 4, :], tmp[:, 5, :], vfm[:, p, :]
                mix(f"r{p}", rr)
                mix(f"k{p}", kx)
                mix(f"v{p}", vv)
                dve.wait_ge(read, NUM[f"la{p}"] + 1)
                if p:
                    dve.wait_ge(rwkv_fm, p)
                TS(tmp[:, 0, :], kx, col(H_KK, p), None, ALU.mult).then_inc(kk_in, 1)
                step(TS(probs[:, 0, :], icl[:, p, :], -1.0, col(H_KA, p), ALU.add, ALU.mult))
                step(STT(out=kx, in0=probs[:, 0, :], scalar=1.0, in1=kx, op0=ALU.add, op1=ALU.mult))
                if p == 0:
                    dve.wait_ge(read, NUM["la2"] + 1)
                STT(out=tmp[:, 2, :], in0=rr, scalar=col(H_RK, p), in1=kx, op0=ALU.mult, op1=ALU.mult).then_inc(bonus_in, 1)
                step(nc.vector.tensor_tensor_scan(probs[:, 0, :], restart, sig[:, p, :], 0.0, ALU.mult, ALU.add))
                c = chunks(probs[:, 0, :])
                mid = c[:, :, CHUNK // 2 - 1:CHUNK // 2]
                step(TT(chunks(probs[:, 1, :]), c, mid.to_broadcast([P, 8, CHUNK]), ALU.subtract))
                step(TT(probs[:, 2, :], probs[:, 1, :], sig[:, p, :], ALU.subtract))
                d1 = chunks(probs[:, 1, :])
                TT(dvec[:, p, 0:7], d1[:, 0:7, CHUNK - 1], c[:, 1:8, CHUNK // 2 - 1], ALU.add).then_inc(decay_in, 1)
                dve.wait_ge(read, NUM[f"kn{p}"] + 1)
                step(TS(tmp[:, 1, :], tmp[:, 1, :], 1e-12, None, ALU.max))
                step(nc.vector.reciprocal(tmp[:, 1, :], tmp[:, 1, :]))
                step(TT(tmp[:, 0, :], tmp[:, 0, :], tmp[:, 1, :], ALU.mult))
                dve.wait_ge(decay_exp, 4 * p + 4)
                STT(out=fm["A"][:, p, :], in0=tmp[:, 0, :], scalar=-1.0, in1=probs[:, 2, :], op0=ALU.mult, op1=ALU.mult)
                step(TT(tmp[:, 0, :], tmp[:, 0, :], icl[:, p, :], ALU.mult))
                TT(fm["B"][:, p, :], tmp[:, 0, :], probs[:, 0, :], ALU.mult)
                TT(fm["K"][:, p, :], kx, probs[:, 0, :], ALU.mult)
                TT(fm["R"][:, p, :], rr, probs[:, 1, :], ALU.mult).then_inc(rwkv_fm, 1)
                dve.wait_ge(read, NUM[f"bn{p}"] + 1)
                TT(bonus[:, p, :], tmp[:, 3, :], vv, ALU.mult).then_inc(bonus_put, 1)
                dve.wait_ge(bonus_put, p + 1)

            ar, ai, ls = (g2s[:, c:c + 8] for c in (H_AR, H_AI, H_LS))

            def sp_(i):
                return spar[:, i, :]

            dve.wait_ge(s_trig, 1)
            step(TT(sp_(1), ai, sp_(0), ALU.mult))
            step(TS(sp_(2), sp_(1), 1.0 / TWO_PI, ROUND, ALU.mult, ALU.add))
            step(TS(sp_(2), sp_(2), -ROUND, None, ALU.add))
            step(STT(out=sp_(1), in0=sp_(2), scalar=-PI_HI, in1=sp_(1), op0=ALU.mult, op1=ALU.add))
            step(STT(out=sp_(1), in0=sp_(2), scalar=-PI_LO, in1=sp_(1), op0=ALU.mult, op1=ALU.add))
            step(TS(sp_(2), sp_(1), 3.1415925, -3.1415925, ALU.min, ALU.max))
            step(STT(out=sp_(4), in0=sp_(2), scalar=-1.0, in1=sp_(2), op0=ALU.mult, op1=ALU.max))
            step(TS(sp_(4), sp_(4), -1.0, 1.5707963, ALU.mult, ALU.add))
            dve.sem_inc(s_par, 1)
            step(TT(sp_(6), ar, sp_(0), ALU.mult))
            step(TS(sp_(6), sp_(6), -100.0, 1.0 / 64, ALU.max, ALU.mult))
            step(TS(sp_(7), sp_(6), 1.0 / 5040, None, ALU.mult))
            for f_ in (1 / 720, 1 / 120, 1 / 24, 1 / 6, 0.5, 1.0):
                step(STT(out=sp_(7), in0=sp_(7), scalar=f_, in1=sp_(6), op0=ALU.add, op1=ALU.mult))
            for _ in range(6):
                step(STT(out=sp_(7), in0=sp_(7), scalar=2.0, in1=sp_(7), op0=ALU.add, op1=ALU.mult))
            step(TS(sp_(8), sp_(7), 1.0, None, ALU.add))
            dve.wait_ge(s_trig, 3)
            step(TT(sp_(6), sp_(8), sp_(5), ALU.mult))
            step(TT(sp_(7), sp_(8), sp_(3), ALU.mult))
            step(TS(sp_(6), sp_(6), -1.0, None, ALU.add))
            step(TT(sp_(9), ar, ar, ALU.mult))
            step(TT(sp_(10), ai, ai, ALU.mult))
            step(TT(sp_(9), sp_(9), sp_(10), ALU.add))
            step(nc.vector.reciprocal(sp_(9), sp_(9)))
            step(TT(sp_(10), sp_(6), ar, ALU.mult))
            step(TT(sp_(11), sp_(7), ai, ALU.mult))
            step(TT(sp_(10), sp_(10), sp_(11), ALU.add))
            step(TT(sp_(10), sp_(10), sp_(9), ALU.mult))
            step(TT(sp_(11), sp_(7), ar, ALU.mult))
            step(TT(sp_(12), sp_(6), ai, ALU.mult))
            step(TT(sp_(11), sp_(11), sp_(12), ALU.subtract))
            step(TT(sp_(11), sp_(11), sp_(9), ALU.mult))
            cr, ci = (mixw[:, W2_C + i * P:W2_C + (i + 1) * P].rearrange("p (s c) -> p s c", s=8) for i in range(2))
            fr, fi = (spar[:, i, :].rearrange("p (s o) -> p s o", o=1).to_broadcast([P, 8, 16]) for i in (10, 11))
            t_ = [sw[:, i, :, :] for i in range(4)]
            step(TT(t_[0], cr, fr, ALU.mult))
            step(TT(t_[1], ci, fi, ALU.mult))
            step(TT(t_[2], cr, fi, ALU.mult))
            step(TT(t_[3], ci, fr, ALU.mult))
            step(TT(cr, t_[0], t_[1], ALU.subtract))
            step(TT(t_[2], t_[2], t_[3], ALU.add))
            step(TS(ci, t_[2], -1.0, None, ALU.mult))
            dve.sem_inc(s_cw, 1)

            def powers(tab, n_max):
                n = 1
                while n < n_max:
                    c0, s0 = tab[:, 0, :, 1:n + 1], tab[:, 1, :, 1:n + 1]
                    cn, sn = (tab[:, i, :, n:n + 1].to_broadcast([P, 8, n]) for i in range(2))
                    u_ = [sw[:, i, :, 0:n] for i in range(4)]
                    step(TT(u_[0], c0, cn, ALU.mult))
                    step(TT(u_[1], s0, sn, ALU.mult))
                    step(TT(u_[2], s0, cn, ALU.mult))
                    step(TT(u_[3], c0, sn, ALU.mult))
                    step(TT(tab[:, 0, :, n + 1:2 * n + 1], u_[0], u_[1], ALU.subtract))
                    step(TT(tab[:, 1, :, n + 1:2 * n + 1], u_[2], u_[3], ALU.add))
                    n *= 2

            for tab in (fine, coarse):
                step(nc.vector.memset(tab[:, 0, :, 0:1], 1.0))
                step(nc.vector.memset(tab[:, 1, :, 0:1], 0.0))
            step(nc.vector.tensor_copy(fine[:, 0, :, 1:2], spar[:, 5, :].rearrange("p (s o) -> p s o", o=1)))
            step(nc.vector.tensor_copy(fine[:, 1, :, 1:2], spar[:, 3, :].rearrange("p (s o) -> p s o", o=1)))
            powers(fine, 32)
            for i in range(2):
                step(nc.vector.tensor_copy(coarse[:, i, :, 1:2], fine[:, i, :, 32:33]))
            powers(coarse, 16)
            dve.sem_inc(s_par, 1)

            def d_keys(u):
                return 2 if u // 8 == 0 and u % NT else 1

            for u in range(UNITS2 + 1):
                if u < UNITS2:
                    dve.wait_ge(d_scores, u + 1)
                    nc.vector.tensor_reduce(dstat[:, 0, u:u + 1], psum[:, u % 3, 0:d_keys(u) * P], AX.X, ALU.max,
                                            negate=True).then_inc(d_nmax, 1)
                if u >= 1:
                    v = u - 1
                    n = d_keys(v) * P
                    dve.wait_ge(d_exp, v + 1)
                    nc.vector.reciprocal(stat[:, v % 3, 2:3], dstat[:, 1, v:v + 1]).then_inc(d_rsum, 1)
                    dve.wait_ge(d_rsum, v + 1)
                    TS(probs[:, v % 3, 0:n], probs[:, v % 3, 0:n], stat[:, v % 3, 2:3], None, ALU.mult).then_inc(d_norm, 1)
            dve.wait_ge(d_ln, 1)
            TT(dstat[:, 2, :], dstat[:, 2, :], dstat[:, 0, :], ALU.subtract).then_inc(d_lse, 1)

            def ordered(t, g):
                return t if g == 0 else t.rearrange("p (a r) -> p r a", r=4 if g == 1 else 16)

            def as_group(t, g):
                return t if g == 0 else t.rearrange("p (r a) -> p r a", r=4 if g == 1 else 16)

            for g in range(3):
                dve.wait_ge(d_lseb, g + 1)
                step(nc.vector.tensor_copy(ordered(tmp[:, g, :], g), as_group(psum[:, g, :], g)))
            top, tot = raw[:, 0, 0:S], raw[:, 1, 0:S]
            step(TT(top, tmp[:, 0, :], tmp[:, 1, :], ALU.max))
            step(TT(top, top, tmp[:, 2, :], ALU.max))
            for g in range(3):
                TT(tmp[:, 3 + g, :], tmp[:, g, :], top, ALU.subtract).then_inc(d_diff, 1)
            dve.wait_ge(d_wexp, 3)
            step(TT(tot, tmp[:, 3, :], tmp[:, 4, :], ALU.add))
            step(TT(tot, tot, tmp[:, 5, :], ALU.add))
            step(nc.vector.reciprocal(tot, tot))
            for g in range(3):
                step(TT(tmp[:, 3 + g, :], tmp[:, 3 + g, :], tot, ALU.mult))
                TT(ordered(y[:, g, :], g), as_group(psum[:, 5 + g, :], g), ordered(tmp[:, 3 + g, :], g), ALU.mult)\
                    .then_inc(attn_y, 1)
            dve.wait_ge(attn_y, 3)
            nc.vector.memset(zst, 0.0).then_inc(z_zero, 1)
            dve.wait_ge(z_zero, 1)

            def two(t):
                return t.rearrange("p (e c) -> p e c", e=2)

            def mask2(m):
                return m.rearrange("p (o c) -> p o c", o=1).to_broadcast([P, 2, P])

            for t in range(NT):
                for name in VEC_STEPS:
                    for p in range(3):
                        A, B = psum[:, 2 * p, :], psum[:, 2 * p + 1, :]

                        def after(mm_name):
                            dve.wait_ge(rw_mm, done(MM_STEPS, mm_name, t, p))

                        def masked(o, src, m):
                            return TT(two(cm(p, o)), two(src), mask2(m), ALU.mult)

                        def add(o, src, other):
                            return TT(cm(p, o), src, cm(p, other), ALU.add)

                        def rows(e):
                            return slice(HD * e, HD * e + HD)

                        if name == "N":
                            after("M12b")
                            masked("N", A[:, 0:256], mk16l)
                            masked("E1", A[:, 0:256], mke1)
                            masked("E2", A[:, 0:256], mke2)
                            last = masked("Nt", A[:, 256:512], mk16u)
                        elif name == "M34":
                            after("M34b")
                            masked("Mak", B[:, 0:256], mkus)
                            last = masked("Mrb", B[:, 256:512], mkui)
                        elif name == "Y1":
                            dve.wait_ge(rw_vec, done(VEC_STEPS, "N", t, p))
                            last = TT(two(cm(p, "Ya")), two(cm(p, "Nt")), mask2(ident), ALU.add)
                        elif name == "M5":
                            after("M5b")
                            last = masked("Mrk", B[:, 0:256], mkui)
                        elif name in ("Y2", "Y4", "Y8", "Y32", "XT"):
                            o, other = {"Y2": ("Yb", "Ya"), "Y4": ("Ya", "Yb"), "Y8": ("Yb", "Ya"),
                                        "Y32": ("Ya", "Yb"), "XT": ("Yb", "Ya")}[name]
                            after(name)
                            prev = {"Y2": "Y1", "Y4": "Y2", "Y8": "Y4", "Y32": "Y8", "XT": "Y32"}[name]
                            dve.wait_ge(rw_vec, done(VEC_STEPS, prev, t, p))
                            last = add(o, B[:, 0:256], other)
                        elif name == "PT":
                            after("PTb")
                            last = TT(two(cm(p, "E2", P)), two(A[:, 0:P]),
                                      ident64.rearrange("p (o c) -> p o c", o=1).to_broadcast([P, 2, HD]), ALU.add)
                        elif name in ("Z0", "Z1"):
                            c = 2 * t + int(name[1])
                            after("S" + name[1] + "b")
                            if c < 7:
                                last = TS(zst[:, p, (c + 1) % 4, :], A[:, 0:HD], dvec[:, p, c:c + 1], None, ALU.mult)
                            else:
                                last = nc.vector.engine_nop()
                        else:
                            after("Ub")
                            dve.wait_ge(rw_act, done(ACT_STEPS, "GW", t, p))
                            last = TT(cm(p, "N4", P), B[:, 0:P], cm(p, "N")[:, P:256], ALU.add)
                        last.then_inc(rw_vec, 1)

            for p in range(3):
                dve.wait_ge(gn_mm, p + 1)
                STT(out=tmp[:, p, :], in0=psum[:, p, :], scalar=-1.0 / HD, in1=y[:, 3 + p, :], op0=ALU.mult, op1=ALU.add)\
                    .then_inc(gn_in, 1)
            for p in range(3):
                dve.wait_ge(gn_act, 4 + p)
                dve.wait_ge(gn_in, p + 1)
                step(nc.vector.reciprocal(tmp[:, 3 + p, :], tmp[:, 3 + p, :]))
                step(TT(tmp[:, p, :], tmp[:, p, :], tmp[:, 3 + p, :], ALU.mult))
                step(TS(tmp[:, p, :], tmp[:, p, :], col(H_LW, p), col(H_LB, p), ALU.mult, ALU.add))
                step(TT(tmp[:, p, :], tmp[:, p, :], bonus[:, p, :], ALU.add))
                TT(y[:, 3 + p, :], tmp[:, p, :], glora[:, p, :], ALU.mult).then_inc(rwkv_y, 1)

            def merge(q):
                m = q % KD
                dve.wait_ge(gate_act, q + 1)
                dve.wait_ge(branch_mm, q + 1)
                if q < KD:
                    TT(merged[:, m, :], psum[:, 4 + q % 2, :], probs[:, q % 2, :], ALU.mult).then_inc(merged_put, 1)
                else:
                    dve.wait_ge(merged_put, q)
                    step(TT(probs[:, 2, :], psum[:, 4 + q % 2, :], probs[:, q % 2, :], ALU.mult))
                    TT(merged[:, m, :], merged[:, m, :], probs[:, 2, :], ALU.add).then_inc(merged_put, 1)

            def rotate(s):
                c, sn = tabs[:, s % 2, 0, :], tabs[:, s % 2, 1, :]
                br, bi = psum[:, 0, :], psum[:, 1, :]
                dve.wait_ge(s_tab, s + 1)
                dve.wait_ge(s_bu, s + 1)
                step(TT(hid[:, 12, :], br, c, ALU.mult))
                step(TT(hid[:, 14, :], bi, sn, ALU.mult))
                step(TT(hid[:, 13, :], bi, c, ALU.mult))
                TT(hid[:, 15, :], br, sn, ALU.mult).then_inc(s_rot, 1)
                dve.wait_ge(s_rot, s + 1)
                step(TT(hid[:, 12, :], hid[:, 12, :], hid[:, 14, :], ALU.add))
                step(TT(hid[:, 13, :], hid[:, 13, :], hid[:, 15, :], ALU.subtract))
                mag = spar[:, 8, s:s + 1].to_broadcast([P, S])
                step(nc.vector.tensor_tensor_scan(hid[:, 14, :], mag, hid[:, 12, :], 0.0, ALU.mult, ALU.add))
                step(nc.vector.tensor_tensor_scan(hid[:, 15, :], mag, hid[:, 13, :], 0.0, ALU.mult, ALU.add))

            def turn_back(s):
                c, sn = tabs[:, s % 2, 0, :], tabs[:, s % 2, 1, :]
                qr, qi = hid[:, 14, :], hid[:, 15, :]
                if s >= 2:
                    dve.wait_ge(s_c, s - 1)
                step(TT(hid[:, 12, :], qr, c, ALU.mult))
                step(TT(hid[:, 13, :], qi, sn, ALU.mult))
                step(TT(xst[:, s % 2, 0, :], hid[:, 12, :], hid[:, 13, :], ALU.subtract))
                step(TT(hid[:, 12, :], qr, sn, ALU.mult))
                step(TT(hid[:, 13, :], qi, c, ALU.mult))
                TT(xst[:, s % 2, 1, :], hid[:, 12, :], hid[:, 13, :], ALU.add).then_inc(s_back, 1)
                dve.wait_ge(s_back, s + 1)

            for s in range(8):
                rotate(s)
                merge(2 * s)
                turn_back(s)
                merge(2 * s + 1)
            for m in range(2):
                dve.wait_ge(s_ym, m + 1)
                STT(out=hid[:, 12 + m, :], in0=ussm[:, m, :], scalar=col(H_D, m), in1=psum[:, 2 + m, :],
                    op0=ALU.mult, op1=ALU.add).then_inc(s_gl, 1)
            for m in range(2):
                dve.wait_ge(s_gla, 1 + m)
                step(TS(hid[:, 14 + m, :], hid[:, 14 + m, :], 0.044715, 1.0, ALU.mult, ALU.add))
                TT(hid[:, 14 + m, :], hid[:, 14 + m, :], hid[:, 12 + m, :], ALU.mult).then_inc(s_gl, 1)
            for m in range(2):
                dve.wait_ge(s_gla, 3 + m)
                TT(hid[:, 22 + m, :], hid[:, 14 + m, :], hid[:, 12 + m, :], ALU.mult).then_inc(s_gl, 1)
            for m in range(2):
                dve.wait_ge(glu_mm, 1 + m)
                dve.wait_ge(glu_act, 1 + m)
                TT(y[:, 6 + m, :], psum[:, m, :], hid[:, 16 + m, :], ALU.mult).then_inc(ssm_y, 1)
            for q in range(2 * KD, 3 * KD):
                merge(q)
            step.end()
            residual([(m, (m + 4) % 8, out2_ready, m + 1) for m in range(KD)], 1.0)
            norm(3 * LAYERS + 2, g2s[:, H_NF:H_NF + 8], h)
            swiglu(2 * LAYERS, base, 1.0)
            norm(3 * LAYERS + 3, g2s[:, H_FIN:H_FIN + 8], x)

        @block.gpsimd
        def _(pool):
            pool.dma_start(cstb[:, :, :], t_in["cstb"]).then_inc(cstb_in, 16)
            pool.wait_ge(cst_in, 16)
            with pool.Fori(0, LAYERS) as l:
                step = Chain(pool, gstep, GSTEPS * l, GSTEPS)
                pool.wait_ge(kr_done, l + 1)
                pool.sem_inc(carrier, 1)
                for a in range(HEADS):
                    last = nc.gpsimd.tensor_copy(hid[64:96, 12 + a, :], probs[64:96, 0, :])
                last.then_inc(kpe_put, 1)
                pool.wait_ge(cum_ready, l + 1)
                pool.sem_inc(carrier, 1)
                pool.dma_start(hid[64:65, 6:12, :], probs[64:70, 1, :]).then_inc(aug_in, 16)
                pool.dma_start(hid[65:66, 18:24, :], probs[64:70, 2, :]).then_inc(aug_in, 16)
                pool.dma_start(hid[65:66, 6:12, :], t_in["onerow"]).then_inc(aug_in, 16)
                pool.dma_start(hid[64:65, 18:24, :], t_in["onerow"]).then_inc(aug_in, 16)
                pool.wait_ge(pads_zero, 2)
                pool.wait_ge(kpe_put, l + 1)
                pool.wait_ge(pool_in, 2 * l + 2)
                Z = 16
                rc = cst[:, C_RC:C_RC + 2 * S].rearrange("p (t c) -> p t c", t=2)

                def shifted(o, i, d, r=slice(0, P)):
                    return nc.gpsimd.tensor_tensor(o[r, Z:Z + S], i[r, Z:Z + S], i[r, Z - d:Z - d + S], ALU.add)

                wa, wb = wsum[:, 0, :], wsum[:, 1, :]
                lo, hi = slice(0, 64), slice(64, 128)
                step(shifted(wa, upad[:, 0, :], 1))
                step(shifted(wb, wa, 2, hi))
                step(nc.gpsimd.tensor_tensor(wb[lo, Z:], wa[lo, Z:], rc[lo, 0, :], ALU.mult))
                step(nc.gpsimd.tensor_tensor(wb[hi, Z:], wb[hi, Z:], rc[hi, 0, :], ALU.mult))
                pool.wait_ge(lat_n, 3 * l + 3)
                pool.wait_ge(p_mlaq, 6 * l + 6)
                step(nc.gpsimd.tensor_tensor(tmp[:, 0, :], wb[:, Z:], upad[:, 0, Z:], ALU.subtract))
                pool.sem_inc(pooled, 1)
                step(shifted(wa, upad[:, 1, :], 1))
                step(shifted(wb, wa, 2))
                step(shifted(wa, wb, 4))
                step(shifted(wb, wa, 8, hi))
                step(nc.gpsimd.tensor_tensor(wb[lo, Z:], wa[lo, Z:], rc[lo, 1, :], ALU.mult))
                step(nc.gpsimd.tensor_tensor(wb[hi, Z:], wb[hi, Z:], rc[hi, 1, :], ALU.mult))
                step(nc.gpsimd.tensor_tensor(tmp[:, 4, :], wb[:, Z:], upad[:, 1, Z:], ALU.subtract))
                pool.sem_inc(pooled, 1)
                step.end()
            pool.wait_ge(gn_mm, 3)
            pool.wait_ge(s_cw, 1)
            pool.wait_ge(s_par, 2)
            nc.gpsimd.memset(cmat, 0.0).then_inc(s_cz, 1)
            pool.wait_ge(s_cz, 1)
            for im in range(2):
                src = mixw[:, W2_C + im * P:W2_C + (im + 1) * P].rearrange("p (s c) -> p s c", s=8)
                for s in range(8):
                    for half in range(2):
                        r = slice(64 * half, 64 * half + 64)
                        c = 32 * (s % 4) + 16 * half
                        last = nc.gpsimd.tensor_copy(cmat[r, im, s, c:c + 16], src[r, s, :])
            last.then_inc(s_cz, 1)
            pool.wait_ge(s_cz, 2)
            pool.sem_inc(s_cw, 1)

            def spread(t, axis):
                if axis:
                    return t.rearrange("p (o j) -> p o j", o=1).to_broadcast([P, 16, 32])
                return t.rearrange("p (i o) -> p i o", o=1).to_broadcast([P, 16, 32])

            def grid(t):
                return t.rearrange("p (i j) -> p i j", j=32)

            for s in range(8):
                if s >= 2:
                    pool.wait_ge(s_back, s - 1)
                ca, sa = (spread(coarse[:, i, s, 0:16], 0) for i in range(2))
                cb, sb_ = (spread(fine[:, i, s, 0:32], 1) for i in range(2))
                for n, (o, u, v) in enumerate(((hid[:, 16, :], ca, cb), (hid[:, 17, :], sa, sb_),
                                               (hid[:, 18, :], sa, cb), (hid[:, 19, :], ca, sb_))):
                    nc.gpsimd.tensor_tensor(grid(o), u, v, ALU.mult).then_inc(s_cz, 1)
                pool.wait_ge(s_cz, 2 + 6 * s + 4)
                nc.gpsimd.tensor_tensor(tabs[:, s % 2, 0, :], hid[:, 16, :], hid[:, 17, :], ALU.subtract).then_inc(s_cz, 1)
                nc.gpsimd.tensor_tensor(tabs[:, s % 2, 1, :], hid[:, 18, :], hid[:, 19, :], ALU.add).then_inc(s_cz, 1)
                pool.wait_ge(s_cz, 2 + 6 * s + 6)
                pool.sem_inc(s_tab, 1)


_OUT_SHAPE = (1, S, D)


def pack_inputs(a):
    import numpy as np
    f = np.float32
    t = {}
    t["x"] = a["x"][0].T.reshape(KD, P, S).transpose(1, 0, 2)

    def tiles(w):
        return w.reshape(-1, P, w.shape[1]).transpose(1, 0, 2)

    gus, d1s, d2s = [], [], []

    def ffn(gu, down):
        g = gu[:, :FF].reshape(KD, P, NJ, P)
        u = gu[:, FF:].reshape(KD, P, NJ, P)
        gus.append(np.stack([g, u]).transpose(3, 2, 0, 1, 4).reshape(NJ, P, 2 * KD * P))
        d1s.append(down[:, :HALF].reshape(NJ, P, HALF))
        d2s.append(down[:, HALF:].reshape(2, NJ // 2, P, HALF).transpose(0, 2, 1, 3))

    for l in range(LAYERS):
        ffn(a["ffn1_w_gu"][l], a["ffn1_w_down"][l])
        ffn(a["ffn2_w_gu"][l], a["ffn2_w_down"][l])
    ffn(a["ffn_w_gate_up_2"][0], a["ffn_w_down_2"][0])
    t["wgu"], t["wd1"], t["wd2"] = np.stack(gus), np.stack(d1s), np.stack(d2s)

    mix = np.zeros((LAYERS, MIX_ITEMS, P, SLOT), f)
    small = np.zeros((LAYERS, P, M_W), f)
    gains = np.zeros((P, LAYERS, G_W), f)
    for l in range(LAYERS):
        w = a["w_in"][l]
        kr = w[:, 384:416]
        fox = w[:, 672:1824]
        items = [np.concatenate([w[:, 256:384], kr, kr[:, 16:], kr[:, :16], w[:, 1824:1830]], 1),
                 w[:, 0:256], w[:, 416:672]]
        items += [np.concatenate([fox[:, P * p:P * p + P], fox[:, 384 + P * p:384 + P * p + P]], 1) for p in range(3)]
        items += [fox[:, 768:1152]]
        for i, it in enumerate(items):
            mix[l, i, :, :KD * it.shape[1]] = tiles(it).reshape(P, -1)
        for m in range(KD):
            mix[l, 7 + m // 3, :, (m % 3) * D:(m % 3 + 1) * D] = tiles(a["w_out"][l][:, m * P:(m + 1) * P]).reshape(P, -1)
        wq = a["w_q_b"][l].reshape(QR, HEADS, NOPE + ROPE)
        sw = np.concatenate([wq[:, :, NOPE + ROPE // 2:], wq[:, :, NOPE:NOPE + ROPE // 2]], 2).reshape(QR, -1)
        small[l, :, M_QB:M_QB + 1536] = tiles(np.concatenate([wq.reshape(QR, -1), sw], 1)).reshape(P, -1)
        wkv = a["w_kv_b"][l].reshape(KVR, HEADS, 2, 64)
        small[l, :, M_KV:M_KV + 768] = wkv.transpose(0, 2, 1, 3).reshape(KVR, -1)
        small[l, :, M_PW:M_PW + 128] = a["pool_w"][l].reshape(2, P, 64).transpose(1, 0, 2).reshape(P, -1)
        for c, v in ((G_N1, a["ffn1_norm"][l]), (G_NM, a["mix_norm"][l]), (G_N2, a["ffn2_norm"][l]),
                     (G_QA, a["q_a_norm"][l]), (G_KVA, a["kv_a_norm"][l]), (G_PS, a["pool_scale"][l]),
                     (G_FIN, a["final_norm"])):
            n = v.shape[0] // P
            gains[:, l, c:c + n] = v.reshape(n, P).T
        gains[64:70, l, G_FB] = a["fox_b_f"][l]
    t["wmix"], t["wsmall"], t["gains"] = mix, small, gains

    cst = np.zeros((P, C_W), f)
    cst[:, C_ID:C_ID + P] = np.eye(P)
    cst[:, C_ONE:C_ONE + P] = 1.0
    freq = (10000.0 ** (-np.arange(0, ROPE, 2, dtype=f) / f(ROPE))).astype(f)
    ang = (np.arange(S, dtype=f)[None, :] * freq[:, None]).astype(f)
    row = np.arange(P) % ROPE
    sign = np.where(row < ROPE // 2, -1.0, 1.0)[:, None]
    cst[:, C_COS:C_COS + S] = np.cos(ang.astype(np.float64))[row % (ROPE // 2)]
    cst[:, C_SIN:C_SIN + S] = np.sin(ang.astype(np.float64))[row % (ROPE // 2)] * sign
    count = np.arange(1, S + 1)
    for i, w in enumerate((2, 4, 8, 16)):
        cst[64 * (i % 2):64 * (i % 2) + 64, C_RC + S * (i // 2):C_RC + S * (i // 2) + S] = 1.0 / np.minimum(count, w)
    cst[:, C_EPS] = EPS
    cst[:, C_EPS + 1] = 64e-5
    t["cst"] = cst
    b = np.zeros((P, 4, P), f)
    b[:, 0] = np.eye(P)
    b[:, 1] = np.where(np.arange(P)[None, :] <= np.arange(P)[:, None], 0.0, -1e30)
    qi, kj = np.arange(P)[:, None], np.arange(P)[None, :]
    b[:, 2] = np.where(kj >= qi, 0.0, -1e30)
    b[:, 3] = np.where((kj <= qi) & (kj // 32 == qi // 32), 0.0, -1e30)
    t["cstb"] = b
    t["onerow"] = np.ones((1, HEADS, S), f)

    mix2 = np.zeros((B2_ITEMS, P, SLOT), f)
    w = a["w_in_2"][0]
    o = 3 * RW
    rw, lora = w[:, o:o + 3 * RW], w[:, 2 * o:2 * o + 256]
    su, gate = w[:, 2 * o + 256:2 * o + 512], w[:, 2 * o + 512:]
    items = [lora]
    items += [np.concatenate([rw[:, n * RW + p * P:n * RW + p * P + P] for n in range(3)], 1) for p in range(3)]
    items += [w[:, 0:RW], w[:, RW:2 * RW], w[:, 2 * RW:3 * RW], su]
    for i, it in enumerate(items):
        mix2[i, :, :KD * it.shape[1]] = tiles(it).reshape(P, -1)
    for b, wb in ((0, a["w_branch_attn_2"][0]), (1, a["w_branch_rwkv_2"][0]), (2, a["w_branch_ssm_2"][0])):
        for m in range(KD):
            q = b * KD + m
            col = np.concatenate([gate[:, b * D + m * P:b * D + (m + 1) * P], wb[:, m * P:(m + 1) * P]], 0)
            n = col.shape[0]
            mix2[8 + q // 2, :, (q % 2) * 1408:(q % 2) * 1408 + n] = tiles(col).reshape(P, -1)
    for m in range(KD):
        mix2[20 + m // 2, :, (m % 2) * D:(m % 2 + 1) * D] = tiles(a["w_out_2"][0][:, m * P:(m + 1) * P]).reshape(P, -1)
    t["wmix2"] = mix2
    sm = np.zeros((P, M_W), f)
    sm[0:64, W2_WA:W2_WA + RW] = a["rwkv_w2_2"][0]
    sm[64:128, W2_WA:W2_WA + RW] = a["rwkv_a2_2"][0]
    sm[:, W2_G:W2_G + RW] = a["rwkv_g2_2"][0]
    sm[:, W2_GV:W2_GV + 512] = tiles(a["ssm_glu_val_2"][0]).reshape(P, -1)
    sm[:, W2_GG:W2_GG + 512] = tiles(a["ssm_glu_gate_2"][0]).reshape(P, -1)
    for i, n in enumerate(("re", "im")):
        c = a[f"ssm_c_{n}_2"][0]
        sm[:, W2_C + i * P:W2_C + (i + 1) * P] = c.transpose(0, 2, 1).reshape(8, P, 16).transpose(1, 0, 2).reshape(P, P)
        b = a[f"ssm_b_{n}_2"][0]
        for g in range(16):
            r = 16 * (g % 8)
            c0 = W2_B + (g // 8 * 2 + i) * P + 64 * (g % 2)
            sm[r:r + 16, c0:c0 + 64] = b[g].T
    t["wsmall2"] = sm
    g2 = np.zeros((P, G2_W), f)
    for c, n in ((H_NM, "norm_mix"), (H_NF, "norm_ffn"), (H_FIN, "norm_final"), (H_MIX, "rwkv_shift_mix"),
                 (H_W0, "rwkv_w0"), (H_A0, "rwkv_a0"), (H_KK, "rwkv_k_k"), (H_KA, "rwkv_k_a"), (H_RK, "rwkv_r_k"),
                 (H_LW, "rwkv_ln_w"), (H_LB, "rwkv_ln_b"), (H_AR, "ssm_a_re"), (H_AI, "ssm_a_im"), (H_D, "ssm_d")):
        v = a[n + "_2"].reshape(-1, P)
        g2[:, c:c + v.shape[0]] = v.T
    g2[:, H_LS:H_LS + 8] = np.repeat(a["ssm_log_step_2"][0], 64).reshape(8, P).T
    t["g2s"] = g2
    i, j = np.arange(P)[:, None], np.arange(P)[None, :]
    low = j < i
    same = i // 64 == j // 64
    masks = [low & (i // 16 == j // 16), low & (i // 32 == j // 32) & (i // 16 != j // 16),
             low & same & (i // 32 != j // 32), (j > i) & (i // 16 == j // 16), (j > i) & same, (j >= i) & same, same]
    cs2 = np.zeros((P, 2048), f)
    for n, m in enumerate(masks):
        cs2[:, n * P:(n + 1) * P] = m
    cs2[:, 7 * P:7 * P + 64] = np.arange(64)[None, :] == i % 64
    cs2[:, 960:960 + S] = np.arange(S) % CHUNK != 0
    t["cst2"] = cs2
    return {k: np.ascontiguousarray(v) for k, v in t.items()}


def kernel(**inputs):
    import numpy as np
    import concourse.bacc as bacc
    from concourse.bass_utils import run_bass_kernel_spmd

    nc = bacc.Bacc("TRN2", target_bir_lowering=False, num_devices=1)
    arrays = pack_inputs({k: np.asarray(v) for k, v in inputs.items()})
    t_in = {k: nc.dram_tensor("in_" + k, v.shape, mybir.dt.from_np(v.dtype), kind="ExternalInput").ap()
            for k, v in arrays.items()}
    out = nc.dram_tensor("out", (P, KD, S), F32, kind="ExternalOutput").ap()
    build(nc, t_in, out)
    r = run_bass_kernel_spmd(nc, [{"in_" + k: v for k, v in arrays.items()}], core_ids=[0])
    got = r.results[0]["out"]
    return np.ascontiguousarray(got.transpose(1, 0, 2).reshape(D, S).T).reshape(_OUT_SHAPE)
```

```python
from contextlib import ExitStack

import concourse.bass as bass
from concourse import mybir

ALU = mybir.AluOpType
ACT = mybir.ActivationFunctionType
AX = mybir.AxisListType
F32 = mybir.dt.float32
BF16 = mybir.dt.bfloat16
F32R = mybir.dt.float32r

P = 128
S = 512
D = 1024
KD = D // P
FF = 2816
NJ = FF // P
HALF = D // 2
LAYERS = 2
EPS = 1e-6
NT = S // P

QR, KVR, ROPE, NOPE = 256, 128, 32, 64
HEADS = 6
HD = 64
MLA_SCALE = (NOPE + ROPE) ** -0.5
FOX_SCALE = HD ** -0.5
UNITS = 2 * HEADS * NT

SLOT = 8 * 384
MIX_COLS = [198, 256, 256, 256, 256, 256, 256, 128]
MIX_OUT = 4
MIX_ITEMS = len(MIX_COLS) + MIX_OUT
FFN_ITEMS = NJ + 6
LAYER_ITEMS = 2 * FFN_ITEMS + MIX_ITEMS

C_ID, C_ONE, C_COS, C_SIN, C_RC, C_EPS = 0, 128, 256, 768, 1280, 2304
C_W = 2308
M_QB, M_KV, M_PW = 0, 1536, 2304
M_W = 2560
G_N1, G_NM, G_N2, G_QA, G_KVA, G_PS, G_FB, G_FIN = 0, 8, 16, 24, 26, 27, 29, 30
G_W = 38



RW = 384
CHUNK = 64
KAPPA = 0.6065306597126334
B2_ITEMS = 24
UNITS2 = 6 * NT
W2_WA, W2_G, W2_GV, W2_GG, W2_C, W2_B = 0, 384, 768, 1280, 1792, 2048
(H_NM, H_NF, H_FIN, H_MIX, H_W0, H_A0, H_KK, H_KA, H_RK, H_LW, H_LB, H_AR, H_AI, H_LS, H_D) = (
    0, 8, 16, 24, 35, 38, 41, 44, 47, 50, 53, 56, 64, 72, 80)
G2_W = 82
PRODUCTS = (["xwa", "xg", "r0", "k0", "v0"] + ["lw0", "lw1", "lw2", "la0", "la1", "la2", "lg0", "lg1", "lg2"]
            + ["r1", "k1", "v1", "kn0", "bn0", "r2", "k2", "v2", "kn1", "bn1", "aq0", "aq1", "aq2", "kn2", "bn2",
               "ak0", "ak1", "ak2", "av0", "av1", "av2", "su0", "su1", "av2t"]
            + [f"t{n}{t}" for n in "ABKV" for t in range(NT)])
NUM = {n: i for i, n in enumerate(PRODUCTS)}
MM_STEPS = ("M12a", "M12b", "M34a", "M34b", "NN2", "M5a", "M5b", "Y2", "NN4", "Y4", "N8", "X1", "Y8", "TF1", "Y32",
            "TF2", "XT", "GW", "PTa", "PTb", "S0a", "S0b", "S1a", "S1b", "Ua", "Ub", "Y")
VEC_STEPS = ("N", "M34", "Y1", "M5", "Y2", "Y4", "Y8", "Y32", "XT", "PT", "Z0", "Z1", "U")
ACT_STEPS = ("N2", "N4", "N8", "X1", "TF1", "TF2", "GW", "GT", "Y")


def done(steps, name, t, p):
    return (t * len(steps) + steps.index(name)) * 3 + p + 1

TWO_PI = 6.283185307179586
PI_HI = 6.28125
PI_LO = TWO_PI - PI_HI
ROUND = 12582912.0
GELU_C = 0.7978845608028654
W_STEPS = 283


DOWN_COLS = [4 * HALF] * 5 + [2 * HALF]
OUT_SPLIT = {30: 8, 34: 9}
NEXT_ITEM = {1: 1, 7: 2, 11: 3, 15: 4, 19: 5}


class Chain:

    def __init__(self, eng, sem, base, steps):
        self.eng, self.sem, self.base, self.steps, self.k = eng, sem, base, steps, 0

    def __call__(self, ins):
        self.k += 1
        ins.then_inc(self.sem, 1)
        self.eng.wait_ge(self.sem, self.base + self.k)

    def end(self):
        assert self.k == self.steps, (self.k, self.steps)


def used(n):
    return n + 3


def build(nc, t_in, out):
    with ExitStack() as ctx:
        def sb(name, shape, dt=F32):
            return ctx.enter_context(nc.sbuf_tensor(name, shape, dt))

        def sem(name):
            return ctx.enter_context(nc.semaphore(name))

        psum = ctx.enter_context(nc.psum_tensor("psum", [P, 8, 512], F32))
        x = sb("x", [P, KD, S])
        with ExitStack() as whole:
            h, ring, wdr, d2, hid = (whole.enter_context(nc.sbuf_tensor(n, shape, F32)) for n, shape in (
                ("h", [P, KD, S]),
                ("ring", [P, 2, SLOT]),
                ("wdr", [P, 2, HALF]),
                ("d2", [P, 22, S]),
                ("hid", [P, 24, S])))
        h_lo = sb("h_lo", [P, KD, S], F32R)
        ring_lo = sb("ring_lo", [P, 2, SLOT], F32R)
        wdr_lo = sb("wdr_lo", [P, 2, HALF], F32R)
        highs = sb("highs", [P, 22, S], F32R)
        hid_r = sb("hid_r", [P, 24, S], F32R)
        mixw = sb("mixw", [P, M_W])
        gains = sb("gains", [P, LAYERS, G_W])
        cst = sb("cst", [P, C_W])
        cstb = sb("cstb", [P, 4, P], BF16)
        scr = sb("scr", [P, 6720])
        tmp = scr[:, 0:6 * S].rearrange("p (a c) -> p a c", a=6)
        probs = scr[:, 6 * S:9 * S].rearrange("p (a c) -> p a c", a=3)
        upad = scr[:, 4608:5664].rearrange("p (a c) -> p a c", a=2)
        wsum = scr[:, 5664:6720].rearrange("p (a c) -> p a c", a=2)
        root_of_eps = sb("root_of_eps", [P, 1])
        stat = sb("stat", [P, 3, 4])
        ident = cst[:, C_ID:C_ID + P]
        ones = cst[:, C_ONE:C_ONE + P]
        cos = cst[:, C_COS:C_COS + S]
        sin = cst[:, C_SIN:C_SIN + S]
        eps = cst[:, C_EPS:C_EPS + 1]

        h_hi = highs[:, 0:8, :]
        gu_hi = highs[:, 8:16, :].rearrange("p a b -> p (a b)").rearrange("p (s c) -> p s c", s=2)
        hid_hi, hid_lo = highs[:, 16:18, :], highs[:, 18:20, :]
        wd_hi = highs[:, 20:22, :]
        mix_hi = [highs[:, 14 + 4 * b:18 + 4 * b, :].rearrange("p a b -> p (a b)") for b in range(2)]
        out_hi = [hid_r[:, 12 * b:12 * b + 4, :].rearrange("p a b -> p (a b)") for b in range(2)]
        hid_squares = hid[:, 4:12, :]
        y_hi, y_lo = h_lo, highs[:, 0:8, :]
        y = d2[:, 0:8, :]
        vt = [d2[:, 8 + 3 * b:11 + 3 * b, :].rearrange("p a b -> p (a b)").rearrange(
            "p (t c) -> p t c", t=NT) for b in range(2)]
        pt = [d2[:, 14 + 4 * b:18 + 4 * b, :] for b in range(2)]

        cst_in = sem("cst_in")
        cstb_in = sem("cstb_in")
        gains_in = sem("gains_in")
        x_in = sem("x_in")
        ring_in = [sem("ring_in0"), sem("ring_in1")]
        wdr_in = [sem("wdr_in0"), sem("wdr_in1")]
        mixw_in = sem("mixw_in")
        aug_in = sem("aug_in")
        out_done = sem("out_done")
        ring_free = sem("ring_free")
        wdr_free = sem("wdr_free")
        sq_ready = sem("sq_ready")
        sumsq_ready = sem("sumsq_ready")
        rms_ready = sem("rms_ready")
        pads_zero = sem("pads_zero")
        rstd_ready = sem("rstd_ready")
        h_ready = sem("h_ready")
        x_upd = sem("x_upd")
        h_high = sem("h_high")
        h_split = sem("h_split")
        ring_high = sem("ring_high")
        ring_split = sem("ring_split")
        wd_high = sem("wd_high")
        wd_split = sem("wd_split")
        hid_high = sem("hid_high")
        hid_split = sem("hid_split")
        hid_used = sem("hid_used")
        y_split = sem("y_split")
        gate_ready = sem("gate_ready")
        silu_ready = sem("silu_ready")
        hid_ready = sem("hid_ready")
        down_ready = sem("down_ready")
        p_kv = sem("p_kv")
        p_qa = sem("p_qa")
        p_pool = sem("p_pool")
        p_foxqk = sem("p_foxqk")
        p_foxv = sem("p_foxv")
        p_sw = sem("p_sw")
        p_mlaq = sem("p_mlaq")
        p_mlak = sem("p_mlak")
        p_mlav = sem("p_mlav")
        lat_sq = sem("lat_sq")
        lat_ss = sem("lat_ss")
        lat_rms = sem("lat_rms")
        lat_n = sem("lat_n")
        pool_in = sem("pool_in")
        pooled = sem("pooled")
        p_pooly = sem("p_pooly")
        pool_out = sem("pool_out")
        kr_done = sem("kr_done")
        kpe_put = sem("kpe_put")
        fz_ready = sem("fz_ready")
        fe_ready = sem("fe_ready")
        cum_ready = sem("cum_ready")
        foxq_put = sem("foxq_put")
        foxk_put = sem("foxk_put")
        foxv_put = sem("foxv_put")
        mlaqn_put = sem("mlaqn_put")
        mlaqr_put = sem("mlaqr_put")
        mlak_put = sem("mlak_put")
        mlav_put = sem("mlav_put")
        scores = sem("scores")
        nmax = sem("nmax")
        expd = sem("expd")
        rsum = sem("rsum")
        normd = sem("normd")
        turned = sem("turned")
        pt_put = sem("pt_put")
        yh_ready = sem("yh_ready")
        y_put = sem("y_put")
        wout_ready = sem("wout_ready")
        carrier = sem("carrier")
        vstep = sem("vstep")
        astep = sem("astep")
        gstep = sem("gstep")
        VSTEPS, GSTEPS = 26, 12


        made = sem("made")
        read = sem("read")
        mixw2_in = sem("mixw2_in")
        mixed = sem("mixed")
        lora_act = sem("lora_act")
        kk_in = sem("kk_in")
        kk_sq = sem("kk_sq")
        bonus_in = sem("bonus_in")
        decay_in = sem("decay_in")
        decay_exp = sem("decay_exp")
        rwkv_fm = sem("rwkv_fm")
        bonus_put = sem("bonus_put")
        w_step = sem("w_step")
        d_scores = sem("d_scores")
        d_nmax = sem("d_nmax")
        d_exp = sem("d_exp")
        d_norm = sem("d_norm")
        d_turned = sem("d_turned")
        d_put = sem("d_put")
        d_out = sem("d_out")
        d_ln = sem("d_ln")
        d_lse = sem("d_lse")
        d_lseb = sem("d_lseb")
        d_diff = sem("d_diff")
        d_wexp = sem("d_wexp")
        d_rsum = sem("d_rsum")
        attn_y = sem("attn_y")
        rw_mm = sem("rw_mm")
        rw_vec = sem("rw_vec")
        rw_act = sem("rw_act")
        gn_mm = sem("gn_mm")
        gn_act = sem("gn_act")
        gn_in = sem("gn_in")
        rwkv_y = sem("rwkv_y")
        z_zero = sem("z_zero")
        s_par = sem("s_par")
        s_trig = sem("s_trig")
        s_bu = sem("s_bu")
        s_rot = sem("s_rot")
        s_back = sem("s_back")
        s_c = sem("s_c")
        s_cw = sem("s_cw")
        s_ym = sem("s_ym")
        s_gl = sem("s_gl")
        s_gla = sem("s_gla")
        glu_mm = sem("glu_mm")
        glu_act = sem("glu_act")
        ssm_y = sem("ssm_y")
        gate_mm = sem("gate_mm")
        branch_mm = sem("branch_mm")
        gate_act = sem("gate_act")
        merged_put = sem("merged_put")
        out2_ready = sem("out2_ready")
        merged_high = sem("merged_high")
        merged_split = sem("merged_split")
        out2_high = sem("out2_high")
        out2_split = sem("out2_split")
        raw = scr[:, 4608:6720].rearrange("p (a c) -> p a c", a=4)
        fm = {n: hid[:, 3 * i:3 * i + 3, :] for i, n in enumerate("ABKR")}
        tm = {n: hid[:, 12 + 3 * i:15 + 3 * i, :].rearrange("p a b -> p (a b)").rearrange("p (t c) -> p t c", t=NT)
              for i, n in enumerate("ABKV")}
        sig, icl = hid[:, 12:15, :], hid[:, 15:18, :]
        vfm = d2[:, 3:6, :]
        ussm = d2[:, 6:8, :]
        glora, bonus = d2[:, 8:11, :], d2[:, 11:14, :]
        dq, dk = d2[:, 14:17, :], d2[:, 17:20, :]
        dv = [d2[:, 20, :], d2[:, 21, :], wdr[:, 0, :]]
        dpt = wdr[:, 1, :].rearrange("p (b c) -> p b c", b=2)
        c2 = cst[:, C_COS:C_COS + 2048]
        mk16l, mke1, mke2, mk16u, mkus, mkui = (c2[:, i * P:(i + 1) * P] for i in range(6))
        heads2 = c2[:, 6 * P:7 * P]
        ident64 = c2[:, 7 * P:7 * P + 64]
        restart = c2[:, 960:960 + S]
        g2s = sb("g2s", [P, G2_W])
        dvec = sb("dvec", [P, 3, 8])
        dstat = sb("dstat", [P, 3, 24])
        core = [d2[:, 14:22, :].rearrange("p a b -> p (a b)")[:, 0:3328], scr[:, 0:3328], scr[:, 3328:6656]]
        zst = d2[:, 14:22, :].rearrange("p a b -> p (a b)")[:, 3328:4096].rearrange("p (q s c) -> p q s c", q=3, s=4)
        R = {n: i for i, n in enumerate(
            ("N", "E1", "E2", "Nt", "Mak", "Mrb", "Mrk", "N2", "N2t", "Ya", "Yb", "N4", "N4t"))}

        def cm(p, name, w=256):
            return core[p][:, R[name] * 256:R[name] * 256 + w]

        merged = hid[:, 0:KD, :]
        merged_hi, merged_lo = highs[:, 8:16, :], hid_r[:, 0:KD, :]
        out2_hi = [t.rearrange("p a b -> p (a b)") for t in (highs[:, 16:20, :], hid_r[:, 12:16, :])]
        tabs = hid[:, 8:12, :].rearrange("p (b i) c -> p b i c", b=2)
        cmat = d2[:, 14:18, :].rearrange("p a b -> p (a b)").rearrange("p (i s c) -> p i s c", i=2, s=8)
        xst = d2[:, 18:22, :].rearrange("p (b i) c -> p b i c", b=2)
        spar = sb("spar", [P, 13, 8])
        sw = sb("sw", [P, 4, 8, 16])
        fine = sb("fine", [P, 2, 8, 33])
        coarse = sb("coarse", [P, 2, 8, 17])
        cst2_eps = cst[:, C_EPS + 1:C_EPS + 2]
        s_tab = sem("s_tab")
        s_cz = sem("s_cz")
        wgu, wd1, wd2, wmix, wsmall = t_in["wgu"], t_in["wd1"], t_in["wd2"], t_in["wmix"], t_in["wsmall"]

        block = ctx.enter_context(nc.Block())

        def mm(o, w, r, start, stop):
            return nc.tensor.matmul(o, w, r, start=start, stop=stop, skip_group_check=True)

        @block.sync
        def _(sp):
            sp.dma_start(x[:, :, :], t_in["x"]).then_inc(x_in, 16)

            def gu_item(f, j, s, n):
                sp.wait_ge(ring_free, n + 1)
                sp.dma_start(ring[:, s, 0:2 * KD * P], wgu[f, j]).then_inc(ring_in[s], 16)

            def wd_item(f, j, s, n):
                sp.wait_ge(wdr_free, n + 1)
                sp.dma_start(wdr[:, s, :], wd1[f, j]).then_inc(wdr_in[s], 16)

            def swiglu(f, n0):
                with sp.Fori(0, NJ // 2) as jj:
                    for s in range(2):
                        gu_item(f, 2 * jj + s, s, n0 + 2 * jj + s)
                        wd_item(f, 2 * jj + s, s, f * NJ + 2 * jj + s)
                for i in range(6):
                    sp.wait_ge(ring_free, n0 + NJ + i + 1)
                    sp.dma_start(ring[:, i % 2, 0:DOWN_COLS[i]], wd2[f, i][:, 0:DOWN_COLS[i]]).then_inc(ring_in[i % 2], 16)

            def mixer(l, n0):
                for i in range(MIX_ITEMS):
                    c = 2 * D if i >= len(MIX_COLS) else KD * MIX_COLS[i]
                    sp.wait_ge(ring_free, n0 + i + 1)
                    sp.dma_start(ring[:, i % 2, 0:c], wmix[l, i][:, 0:c]).then_inc(ring_in[i % 2], 16)

            with sp.Fori(0, LAYERS) as l:
                swiglu(2 * l, l * LAYER_ITEMS)
                mixer(l, l * LAYER_ITEMS + FFN_ITEMS)
                swiglu(2 * l + 1, l * LAYER_ITEMS + FFN_ITEMS + MIX_ITEMS)
            base = LAYERS * LAYER_ITEMS
            last = ["xg", "v0", "v1", "v2", "aq2", "ak2", "av2", "su1"]
            for i in range(8):
                if i < 2:
                    sp.wait_ge(ring_free, base + i + 1)
                else:
                    sp.wait_ge(made, NUM[last[i - 2]] + 1)
                sp.dma_start(ring[:, i % 2, :], t_in["wmix2"][i]).then_inc(ring_in[i % 2], 16)
            for i in range(12):
                if i < 2:
                    sp.wait_ge(made, NUM[last[6 + i]] + 1)
                else:
                    sp.wait_ge(branch_mm, 2 * (i - 2) + 2)
                sp.dma_start(ring[:, i % 2, :], t_in["wmix2"][8 + i]).then_inc(ring_in[i % 2], 16)
            for i in range(4):
                if i < 2:
                    sp.wait_ge(branch_mm, 2 * (10 + i) + 2)
                else:
                    sp.wait_ge(out2_ready, 2 * (i - 2) + 2)
                sp.dma_start(ring[:, i % 2, :], t_in["wmix2"][20 + i]).then_inc(ring_in[i % 2], 16)
            sp.wait_ge(out2_ready, KD)
            swiglu(2 * LAYERS, base)
            sp.wait_ge(x_upd, 88)
            sp.dma_start(out, x[:, :, :]).then_inc(out_done, 16)
            sp.wait_ge(out_done, 16)

        @block.tensor
        def _(pe):
            pe.sem_inc(ring_free, 2)
            pe.sem_inc(wdr_free, 2)
            pe.wait_ge(cst_in, 16)
            pe.wait_ge(cstb_in, 16)

            def norm(n, squares=h):
                for k in range(KD):
                    pe.wait_ge(sq_ready, 8 * n + k + 1)
                    last = mm(psum[:, 4, :], ones, squares[:, k, :], k == 0, k == KD - 1)
                last.then_inc(sumsq_ready, 1)

            def mm3(o, w, r, start, stop):
                mm(o, w[0], r[0], start, False)
                mm(o, w[0], r[1], False, False)
                return mm(o, w[1], r[0], False, stop)

            def gate_up(j, s, n0):
                pe.wait_ge(ring_split, n0 + j + 1)
                for g in range(2):
                    for k in range(KD):
                        c = slice((g * KD + k) * P, (g * KD + k + 1) * P)
                        last = mm3(psum[:, 2 * g + s, :], (gu_hi[:, s, c], ring_lo[:, s, c]),
                                   (h_hi[:, k, :], h_lo[:, k, :]), k == 0, k == KD - 1)
                    last.then_inc(ring_free if g else gate_ready, 1)

            def first_gate_up(n0, h0):
                pe.wait_ge(ring_split, n0 + 1)
                for k in range(KD):
                    pe.wait_ge(h_split, h0 + k + 1)
                    for g in range(2):
                        c = slice((g * KD + k) * P, (g * KD + k + 1) * P)
                        last = mm3(psum[:, 2 * g, :], (gu_hi[:, 0, c], ring_lo[:, 0, c]),
                                   (h_hi[:, k, :], h_lo[:, k, :]), k == 0, k == KD - 1)
                        if k == KD - 1:
                            last.then_inc(ring_free if g else gate_ready, 1)

            def down1(j, s, f, start, stop):
                pe.wait_ge(wd_split, f * NJ + j + 1)
                pe.wait_ge(hid_split, 2 * f * NJ + j + 1)
                for m in range(4):
                    c = slice(m * P, (m + 1) * P)
                    last = mm3(psum[:, 4 + m, :], (wd_hi[:, s, c], wdr_lo[:, s, c]),
                               (hid_hi[:, s, :], hid_lo[:, s, :]), start, stop)
                    if m == 3:
                        last.then_inc(wdr_free, 1)
                    elif stop:
                        last.then_inc(down_ready, 1)

            def swiglu(f, n0, h0):
                first_gate_up(n0, h0)
                gate_up(1, 1, n0)
                down1(0, 0, f, True, False)
                with pe.Fori(1, NJ // 2) as jj:
                    for s in range(2):
                        j = 2 * jj + s
                        pe.wait_ge(hid_ready, f * NJ + j - 1)
                        gate_up(j, s, n0)
                        down1(j - 1, 1 - s, f, False, False)
                down1(NJ - 1, 1, f, False, True)
                for k in range(NJ):
                    i = k // 4
                    if k % 4 == 0:
                        pe.wait_ge(ring_split, n0 + NJ + i + 1)
                    pe.wait_ge(hid_split, (2 * f + 1) * NJ + k + 1)
                    for m in range(4):
                        c = slice((k % 4) * HALF + m * P, (k % 4) * HALF + (m + 1) * P)
                        last = mm3(psum[:, m, :], (gu_hi[:, i % 2, c], ring_lo[:, i % 2, c]),
                                   (hid_hi[:, k % 2, :], hid_lo[:, k % 2, :]), k == 0, k == NJ - 1)
                        if m == 3:
                            last.then_inc(ring_free if k % 4 == 3 or k == NJ - 1 else hid_used, 1)
                        elif k == NJ - 1:
                            last.then_inc(down_ready, 1)

            def mixer(l, n0):
                def item(i, cols):
                    pe.wait_ge(ring_split, n0 + i + 1)
                    return [w[:, 0:KD * cols].rearrange("p (k c) -> p k c", k=KD)
                            for w in (mix_hi[i % 2], ring_lo[:, i % 2, :])]

                def project(bank, w, c0, m, done):
                    for k in range(KD):
                        last = mm3(psum[0:m, bank, :], (w[0][:, k, c0:c0 + m], w[1][:, k, c0:c0 + m]),
                                   (h_hi[:, k, :], h_lo[:, k, :]), k == 0, k == KD - 1)
                    last.then_inc(done, 1)

                w = item(0, 198)
                for k in range(KD):
                    pe.wait_ge(h_split, 24 * l + 8 + k + 1)
                    for bank, c, done_ in ((1, slice(0, 128), p_kv), (2, slice(128, 198), ring_free)):
                        last = mm3(psum[0:c.stop - c.start, bank, :], (w[0][:, k, c], w[1][:, k, c]),
                                   (h_hi[:, k, :], h_lo[:, k, :]), k == 0, k == KD - 1)
                        if k == KD - 1:
                            last.then_inc(done_, 1)
                w = item(1, 256)
                project(3, w, 0, 128, p_qa)
                project(4, w, 128, 128, ring_free)
                w = item(2, 256)
                project(7, w, 0, 128, p_pool)
                project(0, w, 128, 128, ring_free)
                pe.wait_ge(lat_sq, 3 * l + 1)
                mm(psum[:, 5, :], ones, tmp[:, 0, :], True, True).then_inc(lat_ss, 1)
                pe.wait_ge(lat_sq, 3 * l + 3)
                mm(psum[:, 6, :], ones, tmp[:, 1, :], True, False)
                mm(psum[:, 6, :], ones, tmp[:, 2, :], False, True).then_inc(lat_ss, 1)
                for p in range(3):
                    w = item(3 + p, 256)
                    if p != 1:
                        pe.wait_ge(pool_in, 2 * l + 2)
                    else:
                        pe.wait_ge(lat_rms, 2 * l + 2)
                    if p == 2:
                        pe.wait_ge(foxq_put, 6 * l + 2)
                        pe.wait_ge(foxk_put, 6 * l + 2)
                    project((7, 5, 7)[p], w, 0, 128, p_foxqk)
                    project((0, 6, 0)[p], w, 128, 128, ring_free)
                pe.wait_ge(lat_n, 3 * l + 3)
                pe.wait_ge(cum_ready, l + 1)
                for i, c0 in ((6, 0), (7, 256)):
                    n = MIX_COLS[i]
                    w = item(i, n)
                    for t in range(NT):
                        c = slice(t * P, (t + 1) * P)
                        for k in range(KD):
                            last = mm3(psum[:, 1 + t, c0:c0 + n], (h_hi[:, k, c], h_lo[:, k, c]),
                                       (w[0][:, k, :], w[1][:, k, :]), k == 0, k == KD - 1)
                        if t == NT - 1:
                            last.then_inc(ring_free, 1)
                        elif i == 7:
                            last.then_inc(p_foxv, 1)
                pe.wait_ge(mixw_in, 16 * l + 16)
                wq = mixw[:, M_QB:M_QB + 1536].rearrange("p (k c) -> p k c", k=2)
                pe.wait_ge(foxq_put, 6 * l + 4)
                pe.wait_ge(foxk_put, 6 * l + 4)
                for g in range(2):
                    for k in range(2):
                        last = mm(psum[0:96, 5 + g, :], wq[:, k, 576 + 96 * g:672 + 96 * g], tmp[:, 3 + k, :], k == 0, k == 1)
                    last.then_inc(p_sw, 1)
                for a in range(HEADS):
                    if a == 0:
                        pe.wait_ge(foxq_put, 6 * l + 6)
                        pe.wait_ge(foxk_put, 6 * l + 6)
                    if a >= 2:
                        pe.wait_ge(mlaqn_put, 6 * l + a - 1)
                        pe.wait_ge(mlaqr_put, 6 * l + a - 1)
                    for k in range(2):
                        last = mm(psum[0:96, (7, 0)[a % 2], :], wq[:, k, 96 * a:96 * a + 96], tmp[:, 3 + k, :], k == 0, k == 1)
                    last.then_inc(p_mlaq, 1)
                wkv = mixw[:, M_KV:M_KV + 768]
                pe.wait_ge(foxv_put, 4 * l + 4)
                for p in range(3):
                    mm(psum[:, 1 + p, :], wkv[:, p * P:(p + 1) * P], tmp[:, 5, :], True, True).then_inc(p_mlak, 1)
                for t in range(NT):
                    if t:
                        pe.wait_ge(mlak_put, 6 * l + 2 * t)
                    mm(psum[:, (4, 1, 2, 3)[t], 0:384], tmp[:, 5, t * P:(t + 1) * P], wkv[:, 384:768], True, True)\
                        .then_inc(p_mlav, 1)
                pe.wait_ge(mlaqn_put, 6 * l + 6)
                pe.wait_ge(mlaqr_put, 6 * l + 6)
                pe.wait_ge(mlak_put, 6 * l + 6)
                pe.wait_ge(mlav_put, 4 * l + 4)
                pe.wait_ge(kpe_put, l + 1)
                pe.wait_ge(aug_in, 64 * l + 64)

                def score(u):
                    a, i = divmod(u, NT)
                    rows, n = (96 if a < HEADS else 66), (i + 1) * P
                    if u >= 3:
                        pe.wait_ge(expd, UNITS * l + u - 2)
                    mm(psum[:, u % 3, 0:n], hid[0:rows, a, i * P:(i + 1) * P], hid[0:rows, 12 + a, 0:n], True, False)
                    mm(psum[:, u % 3, n - P:n], cstb[:, 0, :], cstb[:, 1, :], False, True).then_inc(scores, 1)

                def turn(u):
                    i = u % NT
                    pe.wait_ge(normd, UNITS * l + u + 1)
                    if u >= 2:
                        pe.wait_ge(pt_put, UNITS * l + u - 1)
                    for t in range(i + 1):
                        last = nc.tensor.transpose(psum[:, 3 + u % 2, t * P:(t + 1) * P],
                                                   probs[:, u % 3, t * P:(t + 1) * P], ident)
                    last.then_inc(turned, 1)

                def attend(a):
                    pair = a // 2
                    pe.wait_ge(pt_put, UNITS * l + 4 * a + 4)
                    if pair >= 2:
                        pe.wait_ge(y_split, 8 * l + pair - 1)
                    c = HD * (a % HEADS)
                    for t in range(NT):
                        last = mm(psum[HD * (a % 2):HD * (a % 2) + HD, 5 + pair % 2, t * P:S],
                                  vt[a // HEADS][:, t, c:c + HD], pt[a % 2][:, t, t * P:S], t == 0, t == NT - 1)
                    last.then_inc(yh_ready, 1)

                for u in range(UNITS + 4):
                    if u < UNITS:
                        score(u)
                    if 2 <= u < UNITS + 2:
                        turn(u - 2)
                    if u >= 4 and (u - 4) % NT == NT - 1:
                        attend((u - 4) // NT)
                pe.wait_ge(pooled, 2 * l + 2)
                pe.sem_inc(carrier, 1)
                for t in range(2):
                    for g in range(2):
                        r = slice(HD * g, HD * g + HD)
                        last = mm(psum[r, 7, :] if t else psum[r, 0, :], mixw[r, M_PW + HD * t:M_PW + HD * t + HD],
                                  tmp[r, 4 * t, :], True, True)
                    last.then_inc(p_pooly, 1)
                for m in range(KD):
                    i = len(MIX_COLS) + m // 2
                    if m % 2 == 0:
                        pe.wait_ge(ring_split, n0 + i + 1)
                    if m == 0:
                        pe.wait_ge(y_split, 8 * l + 8)
                    for k in range(KD):
                        c = slice((m % 2) * D + k * P, (m % 2) * D + (k + 1) * P)
                        last = mm3(psum[:, (m + 4) % 8, :], (out_hi[i % 2][:, c], ring_lo[:, i % 2, c]),
                                   (y_hi[:, k, :], y_lo[:, k, :]), k == 0, k == KD - 1)
                    last.then_inc(ring_free if m % 2 else wout_ready, 1)

            with pe.Fori(0, LAYERS) as l:
                norm(3 * l)
                swiglu(2 * l, l * LAYER_ITEMS, 24 * l)
                norm(3 * l + 1)
                mixer(l, l * LAYER_ITEMS + FFN_ITEMS)
                norm(3 * l + 2, hid_squares)
                swiglu(2 * l + 1, l * LAYER_ITEMS + FFN_ITEMS + MIX_ITEMS, 24 * l + 16)
            norm(3 * LAYERS)
            base = LAYERS * LAYER_ITEMS
            norm(3 * LAYERS + 1)
            pe.wait_ge(mixw2_in, 32)

            def ring_item(i, cols):
                pe.wait_ge(ring_in[i % 2], (base // 2 + i // 2 + 1) * 16)
                return ring[:, i % 2, 0:KD * cols].rearrange("p (k c) -> p k c", k=KD)

            def product(name):
                n = NUM[name]
                if n >= 8:
                    pe.wait_ge(read, n - 7)
                return psum[:, n % 8, :]

            def project(name, w, c0):
                o = product(name)
                for k in range(KD):
                    last = mm(o, w[:, k, c0:c0 + P], h[:, k, :], k == 0, k == KD - 1)
                last.then_inc(made, 1)

            def head_sum(name, src, ready, value):
                pe.wait_ge(ready, value)
                mm(product(name), heads2, src, True, True).then_inc(made, 1)

            def rkv(p):
                w = ring_item(1 + p, 384)
                for i, n in enumerate("rkv"):
                    project(f"{n}{p}", w, i * P)

            w = ring_item(0, 256)
            firsts = [(product(n), c) for n, c in (("xwa", slice(0, P)), ("xg", slice(P, 2 * P)))]
            for k in range(KD):
                pe.wait_ge(h_ready, 24 * LAYERS + k + 1)
                for o, c in firsts:
                    last = mm(o, w[:, k, c], h[:, k, :], k == 0, k == KD - 1)
                    if k == KD - 1:
                        last.then_inc(made, 1)
            rkv(0)
            lo, hi = slice(0, 64), slice(64, 128)
            for n, r, src, need in (("lw", lo, 2, 1), ("la", hi, 2, 2), ("lg", slice(0, P), 3, 3)):
                pe.wait_ge(lora_act, need)
                c = W2_G if n == "lg" else W2_WA
                for p in range(3):
                    mm(product(f"{n}{p}"), mixw[r, c + p * P:c + (p + 1) * P], tmp[r, src, :], True, True).then_inc(made, 1)
            rkv(1)
            head_sum("kn0", tmp[:, 1, :], kk_sq, 1)
            head_sum("bn0", tmp[:, 2, :], bonus_in, 1)
            rkv(2)
            head_sum("kn1", tmp[:, 1, :], kk_sq, 2)
            head_sum("bn1", tmp[:, 2, :], bonus_in, 2)
            w = ring_item(4, 384)
            for g in range(3):
                project(f"aq{g}", w, g * P)
            head_sum("kn2", tmp[:, 1, :], kk_sq, 3)
            head_sum("bn2", tmp[:, 2, :], bonus_in, 3)
            w = ring_item(5, 384)
            for g in range(3):
                project(f"ak{g}", w, g * P)
            w = ring_item(6, 384)
            for g in range(2):
                o = product(f"av{g}")
                for t in range(NT):
                    for k in range(KD):
                        if g == 0:
                            tok = h[:, k, t * P:(t + 1) * P]
                        else:
                            tok = h[:, k, :].rearrange("p (a r) -> p r a", r=4)[:, t, :]
                        last = mm(o[:, t * P:(t + 1) * P], tok, w[:, k, g * P:(g + 1) * P], k == 0, k == KD - 1)
                last.then_inc(made, 1)
            project("av2", w, 2 * P)
            w = ring_item(7, 256)
            project("su0", w, 0)
            project("su1", w, P)
            o = product("av2t")
            pe.wait_ge(read, NUM["av2"] + 1)
            for t in range(NT):
                last = nc.tensor.transpose(o[:, t * P:(t + 1) * P], hid[:, 18, t * P:(t + 1) * P], ident)
            last.then_inc(made, 1)
            pe.wait_ge(rwkv_fm, 3)
            for n in "ABKV":
                for t in range(NT):
                    o = product(f"t{n}{t}")
                    for p in range(3):
                        src = vfm[:, p, t * P:(t + 1) * P] if n == "V" else fm[n][:, p, t * P:(t + 1) * P]
                        last = nc.tensor.transpose(o[:, p * P:(p + 1) * P], src, ident)
                    last.then_inc(made, 1)
            pe.wait_ge(read, len(PRODUCTS))

            def d_keys(u):
                g, i = u // 8, u % NT
                return 2 if g == 0 and i else 1

            def d_score(u):
                hd, i = divmod(u, NT)
                g, r = hd // 2, slice(HD * (hd % 2), HD * (hd % 2) + HD)
                n = d_keys(u)
                if u >= 3:
                    pe.wait_ge(d_exp, u - 2)
                o = psum[:, u % 3, 0:n * P]
                mm(o, dq[r, g, i * P:(i + 1) * P], dk[r, g, (i + 1 - n) * P:(i + 1) * P], True, False)
                if n == 2:
                    mm(o[:, 0:P], cstb[:, 0, :], cstb[:, 2, :], False, False)
                mm(o[:, (n - 1) * P:n * P], cstb[:, 0, :], cstb[:, 3 if g == 2 else 1, :], False, True).then_inc(d_scores, 1)

            def d_turn(u):
                pe.wait_ge(d_norm, u + 1)
                if u >= 2:
                    pe.wait_ge(d_put, u - 1)
                for t in range(d_keys(u)):
                    last = nc.tensor.transpose(psum[:, 3 + u % 2, t * P:(t + 1) * P], probs[:, u % 3, t * P:(t + 1) * P], ident)
                last.then_inc(d_turned, 1)

            def d_attend(u):
                hd, i = divmod(u, NT)
                g, e, n = hd // 2, hd % 2, d_keys(u)
                pe.wait_ge(d_put, u + 1)
                for t in range(n):
                    kt = i + 1 - n + t
                    last = mm(psum[HD * e:HD * e + HD, 5 + g, i * P:(i + 1) * P],
                              dv[g][:, kt * P + HD * e:kt * P + HD * e + HD], dpt[:, u % 2, t * P:(t + 1) * P],
                              t == 0, t == n - 1)
                last.then_inc(d_out, 1)

            for u in range(UNITS2 + 3):
                if u < UNITS2:
                    d_score(u)
                if 2 <= u < UNITS2 + 2:
                    d_turn(u - 2)
                if u >= 3:
                    d_attend(u - 3)
            pe.wait_ge(d_lse, 1)
            for g in range(3):
                for e in range(2):
                    for i in range(NT):
                        u = 8 * g + 4 * e + i
                        last = mm(psum[HD * e:HD * e + HD, g, i * P:(i + 1) * P],
                                  dstat[:, 2, u:u + 1].to_broadcast([P, HD]), ident, True, True)
                last.then_inc(d_lseb, 1)
            pe.wait_ge(attn_y, 3)
            pe.wait_ge(z_zero, 1)

            def vec(name, t, p):
                pe.wait_ge(rw_vec, done(VEC_STEPS, name, t, p))

            def act_(name, t, p):
                pe.wait_ge(rw_act, done(ACT_STEPS, name, t, p))

            def rw_step(name, t, p):
                A, B = psum[:, 2 * p, :], psum[:, 2 * p + 1, :]
                tok = slice(t * P, (t + 1) * P)
                last = None

                def rows(e):
                    return slice(HD * e, HD * e + HD)

                def sq(o, c, l_, r_):
                    for e in range(2):
                        res = mm(o[:, c + e * P:c + e * P + P], l_[:, e * P:(e + 1) * P], r_[:, e * P:(e + 1) * P], True, True)
                    return res

                def head(o, c, l_, r_):
                    return mm(o[:, c + half * P:c + half * P + P], fm[l_][rows(half), p, tok], fm[r_][rows(half), p, tok],
                              True, True)

                half = 0
                if name[-1] == "b":
                    half = 1
                    pe.wait_ge(rw_mm, done(MM_STEPS, name[:-1] + "a", t, p))

                if name in ("M12a", "M12b"):
                    if t:
                        act_("Y", t - 1, p)
                    head(A, 0, "A", "B")
                    last = head(A, 256, "B", "A")
                elif name in ("M34a", "M34b"):
                    if t:
                        vec("U", t - 1, p)
                    head(B, 0, "K", "A")
                    last = head(B, 256, "B", "R")
                elif name == "NN2":
                    vec("N", t, p)
                    sq(A, 0, cm(p, "Nt"), cm(p, "N"))
                    last = sq(A, 256, cm(p, "N"), cm(p, "Nt"))
                elif name in ("M5a", "M5b"):
                    vec("M34", t, p)
                    last = head(B, 0, "K", "R")
                elif name == "Y2":
                    act_("N2", t, p)
                    vec("M5", t, p)
                    last = sq(B, 0, cm(p, "N2"), cm(p, "Ya"))
                elif name == "NN4":
                    sq(A, 0, cm(p, "N2t"), cm(p, "N2"))
                    last = sq(A, 256, cm(p, "N2"), cm(p, "N2t"))
                elif name == "Y4":
                    act_("N4", t, p)
                    vec("Y2", t, p)
                    last = sq(B, 0, cm(p, "N4"), cm(p, "Yb"))
                elif name == "N8":
                    last = sq(A, 0, cm(p, "N4t"), cm(p, "N4"))
                elif name == "X1":
                    act_("N8", t, p)
                    for e in range(2):
                        last = mm(A[:, e * HD:e * HD + HD], cm(p, "Mak")[:, e * P:(e + 1) * P],
                                  tm["V"][:, t, (2 * p + e) * HD:(2 * p + e + 1) * HD], True, True)
                elif name == "Y8":
                    vec("Y4", t, p)
                    last = sq(B, 0, cm(p, "N2"), cm(p, "Ya"))
                elif name in ("TF1", "TF2"):
                    y_ = cm(p, "Yb" if name == "TF1" else "Ya")
                    vec("Y8" if name == "TF1" else "Y32", t, p)
                    act_("X1" if name == "TF1" else "TF1", t, p)
                    for e in range(2):
                        nc.tensor.transpose(A[:, e * P:(e + 1) * P], y_[:, e * P:(e + 1) * P], ident)
                    last = sq(A, 256, cm(p, "E1" if name == "TF1" else "E2"), y_)
                elif name in ("Y32", "XT"):
                    act_("TF1" if name == "Y32" else "TF2", t, p)
                    last = sq(B, 0, cm(p, "N2"), cm(p, "N2t"))
                elif name == "GW":
                    vec("XT", t, p)
                    for e in range(2):
                        xt = cm(p, "Yb")[:, e * P:(e + 1) * P]
                        a_ = tm["A"][:, t, (2 * p + e) * HD:(2 * p + e + 1) * HD]
                        mm(B[:, e * HD:e * HD + HD], xt, a_, True, True)
                        mm(B[:, P + e * HD:P + e * HD + HD], xt, cm(p, "Nt")[:, e * HD:e * HD + HD], True, True)
                        last = mm(B[rows(e), 256:384], a_, xt, True, True)
                elif name in ("PTa", "PTb"):
                    act_("GW", t, p)
                    c = half
                    for e in range(2):
                        last = mm(A[rows(e), c * HD:c * HD + HD], cm(p, "N")[rows(c), e * HD:e * HD + HD],
                                  tm["B"][rows(c), t, (2 * p + e) * HD:(2 * p + e + 1) * HD], True, True)
                elif name in ("S0a", "S1a"):
                    c = int(name[1])
                    if c == 0:
                        vec("PT", t, p)
                    else:
                        vec("Z0", t, p)
                    for e in range(2):
                        hc = slice((2 * p + e) * HD, (2 * p + e + 1) * HD)
                        o = A[rows(e), 0:HD]
                        mm(o, tm["B"][rows(c), t, hc], cm(p, "N")[rows(c), P + e * HD:P + e * HD + HD], True, False)
                        last = mm(o, tm["K"][rows(c), t, hc], tm["V"][rows(c), t, hc], False, False)
                elif name in ("S0b", "S1b"):
                    c = int(name[1])
                    if t and c == 0:
                        vec("Z1", t - 1, p)
                    for e in range(2):
                        last = mm(A[rows(e), 0:HD], cm(p, "E2")[rows(e), c * HD:c * HD + HD],
                                  zst[rows(e), p, (2 * t + c) % 4, :], False, True)
                elif name in ("Ua", "Ub"):
                    act_("GT", t, p)
                    e = half
                    for c in range(2):
                        last = mm(B[rows(c), e * HD:e * HD + HD], cm(p, "E1")[rows(e), c * HD:c * HD + HD],
                                  zst[rows(e), p, (2 * t + c) % 4, :], True, True)
                else:
                    vec("Z1", t, p)
                    vec("U", t, p)
                    for e in range(2):
                        hc = slice((2 * p + e) * HD, (2 * p + e + 1) * HD)
                        o = A[rows(e), 0:P]
                        ec = slice(e * P, (e + 1) * P)
                        mm(o, tm["V"][:, t, hc], cm(p, "Mrk")[:, ec], True, False)
                        for c in range(2):
                            mm(o[:, c * HD:c * HD + HD], zst[rows(e), p, (2 * t + c) % 4, :],
                               fm["R"][rows(e), p, t * P + c * HD:t * P + c * HD + HD], False, False)
                        last = mm(o, cm(p, "N4")[:, e * HD:e * HD + HD], cm(p, "Mrb")[:, ec], False, True)
                last.then_inc(rw_mm, 1)

            for t in range(NT):
                for name in MM_STEPS:
                    for p in range(3):
                        rw_step(name, t, p)

            for p in range(3):
                pe.wait_ge(rw_act, done(ACT_STEPS, "Y", NT - 1, p))
            for p in range(3):
                mm(psum[:, p, :], heads2, y[:, 3 + p, :], True, True).then_inc(gn_mm, 1)
            for p in range(3):
                pe.wait_ge(gn_act, p + 1)
                mm(psum[:, p, :], heads2, tmp[:, 3 + p, :], True, True).then_inc(gn_mm, 1)

            def merge(branch, m):
                q = branch * KD + m
                item, half = 8 + q // 2, q % 2
                if half == 0:
                    pe.wait_ge(ring_in[item % 2], (base // 2 + item // 2 + 1) * 16)
                w = ring[:, item % 2, half * 1408:half * 1408 + 1408].rearrange("p (k c) -> p k c", k=11)
                if q >= 2:
                    pe.wait_ge(merged_put, q - 1)
                    pe.wait_ge(gate_act, q - 1)
                for k in range(KD):
                    last = mm(psum[:, 6 + q % 2, :], w[:, k, :], h[:, k, :], k == 0, k == KD - 1)
                last.then_inc(gate_mm, 1)
                k0, n = ((0, 3), (3, 3), (6, 2))[branch]
                if m == 0 and branch == 1:
                    pe.wait_ge(rwkv_y, 3)
                if m == 0 and branch == 2:
                    pe.wait_ge(ssm_y, 2)
                for k in range(n):
                    last = mm(psum[:, 4 + q % 2, :], w[:, KD + k, :], y[:, k0 + k, :], k == 0, k == n - 1)
                last.then_inc(branch_mm, 1)

            def drive(s):
                r = slice(32 * (s % 4), 32 * (s % 4) + 32)
                if s:
                    pe.wait_ge(s_rot, s)
                for im in range(2):
                    c = W2_B + ((s // 4) * 2 + im) * P
                    last = mm(psum[:, im, :], mixw[r, c:c + P], ussm[r, s // 4, :], True, True)
                last.then_inc(s_bu, 1)

            def readout(s):
                if s == 0:
                    pe.wait_ge(s_cw, 2)
                pe.wait_ge(s_back, s + 1)
                for im in range(2):
                    last = mm(psum[:, 2 + s // 4, :], cmat[:, im, s, :], xst[:, s % 2, im, :],
                              s % 4 == 0 and im == 0, s % 4 == 3 and im == 1)
                last.then_inc(s_ym if s % 4 == 3 else s_c, 1)

            merge(0, 0)
            pe.wait_ge(gn_act, 6)
            drive(0)
            for s in range(8):
                if s:
                    merge(2 * s // KD, 2 * s % KD)
                    readout(s - 1)
                merge((2 * s + 1) // KD, (2 * s + 1) % KD)
                if s < 7:
                    drive(s + 1)
            readout(7)
            pe.wait_ge(s_gl, 6)
            for n in range(2):
                for m in range(2):
                    for k in range(2):
                        c = (W2_GV, W2_GG)[n] + k * 256 + m * P
                        last = mm(psum[:, 2 * n + m, :], mixw[:, c:c + P], hid[:, 22 + k, :], k == 0, k == 1)
                    last.then_inc(glu_mm, 1)
            for m in range(KD):
                merge(2, m)
            for m in range(KD):
                i = m // 2
                if m % 2 == 0:
                    pe.wait_ge(out2_split, i + 1)
                if m == 0:
                    pe.wait_ge(merged_split, KD)
                for k in range(KD):
                    c = slice((m % 2) * D + k * P, (m % 2) * D + (k + 1) * P)
                    last = mm3(psum[:, (m + 4) % 8, :], (out2_hi[i % 2][:, c], ring_lo[:, i % 2, c]),
                               (merged_hi[:, k, :], merged_lo[:, k, :]), k == 0, k == KD - 1)
                last.then_inc(out2_ready, 1)
            norm(3 * LAYERS + 2)
            swiglu(2 * LAYERS, base, 24 * LAYERS)
            norm(3 * LAYERS + 3)

        @block.scalar
        def _(act):
            act.dma_start(cst[:, :], t_in["cst"]).then_inc(cst_in, 16)
            act.dma_start(gains[:, :, :], t_in["gains"]).then_inc(gains_in, 16)
            act.dma_start(g2s[:, :], t_in["g2s"]).then_inc(gains_in, 16)
            act.wait_ge(cst_in, 16)
            act.wait_ge(gains_in, 32)
            act.wait_ge(x_in, 16)

            def norm(n, early=None, squares=h):
                for k in range(KD):
                    act.wait_ge(x_upd, 8 * n + k + 1)
                    nc.scalar.activation(squares[:, k, :], x[:, k, :], ACT.Square).then_inc(sq_ready, 1)
                if early is not None:
                    early()
                nc.scalar.activation(root_of_eps[:, :], eps, ACT.Sqrt)
                act.wait_ge(sumsq_ready, n + 1)
                nc.scalar.activation(tmp[:, 0, :], psum[:, 4, :], ACT.Sqrt, bias=eps, scale=1.0 / D).then_inc(rms_ready, 1)

            def split_ring(i, s, n, cols=2 * KD * P, into=None):
                act.wait_ge(ring_in[s], n * 8 + 8 * (i - s) + 16)
                into = gu_hi[:, s, :] if into is None else into[s]
                nc.scalar.activation(into[:, 0:cols], ring[:, s, 0:cols], ACT.Copy).then_inc(ring_high, 1)

            def norm_split(n, early, h0, squares=h):
                norm(n, early, squares)
                for k in range(KD):
                    act.wait_ge(h_ready, h0 + k + 1)
                    nc.scalar.activation(h_hi[:, k, :], h[:, k, :], ACT.Copy).then_inc(h_high, 1)

            def swiglu(f, n0, free0):
                with act.Fori(0, NJ // 2) as jj:
                    for s in range(2):
                        j = 2 * jj + s
                        act.wait_ge(ring_in[1 - s], n0 * 8 + 16 * jj + 16 + 16 * s)
                        nc.scalar.activation(gu_hi[:, 1 - s, 0:2 * KD * P], ring[:, 1 - s, 0:2 * KD * P], ACT.Copy)\
                            .then_inc(ring_high, 1)
                        act.wait_ge(wdr_in[s], 16 * (f * (NJ // 2) + jj + 1))
                        nc.scalar.activation(wd_hi[:, s, :], wdr[:, s, :], ACT.Copy).then_inc(wd_high, 1)
                        act.wait_ge(gate_ready, f * NJ + j + 1)
                        nc.scalar.activation(probs[:, s, :], psum[:, s, :], ACT.Silu).then_inc(silu_ready, 1)
                        act.wait_ge(wdr_free, f * NJ + j + 1)
                        act.wait_ge(hid_ready, f * NJ + j + 1)
                        nc.scalar.activation(hid_hi[:, s, :], hid[:, j, :], ACT.Copy).then_inc(hid_high, 1)
                for k in range(NJ):
                    if k < 2:
                        act.wait_ge(wdr_free, used(f * NJ + NJ - 2 + k))
                    elif (k - 2) % 4 == 3:
                        act.wait_ge(ring_free, used(free0 + NJ + (k - 2) // 4))
                    else:
                        act.wait_ge(hid_used, f * (NJ - 6) + (k - 2) - (k - 2) // 4 + 1)
                    nc.scalar.activation(hid_hi[:, k % 2, :], hid[:, k, :], ACT.Copy).then_inc(hid_high, 1)
                    if k in NEXT_ITEM:
                        i = NEXT_ITEM[k]
                        split_ring(NJ + i, i % 2, n0, DOWN_COLS[i])

            def mixer(l):
                n0 = l * LAYER_ITEMS + FFN_ITEMS
                act.dma_start(mixw[:, :], wsmall[l]).then_inc(mixw_in, 16)
                def split(i):
                    split_ring(i, i % 2, n0, KD * MIX_COLS[i], mix_hi)

                split(1)
                act.wait_ge(p_kv, l + 1)
                nc.scalar.activation(tmp[:, 0, :], psum[:, 1, :], ACT.Square).then_inc(lat_sq, 1)
                act.wait_ge(p_qa, l + 1)
                nc.scalar.activation(tmp[:, 1, :], psum[:, 3, :], ACT.Square).then_inc(lat_sq, 1)
                split(2)
                act.wait_ge(ring_free, used(n0 + 1))
                nc.scalar.activation(tmp[:, 2, :], psum[:, 4, :], ACT.Square).then_inc(lat_sq, 1)
                act.wait_ge(pads_zero, 2)
                for t in range(2):
                    if t:
                        act.wait_ge(ring_free, used(n0 + 2))
                    else:
                        act.wait_ge(p_pool, l + 1)
                    nc.scalar.activation(upad[:, t, 16:], psum[:, (7, 0)[t], :], ACT.Copy).then_inc(pool_in, 1)
                    if t == 0:
                        split(3)
                act.wait_ge(lat_ss, 2 * l + 1)
                nc.scalar.activation(tmp[:, 0, :], psum[:, 5, :], ACT.Sqrt, bias=eps, scale=1.0 / KVR).then_inc(lat_rms, 1)
                act.wait_ge(lat_ss, 2 * l + 2)
                nc.scalar.activation(tmp[:, 1, :], psum[:, 6, :], ACT.Sqrt, bias=eps, scale=1.0 / QR).then_inc(lat_rms, 1)
                g = slice(64, 70)
                act.wait_ge(fz_ready, l + 1)
                nc.scalar.activation(wdr[g, 0, :], probs[g, 1, :], ACT.Exp, scale=-1.0).then_inc(astep, 1)
                act.wait_ge(astep, l + 1)
                nc.scalar.activation(wdr[g, 1, :], wdr[g, 0, :], ACT.Ln, bias=1.0).then_inc(fe_ready, 1)
                for p in range(3):
                    split(4 + p)
                    act.wait_ge(p_foxqk, 3 * l + p + 1)
                    for e in range(2):
                        nc.scalar.activation(hid[0:HD, 6 + 2 * p + e, :], psum[HD * e:HD * e + HD, (7, 5, 7)[p], :],
                                             ACT.Copy, scale=FOX_SCALE).then_inc(foxq_put, 1)
                split(7)
                for t in range(NT):
                    if t < NT - 1:
                        act.wait_ge(p_foxv, 3 * l + t + 1)
                    else:
                        act.wait_ge(ring_free, used(n0 + 7))
                    nc.scalar.activation(vt[1][:, t, :], psum[:, 1 + t, 0:384], ACT.Copy).then_inc(foxv_put, 1)
                for a in range(HEADS):
                    act.wait_ge(p_mlaq, 6 * l + a + 1)
                    nc.scalar.activation(hid[0:NOPE, a, :], psum[0:NOPE, (7, 0)[a % 2], :], ACT.Copy,
                                         scale=MLA_SCALE).then_inc(mlaqn_put, 1)
                for t in range(NT):
                    act.wait_ge(p_mlav, 4 * l + t + 1)
                    nc.scalar.activation(vt[0][:, t, :], psum[:, (4, 1, 2, 3)[t], 0:384], ACT.Copy).then_inc(mlav_put, 1)

                def put_turned(u):
                    a, i = divmod(u, NT)
                    act.wait_ge(turned, UNITS * l + u + 1)
                    if i == 0 and a >= 2:
                        act.wait_ge(yh_ready, 12 * l + a - 1)
                    nc.scalar.activation(pt[a % 2][:, 0:i + 1, i * P:(i + 1) * P],
                                         psum[:, 3 + u % 2, 0:(i + 1) * P].rearrange("p (t c) -> p t c", t=i + 1),
                                         ACT.Copy).then_inc(pt_put, 1)

                def put_y(pair):
                    act.wait_ge(yh_ready, 12 * l + 2 * pair + 2)
                    nc.scalar.activation(y_hi[:, pair if pair < 3 else pair + 2, :], psum[:, 5 + pair % 2, :],
                                         ACT.Copy).then_inc(y_put, 1)

                for u in range(UNITS + 2):
                    if u < UNITS:
                        n = (u % NT + 1) * P
                        act.wait_ge(nmax, UNITS * l + u + 1)
                        if u >= 3:
                            act.wait_ge(turned, UNITS * l + u - 2)
                        nc.scalar.activation(probs[:, u % 3, 0:n], psum[:, u % 3, 0:n], ACT.Exp,
                                             bias=stat[:, u % 3, 0:1], accum_out=stat[:, u % 3, 1:2]).then_inc(expd, 1)
                    if u >= 2:
                        put_turned(u - 2)
                    if u >= 12 and (u - 12) % 8 == 0:
                        put_y((u - 12) // 8)
                    if u in OUT_SPLIT:
                        split_ring(OUT_SPLIT[u], OUT_SPLIT[u] % 2, n0, 2 * D, out_hi)
                put_y(5)
                for t in range(2):
                    act.wait_ge(p_pooly, 2 * l + t + 1)
                    nc.scalar.activation(y_hi[:, 3 + t, :], psum[:, (0, 7)[t], :], ACT.Copy,
                                         scale=gains[:, l, G_PS + t:G_PS + t + 1]).then_inc(pool_out, 1)
                for i in (10, 11):
                    split_ring(i, i % 2, n0, 2 * D, out_hi)

            with act.Fori(0, LAYERS) as l:
                n0 = l * LAYER_ITEMS
                norm_split(3 * l, lambda: split_ring(0, 0, n0), 24 * l)
                swiglu(2 * l, n0, n0)
                n1 = l * LAYER_ITEMS + FFN_ITEMS
                norm_split(3 * l + 1, lambda: split_ring(0, 0, n1, KD * MIX_COLS[0], mix_hi), 24 * l + 8)
                mixer(l)
                n2 = l * LAYER_ITEMS + FFN_ITEMS + MIX_ITEMS
                norm_split(3 * l + 2, lambda: split_ring(0, 0, n2), 24 * l + 16, hid_squares)
                n0 = n2
                swiglu(2 * l + 1, n0, n0)
            norm(3 * LAYERS)
            norm(3 * LAYERS + 1)
            act.dma_start(mixw[:, :], t_in["wsmall2"]).then_inc(mixw2_in, 16)
            act.dma_start(c2, t_in["cst2"]).then_inc(mixw2_in, 16)

            def read_out(name, out_, in_, func=ACT.Copy, **kw):
                act.wait_ge(made, NUM[name] + 1)
                nc.scalar.activation(out_, in_, func, **kw).then_inc(read, 1)

            def bank(name):
                return psum[:, NUM[name] % 8, :]

            raws = ["xwa", "xg", "r0", "k0", "v0", "r1", "k1", "v1", "r2", "k2", "v2"]

            def raw_out(name):
                i = raws.index(name)
                if i >= 4:
                    act.wait_ge(mixed, i - 3)
                read_out(name, raw[:, i % 4, 16:], bank(name))

            def prep(p):
                act.wait_ge(decay_in, p + 1)
                nc.scalar.activation(dvec[:, p, 0:7], dvec[:, p, 0:7], ACT.Exp, scale=-KAPPA).then_inc(decay_exp, 1)
                nc.scalar.activation(probs[:, 2, :], probs[:, 2, :], ACT.Exp, scale=-KAPPA).then_inc(decay_exp, 1)
                nc.scalar.activation(probs[:, 0, :], probs[:, 1, :], ACT.Exp, scale=KAPPA).then_inc(decay_exp, 1)
                act.wait_ge(decay_exp, 4 * p + 3)
                nc.scalar.activation(probs[:, 1, :], probs[:, 1, :], ACT.Exp, scale=-KAPPA).then_inc(decay_exp, 1)
                act.wait_ge(kk_in, p + 1)
                nc.scalar.activation(tmp[:, 1, :], tmp[:, 0, :], ACT.Square).then_inc(kk_sq, 1)
                act.wait_ge(made, NUM[f"kn{p}"] + 1)
                nc.scalar.activation(tmp[:, 1, :], bank(f"kn{p}"), ACT.Sqrt).then_inc(read, 1)
                read_out(f"bn{p}", tmp[:, 3, :], bank(f"bn{p}"))

            raw_out("xwa")
            raw_out("xg")
            raw_out("r0")
            raw_out("k0")
            act.wait_ge(mixed, 2)
            nc.scalar.activation(tmp[0:64, 2, :], tmp[0:64, 0, :], ACT.Tanh).then_inc(lora_act, 1)
            nc.scalar.activation(tmp[64:128, 2, :], tmp[64:128, 0, :], ACT.Copy).then_inc(lora_act, 1)
            nc.scalar.activation(tmp[:, 3, :], tmp[:, 1, :], ACT.Sigmoid).then_inc(lora_act, 1)
            raw_out("v0")
            for p in range(3):
                read_out(f"lw{p}", sig[:, p, :], bank(f"lw{p}"), ACT.Sigmoid, bias=g2s[:, H_W0 + p:H_W0 + p + 1])
            for p in range(3):
                read_out(f"la{p}", icl[:, p, :], bank(f"la{p}"), ACT.Sigmoid, bias=g2s[:, H_A0 + p:H_A0 + p + 1])
            for p in range(3):
                read_out(f"lg{p}", glora[:, p, :], bank(f"lg{p}"))
            raw_out("r1")
            raw_out("k1")
            raw_out("v1")
            prep(0)
            raw_out("r2")
            raw_out("k2")
            raw_out("v2")
            prep(1)

            def ordered(t, g):
                return t if g == 0 else t.rearrange("p (a r) -> p r a", r=4 if g == 1 else 16)

            def as_group(t, g):
                return t if g == 0 else t.rearrange("p (r a) -> p r a", r=4 if g == 1 else 16)

            for g in range(3):
                read_out(f"aq{g}", as_group(dq[:, g, :], g), ordered(bank(f"aq{g}"), g), scale=HD ** -0.5)
            nc.scalar.activation(spar[:, 0, :], g2s[:, H_LS:H_LS + 8], ACT.Exp).then_inc(s_trig, 1)
            prep(2)
            for g in range(3):
                read_out(f"ak{g}", as_group(dk[:, g, :], g), ordered(bank(f"ak{g}"), g))
                if g == 0:
                    act.wait_ge(s_par, 1)
                    nc.scalar.activation(spar[:, 3, :], spar[:, 2, :], ACT.Sin).then_inc(s_trig, 1)
                    nc.scalar.activation(spar[:, 5, :], spar[:, 4, :], ACT.Sin).then_inc(s_trig, 1)
            for g in range(2):
                read_out(f"av{g}", dv[g], bank(f"av{g}"))
            read_out("av2", as_group(hid[:, 18, :], 2), ordered(bank("av2"), 2))
            for m in range(2):
                read_out(f"su{m}", ussm[:, m, :], bank(f"su{m}"))
            read_out("av2t", dv[2], bank("av2t"))
            act.wait_ge(bonus_put, 3)
            for n in "ABKV":
                for t in range(NT):
                    read_out(f"t{n}{t}", tm[n][:, t, :], bank(f"t{n}{t}")[:, 0:384])

            def d_keys(u):
                return 2 if u // 8 == 0 and u % NT else 1

            for u in range(UNITS2 + 2):
                if u < UNITS2:
                    n = d_keys(u) * P
                    act.wait_ge(d_nmax, u + 1)
                    if u >= 3:
                        act.wait_ge(d_turned, u - 2)
                    nc.scalar.activation(probs[:, u % 3, 0:n], psum[:, u % 3, 0:n], ACT.Exp, bias=dstat[:, 0, u:u + 1],
                                         accum_out=dstat[:, 1, u:u + 1]).then_inc(d_exp, 1)
                if u >= 2:
                    v = u - 2
                    n = d_keys(v) * P
                    act.wait_ge(d_turned, v + 1)
                    if v >= 2:
                        act.wait_ge(d_out, v - 1)
                    nc.scalar.activation(dpt[:, v % 2, 0:n], psum[:, 3 + v % 2, 0:n], ACT.Copy).then_inc(d_put, 1)
            act.wait_ge(d_exp, UNITS2)
            nc.scalar.activation(dstat[:, 2, :], dstat[:, 1, :], ACT.Ln).then_inc(d_ln, 1)
            for g in range(3):
                act.wait_ge(d_diff, g + 1)
                nc.scalar.activation(tmp[:, 3 + g, :], tmp[:, 3 + g, :], ACT.Exp).then_inc(d_wexp, 1)

            for t in range(NT):
                for name in ACT_STEPS:
                    for p in range(3):
                        A, B = psum[:, 2 * p, :], psum[:, 2 * p + 1, :]
                        src = {"N2": ("NN2", cm(p, "N2", 512), A), "N4": ("NN4", cm(p, "N4", 512), A),
                               "N8": ("N8", cm(p, "N2"), A[:, 0:256]), "X1": ("X1", cm(p, "Nt", P), A[:, 0:P]),
                               "TF1": ("TF1", cm(p, "N2", 512), A), "TF2": ("TF2", cm(p, "N2", 512), A),
                               "GW": ("GW", cm(p, "N"), B[:, 0:256]), "GT": ("GW", cm(p, "E1", P), B[:, 256:384]),
                               "Y": ("Y", y[:, 3 + p, t * P:(t + 1) * P], A[:, 0:P])}[name]
                        act.wait_ge(rw_mm, done(MM_STEPS, src[0], t, p))
                        nc.scalar.activation(src[1], src[2], ACT.Copy).then_inc(rw_act, 1)
            for p in range(3):
                act.wait_ge(gn_in, p + 1)
                nc.scalar.activation(tmp[:, 3 + p, :], tmp[:, p, :], ACT.Square).then_inc(gn_act, 1)
            for p in range(3):
                act.wait_ge(gn_mm, 4 + p)
                nc.scalar.activation(tmp[:, 3 + p, :], psum[:, p, :], ACT.Sqrt, bias=cst2_eps, scale=1.0 / HD)\
                    .then_inc(gn_act, 1)

            def gate(q):
                act.wait_ge(gate_mm, q + 1)
                nc.scalar.activation(probs[:, q % 2, :], psum[:, 6 + q % 2, :], ACT.Sigmoid).then_inc(gate_act, 1)

            for q in range(2 * KD):
                gate(q)
            for m in range(2):
                act.wait_ge(s_gl, m + 1)
                nc.scalar.activation(hid[:, 14 + m, :], hid[:, 12 + m, :], ACT.Square).then_inc(s_gla, 1)
            for m in range(2):
                act.wait_ge(s_gl, 3 + m)
                nc.scalar.activation(hid[:, 14 + m, :], hid[:, 14 + m, :], ACT.Sigmoid, scale=2 * GELU_C).then_inc(s_gla, 1)
            for m in range(2):
                act.wait_ge(glu_mm, 3 + m)
                nc.scalar.activation(hid[:, 16 + m, :], psum[:, 2 + m, :], ACT.Sigmoid).then_inc(glu_act, 1)

            def high_merged(m):
                act.wait_ge(merged_put, 2 * KD + m + 1)
                nc.scalar.activation(merged_hi[:, m, :], merged[:, m, :], ACT.Copy).then_inc(merged_high, 1)

            def high_out(i):
                act.wait_ge(ring_in[i % 2], (LAYERS * LAYER_ITEMS // 2 + (20 + i) // 2 + 1) * 16)
                nc.scalar.activation(out2_hi[i % 2][:, 0:2 * D], ring[:, i % 2, 0:2 * D], ACT.Copy).then_inc(out2_high, 1)

            act.wait_ge(glu_mm, 4)
            for m in range(KD):
                gate(2 * KD + m)
                if m:
                    high_merged(m - 1)
                if m == KD - 2:
                    high_out(0)
            high_merged(KD - 1)
            for i in range(1, 4):
                high_out(i)
            base = LAYERS * LAYER_ITEMS
            norm_split(3 * LAYERS + 2, lambda: split_ring(0, 0, base + B2_ITEMS), 24 * LAYERS + 8)
            swiglu(2 * LAYERS, base + B2_ITEMS, base)
            norm(3 * LAYERS + 3)

        @block.vector
        def _(dve):
            nc.vector.memset(upad[:, :, :], 0.0).then_inc(pads_zero, 1)
            nc.vector.memset(wsum[:, :, :], 0.0).then_inc(pads_zero, 1)
            dve.wait_ge(cst_in, 16)
            dve.wait_ge(gains_in, 32)
            dve.wait_ge(x_in, 16)
            for k in range(KD):
                dve.sem_inc(x_upd, 1)

            def norm(n, gain, into, split=None):
                dve.wait_ge(rms_ready, n + 1)
                nc.vector.reciprocal(tmp[:, 1, :], tmp[:, 0, :]).then_inc(rstd_ready, 1)
                dve.wait_ge(rstd_ready, n + 1)
                for k in range(KD):
                    nc.vector.scalar_tensor_tensor(out=into[:, k, :], in0=x[:, k, :], scalar=gain[:, k:k + 1],
                                                   in1=tmp[:, 1, :], op0=ALU.mult, op1=ALU.mult)\
                        .then_inc(h_ready if into is h else x_upd, 1)
                    if split is not None and k:
                        split(k - 1)
                if split is not None:
                    split(KD - 1)

            def residual(order, scale):
                for m, bank, ready, value in order:
                    dve.wait_ge(ready, value)
                    nc.vector.scalar_tensor_tensor(out=x[:, m, :], in0=psum[:, bank, :], scalar=scale, in1=x[:, m, :],
                                                   op0=ALU.mult, op1=ALU.add).then_inc(x_upd, 1)

            def low(out_, whole, hi, made):
                return nc.vector.tensor_tensor(out_, whole, hi, ALU.subtract).then_inc(made, 1)

            def low_ring(s, cols=2 * KD * P, hi=None):
                hi = gu_hi[:, s, 0:cols] if hi is None else hi[s][:, 0:cols]
                low(ring_lo[:, s, 0:cols], ring[:, s, 0:cols], hi.bitcast(F32), ring_split)

            def norm_split(n, n0, h0, gain, cols=2 * KD * P, hi=None):
                dve.wait_ge(ring_high, n0 + 1)
                low_ring(0, cols, hi)

                def split(k):
                    dve.wait_ge(h_high, h0 + k + 1)
                    low(h_lo[:, k, :], h[:, k, :], h_hi[:, k, :].bitcast(F32), h_split)

                norm(n, gain, h, split)

            def swiglu(f, n0, scale=0.5):
                with dve.Fori(0, NJ // 2) as jj:
                    for s in range(2):
                        j = 2 * jj + s
                        dve.wait_ge(ring_high, n0 + j + 2)
                        low_ring(1 - s)
                        dve.wait_ge(wd_high, f * NJ + j + 1)
                        low(wdr_lo[:, s, :], wdr[:, s, :], wd_hi[:, s, :].bitcast(F32), wd_split)
                        dve.wait_ge(silu_ready, f * NJ + j + 1)
                        dve.wait_ge(ring_free, used(n0 + j))
                        nc.vector.tensor_tensor(hid[:, j, :], probs[:, s, :], psum[:, 2 + s, :], ALU.mult)\
                            .then_inc(hid_ready, 1)
                        dve.wait_ge(hid_high, 2 * f * NJ + j + 1)
                        low(hid_lo[:, s, :], hid[:, j, :], hid_hi[:, s, :].bitcast(F32), hid_split)
                for k in range(NJ):
                    dve.wait_ge(hid_high, (2 * f + 1) * NJ + k + 1)
                    low(hid_lo[:, k % 2, :], hid[:, k, :], hid_hi[:, k % 2, :].bitcast(F32), hid_split)
                    if k in NEXT_ITEM:
                        i = NEXT_ITEM[k]
                        dve.wait_ge(ring_high, n0 + NJ + i + 1)
                        low_ring(i % 2, DOWN_COLS[i])
                residual([(m, 4 + m, down_ready, 6 * f + m + 1) for m in range(3)]
                         + [(3, 7, wdr_free, used((f + 1) * NJ - 1))]
                         + [(4 + m, m, down_ready, 6 * f + m + 4) for m in range(3)]
                         + [(7, 3, ring_free, used(n0 + FFN_ITEMS - 1))], scale)

            def mixer(l):
                n0 = l * LAYER_ITEMS + FFN_ITEMS
                step = Chain(dve, vstep, VSTEPS * l, VSTEPS)

                def split(i):
                    dve.wait_ge(ring_high, n0 + i + 1)
                    low_ring(i % 2, KD * MIX_COLS[i], mix_hi)

                split(1)
                dve.wait_ge(ring_free, used(n0))
                step(nc.vector.tensor_tensor(probs[0:32, 0, :], psum[0:32, 2, :], cos[0:32, :], ALU.mult))
                step(nc.vector.tensor_tensor(probs[0:32, 2, :], psum[32:64, 2, :], sin[32:64, :], ALU.mult))
                nc.vector.tensor_tensor(probs[64:96, 0, :], probs[0:32, 0, :], probs[0:32, 2, :], ALU.add).then_inc(kr_done, 1)
                g = slice(64, 70)
                step(nc.vector.tensor_scalar(probs[g, 2, :], psum[g, 2, :], gains[g, l, G_FB:G_FB + 1], None, ALU.add))
                nc.vector.scalar_tensor_tensor(out=probs[g, 1, :], in0=probs[g, 2, :], scalar=-1.0, in1=probs[g, 2, :],
                                               op0=ALU.mult, op1=ALU.max).then_inc(fz_ready, 1)
                step(nc.vector.tensor_scalar(probs[g, 2, :], probs[g, 2, :], 0.0, None, ALU.min))
                split(2)
                split(3)
                dve.wait_ge(lat_rms, 2 * l + 1)
                step(nc.vector.reciprocal(tmp[:, 0, :], tmp[:, 0, :]))
                nc.vector.scalar_tensor_tensor(out=tmp[:, 5, :], in0=psum[:, 1, :], scalar=gains[:, l, G_KVA:G_KVA + 1],
                                               in1=tmp[:, 0, :], op0=ALU.mult, op1=ALU.mult).then_inc(lat_n, 1)
                dve.wait_ge(lat_rms, 2 * l + 2)
                step(nc.vector.reciprocal(tmp[:, 1, :], tmp[:, 1, :]))
                for k in range(2):
                    nc.vector.scalar_tensor_tensor(out=tmp[:, 3 + k, :], in0=psum[:, 3 + k, :],
                                                   scalar=gains[:, l, G_QA + k:G_QA + k + 1],
                                                   in1=tmp[:, 1, :], op0=ALU.mult, op1=ALU.mult).then_inc(lat_n, 1)
                dve.wait_ge(fe_ready, l + 1)
                step(nc.vector.tensor_tensor(probs[g, 2, :], probs[g, 2, :], wdr[g, 1, :], ALU.subtract))
                step(nc.vector.tensor_tensor_scan(probs[g, 1, :], ones[g, 0:1].to_broadcast([6, S]), probs[g, 2, :], 0.0, ALU.mult, ALU.add))
                nc.vector.tensor_scalar(probs[g, 2, :], probs[g, 1, :], -1.0, None, ALU.mult).then_inc(cum_ready, 1)
                for p in range(3):
                    split(4 + p)
                    dve.wait_ge(ring_free, used(n0 + 3 + p))
                    for e in range(2):
                        nc.vector.tensor_copy(hid[0:HD, 18 + 2 * p + e, :], psum[HD * e:HD * e + HD, (0, 6, 0)[p], :])\
                            .then_inc(foxk_put, 1)
                split(7)
                for a in range(HEADS):
                    dve.wait_ge(p_sw, 2 * l + a // 3 + 1)
                    r = slice(32 * (a % 3), 32 * (a % 3) + 32)
                    b = a % 2
                    dve.wait_ge(p_mlaq, 6 * l + a + 1)
                    step(nc.vector.scalar_tensor_tensor(out=tmp[64:96, 1, :], in0=psum[64:96, (7, 0)[b], :], scalar=MLA_SCALE,
                                                        in1=cos[64:96, :], op0=ALU.mult, op1=ALU.mult))
                    step(nc.vector.scalar_tensor_tensor(out=tmp[64:96, 2, :], in0=psum[r, 5 + a // 3, :], scalar=MLA_SCALE,
                                                        in1=sin[r, :], op0=ALU.mult, op1=ALU.mult))
                    step(nc.vector.tensor_tensor(hid[64:96, a, :], tmp[64:96, 1, :], tmp[64:96, 2, :], ALU.add))
                    dve.sem_inc(mlaqr_put, 1)
                for p in range(3):
                    dve.wait_ge(p_mlak, 3 * l + p + 1)
                    for e in range(2):
                        nc.vector.tensor_copy(hid[0:NOPE, 12 + 2 * p + e, :], psum[HD * e:HD * e + HD, 1 + p, :])\
                            .then_inc(mlak_put, 1)

                def negmax(u):
                    n = (u % NT + 1) * P
                    dve.wait_ge(scores, UNITS * l + u + 1)
                    nc.vector.tensor_reduce(stat[:, u % 3, 0:1], psum[:, u % 3, 0:n], AX.X, ALU.max, negate=True)\
                        .then_inc(nmax, 1)

                def normalise(u):
                    n = (u % NT + 1) * P
                    dve.wait_ge(expd, UNITS * l + u + 1)
                    nc.vector.reciprocal(stat[:, u % 3, 2:3], stat[:, u % 3, 1:2]).then_inc(rsum, 1)
                    dve.wait_ge(rsum, UNITS * l + u + 1)
                    nc.vector.tensor_scalar(probs[:, u % 3, 0:n], probs[:, u % 3, 0:n], stat[:, u % 3, 2:3], None, ALU.mult)\
                        .then_inc(normd, 1)

                def low_y(pair):
                    dve.wait_ge(y_put, 6 * l + pair + 1)
                    m = pair if pair < 3 else pair + 2
                    low(y_lo[:, m, :], psum[:, 5 + pair % 2, :], y_hi[:, m, :].bitcast(F32), y_split)

                for u in range(UNITS + 1):
                    if u < UNITS:
                        negmax(u)
                    if u >= 1:
                        normalise(u - 1)
                    if u >= 13 and (u - 13) % 8 == 0:
                        low_y((u - 13) // 8)
                    if u - 1 in OUT_SPLIT:
                        i = OUT_SPLIT[u - 1]
                        dve.wait_ge(ring_high, n0 + i + 1)
                        low_ring(i % 2, 2 * D, out_hi)
                low_y(5)
                for t in range(2):
                    dve.wait_ge(pool_out, 2 * l + t + 1)
                    nc.vector.scalar_tensor_tensor(out=y_lo[:, 3 + t, :], in0=psum[:, (0, 7)[t], :],
                                                   scalar=gains[:, l, G_PS + t:G_PS + t + 1],
                                                   in1=y_hi[:, 3 + t, :].bitcast(F32), op0=ALU.mult, op1=ALU.subtract)\
                        .then_inc(y_split, 1)
                for m in range(KD):
                    if m in (2, 4):
                        j = len(MIX_COLS) + 1 + m // 2
                        dve.wait_ge(ring_high, n0 + j + 1)
                        low_ring(j % 2, 2 * D, out_hi)
                    ready, value = (ring_free, used(n0 + len(MIX_COLS) + m // 2)) if m % 2 else (wout_ready, 4 * l + m // 2 + 1)
                    residual([(m, (m + 4) % 8, ready, value)], 1.0)
                step.end()

            with dve.Fori(0, LAYERS) as l:
                norm_split(3 * l, l * LAYER_ITEMS, 24 * l, gains[:, l, G_N1:G_N1 + 8])
                swiglu(2 * l, l * LAYER_ITEMS)
                norm_split(3 * l + 1, l * LAYER_ITEMS + FFN_ITEMS, 24 * l + 8, gains[:, l, G_NM:G_NM + 8],
                           KD * MIX_COLS[0], mix_hi)
                mixer(l)
                norm_split(3 * l + 2, l * LAYER_ITEMS + FFN_ITEMS + MIX_ITEMS, 24 * l + 16, gains[:, l, G_N2:G_N2 + 8])
                swiglu(2 * l + 1, l * LAYER_ITEMS + FFN_ITEMS + MIX_ITEMS)
            norm(3 * LAYERS, gains[:, 0, G_FIN:G_FIN + 8], x)
            norm(3 * LAYERS + 1, g2s[:, H_NM:H_NM + 8], h)
            base = LAYERS * LAYER_ITEMS
            step = Chain(dve, w_step, 0, W_STEPS)
            TT, TS, STT = nc.vector.tensor_tensor, nc.vector.tensor_scalar, nc.vector.scalar_tensor_tensor
            raws = ["xwa", "xg", "r0", "k0", "v0", "r1", "k1", "v1", "r2", "k2", "v2"]
            mix_col = [9, 10, 0, 3, 6, 1, 4, 7, 2, 5, 8]

            def mix(name, o):
                i = raws.index(name)
                dve.wait_ge(read, NUM[name] + 1)
                z, zp = raw[:, i % 4, 16:], raw[:, i % 4, 15:15 + S]
                step(TT(o, zp, z, ALU.subtract))
                c = H_MIX + mix_col[i]
                STT(out=o, in0=o, scalar=g2s[:, c:c + 1], in1=z, op0=ALU.mult, op1=ALU.add).then_inc(mixed, 1)
                dve.wait_ge(mixed, i + 1)

            dve.wait_ge(mixw2_in, 32)
            mix("xwa", tmp[:, 0, :])
            mix("xg", tmp[:, 1, :])

            def col(c, p):
                return g2s[:, c + p:c + p + 1]

            def chunks(t):
                return t.rearrange("p (c s) -> p c s", s=CHUNK)

            for p in range(3):
                if p == 0:
                    dve.wait_ge(lora_act, 3)
                rr, kx, vv = tmp[:, 4, :], tmp[:, 5, :], vfm[:, p, :]
                mix(f"r{p}", rr)
                mix(f"k{p}", kx)
                mix(f"v{p}", vv)
                dve.wait_ge(read, NUM[f"la{p}"] + 1)
                if p:
                    dve.wait_ge(rwkv_fm, p)
                TS(tmp[:, 0, :], kx, col(H_KK, p), None, ALU.mult).then_inc(kk_in, 1)
                step(TS(probs[:, 0, :], icl[:, p, :], -1.0, col(H_KA, p), ALU.add, ALU.mult))
                step(STT(out=kx, in0=probs[:, 0, :], scalar=1.0, in1=kx, op0=ALU.add, op1=ALU.mult))
                if p == 0:
                    dve.wait_ge(read, NUM["la2"] + 1)
                STT(out=tmp[:, 2, :], in0=rr, scalar=col(H_RK, p), in1=kx, op0=ALU.mult, op1=ALU.mult).then_inc(bonus_in, 1)
                step(nc.vector.tensor_tensor_scan(probs[:, 0, :], restart, sig[:, p, :], 0.0, ALU.mult, ALU.add))
                c = chunks(probs[:, 0, :])
                mid = c[:, :, CHUNK // 2 - 1:CHUNK // 2]
                step(TT(chunks(probs[:, 1, :]), c, mid.to_broadcast([P, 8, CHUNK]), ALU.subtract))
                step(TT(probs[:, 2, :], probs[:, 1, :], sig[:, p, :], ALU.subtract))
                d1 = chunks(probs[:, 1, :])
                TT(dvec[:, p, 0:7], d1[:, 0:7, CHUNK - 1], c[:, 1:8, CHUNK // 2 - 1], ALU.add).then_inc(decay_in, 1)
                dve.wait_ge(read, NUM[f"kn{p}"] + 1)
                step(TS(tmp[:, 1, :], tmp[:, 1, :], 1e-12, None, ALU.max))
                step(nc.vector.reciprocal(tmp[:, 1, :], tmp[:, 1, :]))
                step(TT(tmp[:, 0, :], tmp[:, 0, :], tmp[:, 1, :], ALU.mult))
                dve.wait_ge(decay_exp, 4 * p + 4)
                STT(out=fm["A"][:, p, :], in0=tmp[:, 0, :], scalar=-1.0, in1=probs[:, 2, :], op0=ALU.mult, op1=ALU.mult)
                step(TT(tmp[:, 0, :], tmp[:, 0, :], icl[:, p, :], ALU.mult))
                TT(fm["B"][:, p, :], tmp[:, 0, :], probs[:, 0, :], ALU.mult)
                TT(fm["K"][:, p, :], kx, probs[:, 0, :], ALU.mult)
                TT(fm["R"][:, p, :], rr, probs[:, 1, :], ALU.mult).then_inc(rwkv_fm, 1)
                dve.wait_ge(read, NUM[f"bn{p}"] + 1)
                TT(bonus[:, p, :], tmp[:, 3, :], vv, ALU.mult).then_inc(bonus_put, 1)
                dve.wait_ge(bonus_put, p + 1)

            ar, ai, ls = (g2s[:, c:c + 8] for c in (H_AR, H_AI, H_LS))

            def sp_(i):
                return spar[:, i, :]

            dve.wait_ge(s_trig, 1)
            step(TT(sp_(1), ai, sp_(0), ALU.mult))
            step(TS(sp_(2), sp_(1), 1.0 / TWO_PI, ROUND, ALU.mult, ALU.add))
            step(TS(sp_(2), sp_(2), -ROUND, None, ALU.add))
            step(STT(out=sp_(1), in0=sp_(2), scalar=-PI_HI, in1=sp_(1), op0=ALU.mult, op1=ALU.add))
            step(STT(out=sp_(1), in0=sp_(2), scalar=-PI_LO, in1=sp_(1), op0=ALU.mult, op1=ALU.add))
            step(TS(sp_(2), sp_(1), 3.1415925, -3.1415925, ALU.min, ALU.max))
            step(STT(out=sp_(4), in0=sp_(2), scalar=-1.0, in1=sp_(2), op0=ALU.mult, op1=ALU.max))
            step(TS(sp_(4), sp_(4), -1.0, 1.5707963, ALU.mult, ALU.add))
            dve.sem_inc(s_par, 1)
            step(TT(sp_(6), ar, sp_(0), ALU.mult))
            step(TS(sp_(6), sp_(6), -100.0, 1.0 / 64, ALU.max, ALU.mult))
            step(TS(sp_(7), sp_(6), 1.0 / 5040, None, ALU.mult))
            for f_ in (1 / 720, 1 / 120, 1 / 24, 1 / 6, 0.5, 1.0):
                step(STT(out=sp_(7), in0=sp_(7), scalar=f_, in1=sp_(6), op0=ALU.add, op1=ALU.mult))
            for _ in range(6):
                step(STT(out=sp_(7), in0=sp_(7), scalar=2.0, in1=sp_(7), op0=ALU.add, op1=ALU.mult))
            step(TS(sp_(8), sp_(7), 1.0, None, ALU.add))
            dve.wait_ge(s_trig, 3)
            step(TT(sp_(6), sp_(8), sp_(5), ALU.mult))
            step(TT(sp_(7), sp_(8), sp_(3), ALU.mult))
            step(TS(sp_(6), sp_(6), -1.0, None, ALU.add))
            step(TT(sp_(9), ar, ar, ALU.mult))
            step(TT(sp_(10), ai, ai, ALU.mult))
            step(TT(sp_(9), sp_(9), sp_(10), ALU.add))
            step(nc.vector.reciprocal(sp_(9), sp_(9)))
            step(TT(sp_(10), sp_(6), ar, ALU.mult))
            step(TT(sp_(11), sp_(7), ai, ALU.mult))
            step(TT(sp_(10), sp_(10), sp_(11), ALU.add))
            step(TT(sp_(10), sp_(10), sp_(9), ALU.mult))
            step(TT(sp_(11), sp_(7), ar, ALU.mult))
            step(TT(sp_(12), sp_(6), ai, ALU.mult))
            step(TT(sp_(11), sp_(11), sp_(12), ALU.subtract))
            step(TT(sp_(11), sp_(11), sp_(9), ALU.mult))
            cr, ci = (mixw[:, W2_C + i * P:W2_C + (i + 1) * P].rearrange("p (s c) -> p s c", s=8) for i in range(2))
            fr, fi = (spar[:, i, :].rearrange("p (s o) -> p s o", o=1).to_broadcast([P, 8, 16]) for i in (10, 11))
            t_ = [sw[:, i, :, :] for i in range(4)]
            step(TT(t_[0], cr, fr, ALU.mult))
            step(TT(t_[1], ci, fi, ALU.mult))
            step(TT(t_[2], cr, fi, ALU.mult))
            step(TT(t_[3], ci, fr, ALU.mult))
            step(TT(cr, t_[0], t_[1], ALU.subtract))
            step(TT(t_[2], t_[2], t_[3], ALU.add))
            step(TS(ci, t_[2], -1.0, None, ALU.mult))
            dve.sem_inc(s_cw, 1)

            def powers(tab, n_max):
                n = 1
                while n < n_max:
                    c0, s0 = tab[:, 0, :, 1:n + 1], tab[:, 1, :, 1:n + 1]
                    cn, sn = (tab[:, i, :, n:n + 1].to_broadcast([P, 8, n]) for i in range(2))
                    u_ = [sw[:, i, :, 0:n] for i in range(4)]
                    step(TT(u_[0], c0, cn, ALU.mult))
                    step(TT(u_[1], s0, sn, ALU.mult))
                    step(TT(u_[2], s0, cn, ALU.mult))
                    step(TT(u_[3], c0, sn, ALU.mult))
                    step(TT(tab[:, 0, :, n + 1:2 * n + 1], u_[0], u_[1], ALU.subtract))
                    step(TT(tab[:, 1, :, n + 1:2 * n + 1], u_[2], u_[3], ALU.add))
                    n *= 2

            for tab in (fine, coarse):
                step(nc.vector.memset(tab[:, 0, :, 0:1], 1.0))
                step(nc.vector.memset(tab[:, 1, :, 0:1], 0.0))
            step(nc.vector.tensor_copy(fine[:, 0, :, 1:2], spar[:, 5, :].rearrange("p (s o) -> p s o", o=1)))
            step(nc.vector.tensor_copy(fine[:, 1, :, 1:2], spar[:, 3, :].rearrange("p (s o) -> p s o", o=1)))
            powers(fine, 32)
            for i in range(2):
                step(nc.vector.tensor_copy(coarse[:, i, :, 1:2], fine[:, i, :, 32:33]))
            powers(coarse, 16)
            dve.sem_inc(s_par, 1)

            def d_keys(u):
                return 2 if u // 8 == 0 and u % NT else 1

            for u in range(UNITS2 + 1):
                if u < UNITS2:
                    dve.wait_ge(d_scores, u + 1)
                    nc.vector.tensor_reduce(dstat[:, 0, u:u + 1], psum[:, u % 3, 0:d_keys(u) * P], AX.X, ALU.max,
                                            negate=True).then_inc(d_nmax, 1)
                if u >= 1:
                    v = u - 1
                    n = d_keys(v) * P
                    dve.wait_ge(d_exp, v + 1)
                    nc.vector.reciprocal(stat[:, v % 3, 2:3], dstat[:, 1, v:v + 1]).then_inc(d_rsum, 1)
                    dve.wait_ge(d_rsum, v + 1)
                    TS(probs[:, v % 3, 0:n], probs[:, v % 3, 0:n], stat[:, v % 3, 2:3], None, ALU.mult).then_inc(d_norm, 1)
            dve.wait_ge(d_ln, 1)
            TT(dstat[:, 2, :], dstat[:, 2, :], dstat[:, 0, :], ALU.subtract).then_inc(d_lse, 1)

            def ordered(t, g):
                return t if g == 0 else t.rearrange("p (a r) -> p r a", r=4 if g == 1 else 16)

            def as_group(t, g):
                return t if g == 0 else t.rearrange("p (r a) -> p r a", r=4 if g == 1 else 16)

            for g in range(3):
                dve.wait_ge(d_lseb, g + 1)
                step(nc.vector.tensor_copy(ordered(tmp[:, g, :], g), as_group(psum[:, g, :], g)))
            top, tot = raw[:, 0, 0:S], raw[:, 1, 0:S]
            step(TT(top, tmp[:, 0, :], tmp[:, 1, :], ALU.max))
            step(TT(top, top, tmp[:, 2, :], ALU.max))
            for g in range(3):
                TT(tmp[:, 3 + g, :], tmp[:, g, :], top, ALU.subtract).then_inc(d_diff, 1)
            dve.wait_ge(d_wexp, 3)
            step(TT(tot, tmp[:, 3, :], tmp[:, 4, :], ALU.add))
            step(TT(tot, tot, tmp[:, 5, :], ALU.add))
            step(nc.vector.reciprocal(tot, tot))
            for g in range(3):
                step(TT(tmp[:, 3 + g, :], tmp[:, 3 + g, :], tot, ALU.mult))
                TT(ordered(y[:, g, :], g), as_group(psum[:, 5 + g, :], g), ordered(tmp[:, 3 + g, :], g), ALU.mult)\
                    .then_inc(attn_y, 1)
            dve.wait_ge(attn_y, 3)
            nc.vector.memset(zst, 0.0).then_inc(z_zero, 1)
            dve.wait_ge(z_zero, 1)

            def two(t):
                return t.rearrange("p (e c) -> p e c", e=2)

            def mask2(m):
                return m.rearrange("p (o c) -> p o c", o=1).to_broadcast([P, 2, P])

            for t in range(NT):
                for name in VEC_STEPS:
                    for p in range(3):
                        A, B = psum[:, 2 * p, :], psum[:, 2 * p + 1, :]

                        def after(mm_name):
                            dve.wait_ge(rw_mm, done(MM_STEPS, mm_name, t, p))

                        def masked(o, src, m):
                            return TT(two(cm(p, o)), two(src), mask2(m), ALU.mult)

                        def add(o, src, other):
                            return TT(cm(p, o), src, cm(p, other), ALU.add)

                        def rows(e):
                            return slice(HD * e, HD * e + HD)

                        if name == "N":
                            after("M12b")
                            masked("N", A[:, 0:256], mk16l)
                            masked("E1", A[:, 0:256], mke1)
                            masked("E2", A[:, 0:256], mke2)
                            last = masked("Nt", A[:, 256:512], mk16u)
                        elif name == "M34":
                            after("M34b")
                            masked("Mak", B[:, 0:256], mkus)
                            last = masked("Mrb", B[:, 256:512], mkui)
                        elif name == "Y1":
                            dve.wait_ge(rw_vec, done(VEC_STEPS, "N", t, p))
                            last = TT(two(cm(p, "Ya")), two(cm(p, "Nt")), mask2(ident), ALU.add)
                        elif name == "M5":
                            after("M5b")
                            last = masked("Mrk", B[:, 0:256], mkui)
                        elif name in ("Y2", "Y4", "Y8", "Y32", "XT"):
                            o, other = {"Y2": ("Yb", "Ya"), "Y4": ("Ya", "Yb"), "Y8": ("Yb", "Ya"),
                                        "Y32": ("Ya", "Yb"), "XT": ("Yb", "Ya")}[name]
                            after(name)
                            prev = {"Y2": "Y1", "Y4": "Y2", "Y8": "Y4", "Y32": "Y8", "XT": "Y32"}[name]
                            dve.wait_ge(rw_vec, done(VEC_STEPS, prev, t, p))
                            last = add(o, B[:, 0:256], other)
                        elif name == "PT":
                            after("PTb")
                            last = TT(two(cm(p, "E2", P)), two(A[:, 0:P]),
                                      ident64.rearrange("p (o c) -> p o c", o=1).to_broadcast([P, 2, HD]), ALU.add)
                        elif name in ("Z0", "Z1"):
                            c = 2 * t + int(name[1])
                            after("S" + name[1] + "b")
                            if c < 7:
                                last = TS(zst[:, p, (c + 1) % 4, :], A[:, 0:HD], dvec[:, p, c:c + 1], None, ALU.mult)
                            else:
                                last = nc.vector.engine_nop()
                        else:
                            after("Ub")
                            dve.wait_ge(rw_act, done(ACT_STEPS, "GW", t, p))
                            last = TT(cm(p, "N4", P), B[:, 0:P], cm(p, "N")[:, P:256], ALU.add)
                        last.then_inc(rw_vec, 1)

            for p in range(3):
                dve.wait_ge(gn_mm, p + 1)
                STT(out=tmp[:, p, :], in0=psum[:, p, :], scalar=-1.0 / HD, in1=y[:, 3 + p, :], op0=ALU.mult, op1=ALU.add)\
                    .then_inc(gn_in, 1)
            for p in range(3):
                dve.wait_ge(gn_act, 4 + p)
                dve.wait_ge(gn_in, p + 1)
                step(nc.vector.reciprocal(tmp[:, 3 + p, :], tmp[:, 3 + p, :]))
                step(TT(tmp[:, p, :], tmp[:, p, :], tmp[:, 3 + p, :], ALU.mult))
                step(TS(tmp[:, p, :], tmp[:, p, :], col(H_LW, p), col(H_LB, p), ALU.mult, ALU.add))
                step(TT(tmp[:, p, :], tmp[:, p, :], bonus[:, p, :], ALU.add))
                TT(y[:, 3 + p, :], tmp[:, p, :], glora[:, p, :], ALU.mult).then_inc(rwkv_y, 1)

            def merge(q):
                m = q % KD
                dve.wait_ge(gate_act, q + 1)
                dve.wait_ge(branch_mm, q + 1)
                if q < KD:
                    TT(merged[:, m, :], psum[:, 4 + q % 2, :], probs[:, q % 2, :], ALU.mult).then_inc(merged_put, 1)
                else:
                    dve.wait_ge(merged_put, q)
                    step(TT(probs[:, 2, :], psum[:, 4 + q % 2, :], probs[:, q % 2, :], ALU.mult))
                    TT(merged[:, m, :], merged[:, m, :], probs[:, 2, :], ALU.add).then_inc(merged_put, 1)

            def rotate(s):
                c, sn = tabs[:, s % 2, 0, :], tabs[:, s % 2, 1, :]
                br, bi = psum[:, 0, :], psum[:, 1, :]
                dve.wait_ge(s_tab, s + 1)
                dve.wait_ge(s_bu, s + 1)
                step(TT(hid[:, 12, :], br, c, ALU.mult))
                step(TT(hid[:, 14, :], bi, sn, ALU.mult))
                step(TT(hid[:, 13, :], bi, c, ALU.mult))
                TT(hid[:, 15, :], br, sn, ALU.mult).then_inc(s_rot, 1)
                dve.wait_ge(s_rot, s + 1)
                step(TT(hid[:, 12, :], hid[:, 12, :], hid[:, 14, :], ALU.add))
                step(TT(hid[:, 13, :], hid[:, 13, :], hid[:, 15, :], ALU.subtract))
                mag = spar[:, 8, s:s + 1].to_broadcast([P, S])
                step(nc.vector.tensor_tensor_scan(hid[:, 14, :], mag, hid[:, 12, :], 0.0, ALU.mult, ALU.add))
                step(nc.vector.tensor_tensor_scan(hid[:, 15, :], mag, hid[:, 13, :], 0.0, ALU.mult, ALU.add))

            def turn_back(s):
                c, sn = tabs[:, s % 2, 0, :], tabs[:, s % 2, 1, :]
                qr, qi = hid[:, 14, :], hid[:, 15, :]
                if s >= 2:
                    dve.wait_ge(s_c, s - 1)
                step(TT(hid[:, 12, :], qr, c, ALU.mult))
                step(TT(hid[:, 13, :], qi, sn, ALU.mult))
                step(TT(xst[:, s % 2, 0, :], hid[:, 12, :], hid[:, 13, :], ALU.subtract))
                step(TT(hid[:, 12, :], qr, sn, ALU.mult))
                step(TT(hid[:, 13, :], qi, c, ALU.mult))
                TT(xst[:, s % 2, 1, :], hid[:, 12, :], hid[:, 13, :], ALU.add).then_inc(s_back, 1)
                dve.wait_ge(s_back, s + 1)

            for s in range(8):
                rotate(s)
                merge(2 * s)
                turn_back(s)
                merge(2 * s + 1)
            for m in range(2):
                dve.wait_ge(s_ym, m + 1)
                STT(out=hid[:, 12 + m, :], in0=ussm[:, m, :], scalar=col(H_D, m), in1=psum[:, 2 + m, :],
                    op0=ALU.mult, op1=ALU.add).then_inc(s_gl, 1)
            for m in range(2):
                dve.wait_ge(s_gla, 1 + m)
                step(TS(hid[:, 14 + m, :], hid[:, 14 + m, :], 0.044715, 1.0, ALU.mult, ALU.add))
                TT(hid[:, 14 + m, :], hid[:, 14 + m, :], hid[:, 12 + m, :], ALU.mult).then_inc(s_gl, 1)
            for m in range(2):
                dve.wait_ge(s_gla, 3 + m)
                TT(hid[:, 22 + m, :], hid[:, 14 + m, :], hid[:, 12 + m, :], ALU.mult).then_inc(s_gl, 1)
            for m in range(2):
                dve.wait_ge(glu_mm, 1 + m)
                dve.wait_ge(glu_act, 1 + m)
                TT(y[:, 6 + m, :], psum[:, m, :], hid[:, 16 + m, :], ALU.mult).then_inc(ssm_y, 1)

            def low_merged(m):
                dve.wait_ge(merged_high, m + 1)
                low(merged_lo[:, m, :], merged[:, m, :], merged_hi[:, m, :].bitcast(F32), merged_split)

            def low_out(i):
                dve.wait_ge(out2_high, i + 1)
                low(ring_lo[:, i % 2, 0:2 * D], ring[:, i % 2, 0:2 * D], out2_hi[i % 2][:, 0:2 * D].bitcast(F32), out2_split)

            for m in range(KD):
                merge(2 * KD + m)
                if m:
                    low_merged(m - 1)
                if m == KD - 2:
                    low_out(0)
            step.end()
            low_merged(KD - 1)
            low_out(1)
            for m in range(KD):
                if m in (2, 4):
                    low_out(1 + m // 2)
                residual([(m, (m + 4) % 8, out2_ready, m + 1)], 1.0)
            norm_split(3 * LAYERS + 2, base, 24 * LAYERS, g2s[:, H_NF:H_NF + 8])
            swiglu(2 * LAYERS, base, 1.0)
            norm(3 * LAYERS + 3, g2s[:, H_FIN:H_FIN + 8], x)

        @block.gpsimd
        def _(pool):
            pool.dma_start(cstb[:, :, :], t_in["cstb"]).then_inc(cstb_in, 16)
            pool.wait_ge(cst_in, 16)
            with pool.Fori(0, LAYERS) as l:
                step = Chain(pool, gstep, GSTEPS * l, GSTEPS)
                pool.wait_ge(kr_done, l + 1)
                pool.sem_inc(carrier, 1)
                for a in range(HEADS):
                    last = nc.gpsimd.tensor_copy(hid[64:96, 12 + a, :], probs[64:96, 0, :])
                last.then_inc(kpe_put, 1)
                pool.wait_ge(cum_ready, l + 1)
                pool.sem_inc(carrier, 1)
                pool.dma_start(hid[64:65, 6:12, :], probs[64:70, 1, :]).then_inc(aug_in, 16)
                pool.dma_start(hid[65:66, 18:24, :], probs[64:70, 2, :]).then_inc(aug_in, 16)
                pool.dma_start(hid[65:66, 6:12, :], t_in["onerow"]).then_inc(aug_in, 16)
                pool.dma_start(hid[64:65, 18:24, :], t_in["onerow"]).then_inc(aug_in, 16)
                pool.wait_ge(pads_zero, 2)
                pool.wait_ge(kpe_put, l + 1)
                pool.wait_ge(pool_in, 2 * l + 2)
                Z = 16
                rc = cst[:, C_RC:C_RC + 2 * S].rearrange("p (t c) -> p t c", t=2)

                def shifted(o, i, d, r=slice(0, P)):
                    return nc.gpsimd.tensor_tensor(o[r, Z:Z + S], i[r, Z:Z + S], i[r, Z - d:Z - d + S], ALU.add)

                wa, wb = wsum[:, 0, :], wsum[:, 1, :]
                lo, hi = slice(0, 64), slice(64, 128)
                step(shifted(wa, upad[:, 0, :], 1))
                step(shifted(wb, wa, 2, hi))
                step(nc.gpsimd.tensor_tensor(wb[lo, Z:], wa[lo, Z:], rc[lo, 0, :], ALU.mult))
                step(nc.gpsimd.tensor_tensor(wb[hi, Z:], wb[hi, Z:], rc[hi, 0, :], ALU.mult))
                pool.wait_ge(lat_n, 3 * l + 3)
                pool.wait_ge(p_mlaq, 6 * l + 6)
                step(nc.gpsimd.tensor_tensor(tmp[:, 0, :], wb[:, Z:], upad[:, 0, Z:], ALU.subtract))
                pool.sem_inc(pooled, 1)
                step(shifted(wa, upad[:, 1, :], 1))
                step(shifted(wb, wa, 2))
                step(shifted(wa, wb, 4))
                step(shifted(wb, wa, 8, hi))
                step(nc.gpsimd.tensor_tensor(wb[lo, Z:], wa[lo, Z:], rc[lo, 1, :], ALU.mult))
                step(nc.gpsimd.tensor_tensor(wb[hi, Z:], wb[hi, Z:], rc[hi, 1, :], ALU.mult))
                step(nc.gpsimd.tensor_tensor(tmp[:, 4, :], wb[:, Z:], upad[:, 1, Z:], ALU.subtract))
                pool.sem_inc(pooled, 1)
                step.end()
            pool.wait_ge(gn_mm, 3)
            pool.wait_ge(s_cw, 1)
            pool.wait_ge(s_par, 2)
            nc.gpsimd.memset(cmat, 0.0).then_inc(s_cz, 1)
            pool.wait_ge(s_cz, 1)
            for im in range(2):
                src = mixw[:, W2_C + im * P:W2_C + (im + 1) * P].rearrange("p (s c) -> p s c", s=8)
                for s in range(8):
                    for half in range(2):
                        r = slice(64 * half, 64 * half + 64)
                        c = 32 * (s % 4) + 16 * half
                        last = nc.gpsimd.tensor_copy(cmat[r, im, s, c:c + 16], src[r, s, :])
            last.then_inc(s_cz, 1)
            pool.wait_ge(s_cz, 2)
            pool.sem_inc(s_cw, 1)

            def spread(t, axis):
                if axis:
                    return t.rearrange("p (o j) -> p o j", o=1).to_broadcast([P, 16, 32])
                return t.rearrange("p (i o) -> p i o", o=1).to_broadcast([P, 16, 32])

            def grid(t):
                return t.rearrange("p (i j) -> p i j", j=32)

            for s in range(8):
                if s >= 2:
                    pool.wait_ge(s_back, s - 1)
                ca, sa = (spread(coarse[:, i, s, 0:16], 0) for i in range(2))
                cb, sb_ = (spread(fine[:, i, s, 0:32], 1) for i in range(2))
                for n, (o, u, v) in enumerate(((hid[:, 16, :], ca, cb), (hid[:, 17, :], sa, sb_),
                                               (hid[:, 18, :], sa, cb), (hid[:, 19, :], ca, sb_))):
                    nc.gpsimd.tensor_tensor(grid(o), u, v, ALU.mult).then_inc(s_cz, 1)
                pool.wait_ge(s_cz, 2 + 6 * s + 4)
                nc.gpsimd.tensor_tensor(tabs[:, s % 2, 0, :], hid[:, 16, :], hid[:, 17, :], ALU.subtract).then_inc(s_cz, 1)
                nc.gpsimd.tensor_tensor(tabs[:, s % 2, 1, :], hid[:, 18, :], hid[:, 19, :], ALU.add).then_inc(s_cz, 1)
                pool.wait_ge(s_cz, 2 + 6 * s + 6)
                pool.sem_inc(s_tab, 1)


_OUT_SHAPE = (1, S, D)


def pack_inputs(a):
    import numpy as np
    f = np.float32
    t = {}
    t["x"] = a["x"][0].T.reshape(KD, P, S).transpose(1, 0, 2)

    def tiles(w):
        return w.reshape(-1, P, w.shape[1]).transpose(1, 0, 2)

    gus, d1s, d2s = [], [], []

    def ffn(gu, down):
        g = gu[:, :FF].reshape(KD, P, NJ, P)
        u = gu[:, FF:].reshape(KD, P, NJ, P)
        gus.append(np.stack([g, u]).transpose(3, 2, 0, 1, 4).reshape(NJ, P, 2 * KD * P))
        d1s.append(down[:, :HALF].reshape(NJ, P, HALF))
        second = np.zeros((24, P, HALF), f)
        second[:NJ] = down[:, HALF:].reshape(NJ, P, HALF)
        d2s.append(second.reshape(6, 4, P, HALF).transpose(0, 2, 1, 3).reshape(6, P, 4 * HALF))

    for l in range(LAYERS):
        ffn(a["ffn1_w_gu"][l], a["ffn1_w_down"][l])
        ffn(a["ffn2_w_gu"][l], a["ffn2_w_down"][l])
    ffn(a["ffn_w_gate_up_2"][0], a["ffn_w_down_2"][0])
    t["wgu"], t["wd1"], t["wd2"] = np.stack(gus), np.stack(d1s), np.stack(d2s)

    mix = np.zeros((LAYERS, MIX_ITEMS, P, 2 * D), f)
    small = np.zeros((LAYERS, P, M_W), f)
    gains = np.zeros((P, LAYERS, G_W), f)
    for l in range(LAYERS):
        w = a["w_in"][l]
        kr = w[:, 384:416]
        fox = w[:, 672:1824]
        items = [np.concatenate([w[:, 256:384], kr, kr[:, 16:], kr[:, :16], w[:, 1824:1830]], 1),
                 w[:, 0:256], w[:, 416:672]]
        items += [np.concatenate([fox[:, P * p:P * p + P], fox[:, 384 + P * p:384 + P * p + P]], 1) for p in range(3)]
        items += [fox[:, 768:1024], fox[:, 1024:1152]]
        for i, it in enumerate(items):
            mix[l, i, :, :KD * it.shape[1]] = tiles(it).reshape(P, -1)
        for m in range(KD):
            mix[l, 8 + m // 2, :, (m % 2) * D:(m % 2 + 1) * D] = tiles(a["w_out"][l][:, m * P:(m + 1) * P]).reshape(P, -1)
        wq = a["w_q_b"][l].reshape(QR, HEADS, NOPE + ROPE)
        sw = np.concatenate([wq[:, :, NOPE + ROPE // 2:], wq[:, :, NOPE:NOPE + ROPE // 2]], 2).reshape(QR, -1)
        small[l, :, M_QB:M_QB + 1536] = tiles(np.concatenate([wq.reshape(QR, -1), sw], 1)).reshape(P, -1)
        wkv = a["w_kv_b"][l].reshape(KVR, HEADS, 2, 64)
        small[l, :, M_KV:M_KV + 768] = wkv.transpose(0, 2, 1, 3).reshape(KVR, -1)
        small[l, :, M_PW:M_PW + 128] = a["pool_w"][l].reshape(2, P, 64).transpose(1, 0, 2).reshape(P, -1)
        for c, v in ((G_N1, a["ffn1_norm"][l]), (G_NM, a["mix_norm"][l]), (G_N2, a["ffn2_norm"][l]),
                     (G_QA, a["q_a_norm"][l]), (G_KVA, a["kv_a_norm"][l]), (G_PS, a["pool_scale"][l]),
                     (G_FIN, a["final_norm"])):
            n = v.shape[0] // P
            gains[:, l, c:c + n] = v.reshape(n, P).T
        gains[64:70, l, G_FB] = a["fox_b_f"][l]
    t["wmix"], t["wsmall"], t["gains"] = mix, small, gains

    cst = np.zeros((P, C_W), f)
    cst[:, C_ID:C_ID + P] = np.eye(P)
    cst[:, C_ONE:C_ONE + P] = 1.0
    freq = (10000.0 ** (-np.arange(0, ROPE, 2, dtype=f) / f(ROPE))).astype(f)
    ang = (np.arange(S, dtype=f)[None, :] * freq[:, None]).astype(f)
    row = np.arange(P) % ROPE
    sign = np.where(row < ROPE // 2, -1.0, 1.0)[:, None]
    cst[:, C_COS:C_COS + S] = np.cos(ang.astype(np.float64))[row % (ROPE // 2)]
    cst[:, C_SIN:C_SIN + S] = np.sin(ang.astype(np.float64))[row % (ROPE // 2)] * sign
    count = np.arange(1, S + 1)
    for i, w in enumerate((2, 4, 8, 16)):
        cst[64 * (i % 2):64 * (i % 2) + 64, C_RC + S * (i // 2):C_RC + S * (i // 2) + S] = 1.0 / np.minimum(count, w)
    cst[:, C_EPS] = EPS
    cst[:, C_EPS + 1] = 64e-5
    t["cst"] = cst
    b = np.zeros((P, 4, P), f)
    b[:, 0] = np.eye(P)
    b[:, 1] = np.where(np.arange(P)[None, :] <= np.arange(P)[:, None], 0.0, -1e30)
    qi, kj = np.arange(P)[:, None], np.arange(P)[None, :]
    b[:, 2] = np.where(kj >= qi, 0.0, -1e30)
    b[:, 3] = np.where((kj <= qi) & (kj // 32 == qi // 32), 0.0, -1e30)
    t["cstb"] = b
    t["onerow"] = np.ones((1, HEADS, S), f)

    mix2 = np.zeros((B2_ITEMS, P, SLOT), f)
    w = a["w_in_2"][0]
    o = 3 * RW
    rw, lora = w[:, o:o + 3 * RW], w[:, 2 * o:2 * o + 256]
    su, gate = w[:, 2 * o + 256:2 * o + 512], w[:, 2 * o + 512:]
    items = [lora]
    items += [np.concatenate([rw[:, n * RW + p * P:n * RW + p * P + P] for n in range(3)], 1) for p in range(3)]
    items += [w[:, 0:RW], w[:, RW:2 * RW], w[:, 2 * RW:3 * RW], su]
    for i, it in enumerate(items):
        mix2[i, :, :KD * it.shape[1]] = tiles(it).reshape(P, -1)
    for b, wb in ((0, a["w_branch_attn_2"][0]), (1, a["w_branch_rwkv_2"][0]), (2, a["w_branch_ssm_2"][0])):
        for m in range(KD):
            q = b * KD + m
            col = np.concatenate([gate[:, b * D + m * P:b * D + (m + 1) * P], wb[:, m * P:(m + 1) * P]], 0)
            n = col.shape[0]
            mix2[8 + q // 2, :, (q % 2) * 1408:(q % 2) * 1408 + n] = tiles(col).reshape(P, -1)
    for m in range(KD):
        mix2[20 + m // 2, :, (m % 2) * D:(m % 2 + 1) * D] = tiles(a["w_out_2"][0][:, m * P:(m + 1) * P]).reshape(P, -1)
    t["wmix2"] = mix2
    sm = np.zeros((P, M_W), f)
    sm[0:64, W2_WA:W2_WA + RW] = a["rwkv_w2_2"][0]
    sm[64:128, W2_WA:W2_WA + RW] = a["rwkv_a2_2"][0]
    sm[:, W2_G:W2_G + RW] = a["rwkv_g2_2"][0]
    sm[:, W2_GV:W2_GV + 512] = tiles(a["ssm_glu_val_2"][0]).reshape(P, -1)
    sm[:, W2_GG:W2_GG + 512] = tiles(a["ssm_glu_gate_2"][0]).reshape(P, -1)
    for i, n in enumerate(("re", "im")):
        c = a[f"ssm_c_{n}_2"][0]
        sm[:, W2_C + i * P:W2_C + (i + 1) * P] = c.transpose(0, 2, 1).reshape(8, P, 16).transpose(1, 0, 2).reshape(P, P)
        b = a[f"ssm_b_{n}_2"][0]
        for g in range(16):
            r = 16 * (g % 8)
            c0 = W2_B + (g // 8 * 2 + i) * P + 64 * (g % 2)
            sm[r:r + 16, c0:c0 + 64] = b[g].T
    t["wsmall2"] = sm
    g2 = np.zeros((P, G2_W), f)
    for c, n in ((H_NM, "norm_mix"), (H_NF, "norm_ffn"), (H_FIN, "norm_final"), (H_MIX, "rwkv_shift_mix"),
                 (H_W0, "rwkv_w0"), (H_A0, "rwkv_a0"), (H_KK, "rwkv_k_k"), (H_KA, "rwkv_k_a"), (H_RK, "rwkv_r_k"),
                 (H_LW, "rwkv_ln_w"), (H_LB, "rwkv_ln_b"), (H_AR, "ssm_a_re"), (H_AI, "ssm_a_im"), (H_D, "ssm_d")):
        v = a[n + "_2"].reshape(-1, P)
        g2[:, c:c + v.shape[0]] = v.T
    g2[:, H_LS:H_LS + 8] = np.repeat(a["ssm_log_step_2"][0], 64).reshape(8, P).T
    t["g2s"] = g2
    i, j = np.arange(P)[:, None], np.arange(P)[None, :]
    low = j < i
    same = i // 64 == j // 64
    masks = [low & (i // 16 == j // 16), low & (i // 32 == j // 32) & (i // 16 != j // 16),
             low & same & (i // 32 != j // 32), (j > i) & (i // 16 == j // 16), (j > i) & same, (j >= i) & same, same]
    cs2 = np.zeros((P, 2048), f)
    for n, m in enumerate(masks):
        cs2[:, n * P:(n + 1) * P] = m
    cs2[:, 7 * P:7 * P + 64] = np.arange(64)[None, :] == i % 64
    cs2[:, 960:960 + S] = np.arange(S) % CHUNK != 0
    t["cst2"] = cs2
    return {k: np.ascontiguousarray(v) for k, v in t.items()}


def kernel(**inputs):
    import numpy as np
    import concourse.bacc as bacc
    from concourse.bass_utils import run_bass_kernel_spmd

    nc = bacc.Bacc("TRN2", target_bir_lowering=False, num_devices=1)
    arrays = pack_inputs({k: np.asarray(v) for k, v in inputs.items()})
    t_in = {k: nc.dram_tensor("in_" + k, v.shape, mybir.dt.from_np(v.dtype), kind="ExternalInput").ap()
            for k, v in arrays.items()}
    out = nc.dram_tensor("out", (P, KD, S), F32, kind="ExternalOutput").ap()
    build(nc, t_in, out)
    r = run_bass_kernel_spmd(nc, [{"in_" + k: v for k, v in arrays.items()}], core_ids=[0])
    got = r.results[0]["out"]
    return np.ascontiguousarray(got.transpose(1, 0, 2).reshape(D, S).T).reshape(_OUT_SHAPE)
```
